# Optimizing a Trainium2 kernel written in Bass

```python
import jax, jax.numpy as jnp
from jax import lax
import numpy as np

D_MODEL = 1024
BATCH = 1
SEQ = 256
DEPTH = 1

HEAD_DIM = 64
N_HEADS_NA = 8
N_HEADS_DIL = 8
D_NA = N_HEADS_NA * HEAD_DIM
D_DIL = N_HEADS_DIL * HEAD_DIM
D_MIX = D_NA + D_DIL
GRID_W = 64
NA_ROWS_MAX = 8
NA_COLS = 16
DIL_CONFIGS = ((128, 1), (512, 4), (2048, 16))
Q_BLOCK = 128
PEER_HEADS = 8
PEER_NKEYS = 128
PEER_N = PEER_NKEYS * PEER_NKEYS
PEER_DKEY = 256
PEER_TOPK = 16
PEER_TOKEN_BLOCK = 128
EPS = 1e-6


def rmsnorm(x, g):
    xf = x.astype(jnp.float32)
    y = xf * lax.rsqrt(jnp.mean(xf * xf, axis=-1, keepdims=True) + EPS)
    return (y * g.astype(jnp.float32)).astype(x.dtype)

def alibi_slopes(n):
    return (2.0 ** (-8.0 * (np.arange(n) + 1) / n)).astype(np.float32)

def na_index(seq):
    rows = seq // GRID_W
    wr = min(NA_ROWS_MAX, rows)
    t = np.arange(seq)
    r, c = t // GRID_W, t % GRID_W
    r0 = np.clip(r - wr // 2, 0, rows - wr)
    c0 = np.clip(c - NA_COLS // 2, 0, GRID_W - NA_COLS)
    kr = r0[:, None, None] + np.arange(wr)[None, :, None]
    kc = c0[:, None, None] + np.arange(NA_COLS)[None, None, :]
    shape = (seq, wr, NA_COLS)
    idx = np.broadcast_to(kr * GRID_W + kc, shape).reshape(seq, -1)
    dr = np.broadcast_to(kr - r[:, None, None] + NA_ROWS_MAX - 1, shape).reshape(seq, -1)
    dc = np.broadcast_to(kc - c[:, None, None] + NA_COLS - 1, shape).reshape(seq, -1)
    return idx.astype(np.int32), dr.astype(np.int32), dc.astype(np.int32)

def dilated_index(seq, window, dilation):
    half = window // (2 * dilation)
    off = dilation * np.arange(-half, half + 1)
    pos = np.arange(seq)[:, None] + off[None, :]
    valid = (pos >= 0) & (pos < seq)
    idx = np.clip(pos, 0, seq - 1).astype(np.int32)
    return idx, valid, np.abs(off).astype(np.float32)

def gathered_attention(q, k, v, idx, bias, valid):
    B, H, S, hd = q.shape
    nblk = S // Q_BLOCK
    K = idx.shape[-1]
    scale = hd ** -0.5
    q_blocks = jnp.moveaxis(q.reshape(B, H, nblk, Q_BLOCK, hd), 2, 0)
    idx_blocks = idx.reshape(nblk, Q_BLOCK, K)
    bias_blocks = jnp.moveaxis(bias.reshape(H, nblk, Q_BLOCK, K), 1, 0)
    valid_blocks = valid.reshape(nblk, Q_BLOCK, K)

    def block(args):
        qb, ib, bb, mb = args
        kg = jnp.take(k, ib, axis=2)
        vg = jnp.take(v, ib, axis=2)
        s = jnp.einsum('bhqd,bhqkd->bhqk', qb, kg, preferred_element_type=jnp.float32) * scale + bb
        s = jnp.where(mb, s, -jnp.inf)
        lse = jax.nn.logsumexp(s, axis=-1)
        p = jnp.exp(s - lse[..., None])
        o = jnp.einsum('bhqk,bhqkd->bhqd', p.astype(v.dtype), vg)
        return o, lse

    o, lse = lax.map(block, (q_blocks, idx_blocks, bias_blocks, valid_blocks))
    o = jnp.moveaxis(o, 0, 2).reshape(B, H, S, hd)
    lse = jnp.moveaxis(lse, 0, 2).reshape(B, H, S)
    return o, lse

def peer(h, wq, subkeys, u_tab, v_tab):
    B, S, D = h.shape
    T = B * S
    hf = h.reshape(T, D)
    q = (hf @ wq).reshape(T, PEER_HEADS, 2, PEER_DKEY // 2)
    sc = jnp.einsum('thpd,pnd->thpn', q, subkeys, preferred_element_type=jnp.float32)
    top_v, top_i = lax.top_k(sc, PEER_TOPK)
    cand_v = (top_v[:, :, 0, :, None] + top_v[:, :, 1, None, :]).reshape(T, PEER_HEADS, -1)
    cand_id = (top_i[:, :, 0, :, None] * PEER_NKEYS + top_i[:, :, 1, None, :]).reshape(T, PEER_HEADS, -1)
    best_v, best_j = lax.top_k(cand_v, PEER_TOPK)
    ids = jnp.take_along_axis(cand_id, best_j, axis=-1)
    gates = jax.nn.softmax(best_v, axis=-1)
    E = PEER_HEADS * PEER_TOPK
    nblk = T // PEER_TOKEN_BLOCK
    x_blocks = hf.reshape(nblk, PEER_TOKEN_BLOCK, D)
    id_blocks = ids.reshape(nblk, PEER_TOKEN_BLOCK, E)
    g_blocks = gates.reshape(nblk, PEER_TOKEN_BLOCK, E)

    def block(args):
        xb, ib, gb = args
        ub = jnp.take(u_tab, ib, axis=0)
        a = jnp.einsum('td,ted->te', xb, ub, preferred_element_type=jnp.float32)
        w = gb * jax.nn.gelu(a, approximate=False)
        vb = jnp.take(v_tab, ib, axis=0)
        return jnp.einsum('te,ted->td', w.astype(vb.dtype), vb)

    y = lax.map(block, (x_blocks, id_blocks, g_blocks))
    return y.reshape(B, S, D)

def first_inputs(seed: int = 0) -> dict:
    key = jax.random.key(seed)
    ks = jax.random.split(key, 16)
    f32 = jnp.float32
    L, D = DEPTH, D_MODEL

    def nrm(k, shape, std):
        return jax.random.normal(k, shape, f32) * std

    return {
        "x": nrm(ks[0], (BATCH, SEQ, D), 1.0),
        "c": nrm(ks[1], (BATCH, D), 1.0),
        "ada_w": nrm(ks[2], (L, D, 6 * D), 0.5 * D ** -0.5),
        "ada_b": nrm(ks[3], (L, 6 * D), 0.01),
        "norm1_g": 1.0 + nrm(ks[4], (L, D), 0.02),
        "w_in": nrm(ks[5], (L, D, 3 * D_MIX), D ** -0.5),
        "na_rpb": nrm(ks[6], (L, N_HEADS_NA, 2 * NA_ROWS_MAX - 1, 2 * NA_COLS - 1), 0.1),
        "out_norm_na_g": 1.0 + nrm(ks[7], (L, D_NA), 0.02),
        "out_norm_dil_g": 1.0 + nrm(ks[8], (L, D_DIL), 0.02),
        "w_out": nrm(ks[9], (L, D_MIX, D), D_MIX ** -0.5),
        "norm2_g": 1.0 + nrm(ks[10], (L, D), 0.02),
        "peer_wq": nrm(ks[11], (L, D, PEER_HEADS * PEER_DKEY), D ** -0.5),
        "peer_subkeys": nrm(ks[12], (L, 2, PEER_NKEYS, PEER_DKEY // 2), (PEER_DKEY // 2) ** -0.5),
        "peer_u": nrm(ks[13], (L, PEER_N, D), D ** -0.5),
        "peer_v": nrm(ks[14], (L, PEER_N, D), 1.0),
        "final_g": 1.0 + nrm(ks[15], (D,), 0.02),
    }

def first_block(x, c, ada_w, ada_b, norm1_g, w_in, na_rpb, out_norm_na_g, out_norm_dil_g,
              w_out, norm2_g, peer_wq, peer_subkeys, peer_u, peer_v, final_g):
    B, S, D = x.shape

    na_idx_np, na_dr, na_dc = na_index(S)
    na_idx = jnp.asarray(na_idx_np)
    na_valid = jnp.ones(na_idx_np.shape, dtype=bool)
    slopes = alibi_slopes(N_HEADS_DIL)
    dil_tables = []
    for (window, dilation) in DIL_CONFIGS:
        idx_np, valid_np, dist = dilated_index(S, window, dilation)
        bias = np.broadcast_to((-slopes[:, None] * dist[None, :])[:, None, :],
                               (N_HEADS_DIL, S, idx_np.shape[1]))
        dil_tables.append((jnp.asarray(idx_np), jnp.asarray(np.ascontiguousarray(bias)), jnp.asarray(valid_np)))

    def heads(t, n):
        return t.reshape(B, S, n, HEAD_DIM).transpose(0, 2, 1, 3)

    def merge(t):
        return t.transpose(0, 2, 1, 3).reshape(B, S, -1)

    for l in range(DEPTH):
        mod = jax.nn.silu(c) @ ada_w[l] + ada_b[l]
        sh1, sc1, g1, sh2, sc2, g2 = jnp.split(mod[:, None, :], 6, axis=-1)

        h = rmsnorm(x, norm1_g[l]) * (1.0 + sc1) + sh1
        proj = h @ w_in[l]
        qa, ka, va, qd, kd, vd = jnp.split(
            proj, [D_NA, 2 * D_NA, 3 * D_NA, 3 * D_NA + D_DIL, 3 * D_NA + 2 * D_DIL], axis=-1)

        na_bias = na_rpb[l][:, na_dr, na_dc].astype(jnp.float32)
        o_na, _ = gathered_attention(heads(qa, N_HEADS_NA), heads(ka, N_HEADS_NA),
                                     heads(va, N_HEADS_NA), na_idx, na_bias, na_valid)

        qdh, kdh, vdh = heads(qd, N_HEADS_DIL), heads(kd, N_HEADS_DIL), heads(vd, N_HEADS_DIL)
        outs, lses = [], []
        for (idx_d, bias_d, valid_d) in dil_tables:
            o_i, lse_i = gathered_attention(qdh, kdh, vdh, idx_d, bias_d, valid_d)
            outs.append(o_i.astype(jnp.float32))
            lses.append(lse_i)
        alpha = jax.nn.softmax(jnp.stack(lses, 0), axis=0)
        o_dil = jnp.einsum('nbhs,nbhsd->bhsd', alpha, jnp.stack(outs, 0)).astype(x.dtype)

        y = jnp.concatenate([rmsnorm(merge(o_na), out_norm_na_g[l]),
                             rmsnorm(merge(o_dil), out_norm_dil_g[l])], axis=-1) @ w_out[l]
        x = x + g1 * y

        h2 = rmsnorm(x, norm2_g[l]) * (1.0 + sc2) + sh2
        x = x + g2 * peer(h2, peer_wq[l], peer_subkeys[l], peer_u[l], peer_v[l])

    return rmsnorm(x, final_g)


DEPTH_2 = 2

D_MIX_2 = D_MODEL
GLA_HEADS = 4
GLA_DK = 64
GLA_DV = 128
GLA_WIDTH = GLA_HEADS * GLA_DV
GLA_KEY_WIDTH = GLA_HEADS * GLA_DK
GLA_GATE_RANK = 16
GLA_GATE_TEMP = 16.0
GLA_CHUNK = 64
MLA_HEADS = 4
MLA_NOPE = 128
MLA_ROPE = 64
MLA_QK = MLA_NOPE + MLA_ROPE
MLA_DV = 128
MLA_WIDTH = MLA_HEADS * MLA_DV
MLA_Q_RANK = 256
MLA_KV_RANK = 128
ROPE_THETA = 10000.0

IN_SPLITS = (GLA_KEY_WIDTH, GLA_KEY_WIDTH, GLA_WIDTH, GLA_GATE_RANK, GLA_WIDTH,
             MLA_Q_RANK, MLA_KV_RANK, MLA_ROPE, MLA_WIDTH)
D_IN = sum(IN_SPLITS)


def rmsnorm_2(t, g):
    t32 = t.astype(jnp.float32)
    y = t32 * lax.rsqrt(jnp.mean(t32 * t32, axis=-1, keepdims=True) + EPS)
    return (y * g.astype(jnp.float32)).astype(t.dtype)

def apply_rope(t, cos, sin):
    half = t.shape[-1] // 2
    t32 = t.astype(jnp.float32)
    t1, t2 = t32[..., :half], t32[..., half:]
    return jnp.concatenate([t1 * cos - t2 * sin, t1 * sin + t2 * cos], axis=-1).astype(t.dtype)

def gla_mix(q, k, v, log_a, norm_g):
    B, S = q.shape[0], q.shape[1]
    n_chunks = S // GLA_CHUNK

    def to_chunks(t):
        return t.astype(jnp.float32).reshape(B, n_chunks, GLA_CHUNK, GLA_HEADS, -1).transpose(0, 3, 1, 2, 4)

    qc = to_chunks(q) * (GLA_DK ** -0.5)
    kc, vc, lac = to_chunks(k), to_chunks(v), to_chunks(log_a)
    b = jnp.cumsum(lac, axis=3)
    b_last = b[:, :, :, -1:, :]
    q_dec = qc * jnp.exp(b)
    k_inv = kc * jnp.exp(-b)
    k_end = kc * jnp.exp(b_last - b)

    causal = jnp.tril(jnp.ones((GLA_CHUNK, GLA_CHUNK), dtype=bool))
    a_intra = jnp.where(causal, jnp.einsum('bhnik,bhnjk->bhnij', q_dec, k_inv), 0.0)
    o_intra = jnp.einsum('bhnij,bhnjv->bhniv', a_intra, vc)

    chunk_update = jnp.einsum('bhnjk,bhnjv->bhnkv', k_end, vc)
    chunk_decay = jnp.exp(b_last[:, :, :, 0, :])

    def step(state, inp):
        decay, upd = inp
        return decay[..., None] * state + upd, state

    state0 = jnp.zeros((B, GLA_HEADS, GLA_DK, GLA_DV), jnp.float32)
    _, state_prev = lax.scan(step, state0,
                             (jnp.moveaxis(chunk_decay, 2, 0), jnp.moveaxis(chunk_update, 2, 0)))
    state_prev = jnp.moveaxis(state_prev, 0, 2)
    o_inter = jnp.einsum('bhnik,bhnkv->bhniv', q_dec, state_prev)

    o = (o_intra + o_inter).transpose(0, 2, 3, 1, 4).reshape(B, S, GLA_HEADS, GLA_DV)
    o = rmsnorm_2(o.astype(q.dtype), norm_g)
    return o.reshape(B, S, GLA_WIDTH)

def block_causal_attention(q, k, v):
    B, S = q.shape[0], q.shape[1]
    n_blocks = S // Q_BLOCK
    scale = MLA_QK ** -0.5
    kt = k.transpose(0, 2, 1, 3)
    vt = v.transpose(0, 2, 1, 3)
    qb = q.transpose(0, 2, 1, 3).reshape(B, MLA_HEADS, n_blocks, Q_BLOCK, MLA_QK).transpose(2, 0, 1, 3, 4)
    key_idx = jnp.arange(S)

    def one_block(args):
        q_blk, i = args
        s = jnp.einsum('bhqd,bhkd->bhqk', q_blk, kt).astype(jnp.float32) * scale
        q_idx = i * Q_BLOCK + jnp.arange(Q_BLOCK)
        s = jnp.where(key_idx[None, :] <= q_idx[:, None], s, -jnp.inf)
        p = jax.nn.softmax(s, axis=-1).astype(v.dtype)
        return jnp.einsum('bhqk,bhkd->bhqd', p, vt)

    o = lax.map(one_block, (qb, jnp.arange(n_blocks)))
    return o.transpose(1, 0, 3, 2, 4).reshape(B, S, MLA_HEADS * MLA_DV)

def second_inputs(seed: int = 0) -> dict:
    key = jax.random.key(seed)
    ks = jax.random.split(key, 16)
    f32 = jnp.float32

    def w(k, shape, fan_in):
        return jax.random.normal(k, shape, f32) * (fan_in ** -0.5)

    def gain(k, shape):
        return 1.0 + 0.02 * jax.random.normal(k, shape, f32)

    x = jax.random.normal(ks[0], (BATCH, SEQ, D_MODEL), f32)
    offsets = jax.random.randint(ks[1], (BATCH, 1), 0, 1024, dtype=jnp.int32)
    positions = offsets + jnp.arange(SEQ, dtype=jnp.int32)[None, :]
    return {
        "x": x,
        "positions": positions,
        "norm_g": gain(ks[2], (DEPTH_2, D_MODEL)),
        "w_in": w(ks[3], (DEPTH_2, D_MODEL, D_IN), D_MODEL),
        "w_gla_gate_up": w(ks[4], (DEPTH_2, GLA_GATE_RANK, GLA_KEY_WIDTH), GLA_GATE_RANK),
        "b_gla_gate": 0.01 * jax.random.normal(ks[5], (DEPTH_2, GLA_KEY_WIDTH), f32),
        "gla_norm_g": gain(ks[6], (DEPTH_2, GLA_DV)),
        "mla_q_norm_g": gain(ks[7], (DEPTH_2, MLA_Q_RANK)),
        "w_uq": w(ks[8], (DEPTH_2, MLA_Q_RANK, MLA_HEADS * MLA_QK), MLA_Q_RANK),
        "mla_kv_norm_g": gain(ks[9], (DEPTH_2, MLA_KV_RANK)),
        "w_ukv": w(ks[10], (DEPTH_2, MLA_KV_RANK, MLA_HEADS * (MLA_NOPE + MLA_DV)), MLA_KV_RANK),
        "q_head_g": gain(ks[11], (DEPTH_2, MLA_QK)),
        "k_head_g": gain(ks[12], (DEPTH_2, MLA_QK)),
        "w_out": w(ks[13], (DEPTH_2, D_MIX_2, D_MODEL), D_MIX_2),
    }

def second_block(x, positions, norm_g, w_in, w_gla_gate_up, b_gla_gate, gla_norm_g,
              mla_q_norm_g, w_uq, mla_kv_norm_g, w_ukv, q_head_g, k_head_g, w_out):
    B, S = x.shape[0], x.shape[1]
    split_idx = [int(v) for v in np.cumsum(IN_SPLITS)[:-1]]

    inv_freq = ROPE_THETA ** (-jnp.arange(0, MLA_ROPE, 2, dtype=jnp.float32) / MLA_ROPE)
    ang = positions.astype(jnp.float32)[..., None] * inv_freq
    cos = jnp.cos(ang)[:, :, None, :]
    sin = jnp.sin(ang)[:, :, None, :]

    for l in range(DEPTH_2):
        h = rmsnorm_2(x, norm_g[l])
        z = h @ w_in[l]
        (g_q, g_k, g_v, g_lr, g_gate,
         c_q, c_kv, k_pe, m_gate) = jnp.split(z, split_idx, axis=-1)

        gate_logit = (g_lr @ w_gla_gate_up[l] + b_gla_gate[l]).astype(jnp.float32)
        log_a = jax.nn.log_sigmoid(gate_logit) / GLA_GATE_TEMP
        o_gla = gla_mix(g_q.reshape(B, S, GLA_HEADS, GLA_DK),
                        g_k.reshape(B, S, GLA_HEADS, GLA_DK),
                        g_v.reshape(B, S, GLA_HEADS, GLA_DV),
                        log_a.reshape(B, S, GLA_HEADS, GLA_DK),
                        gla_norm_g[l])
        o_gla = o_gla * jax.nn.silu(g_gate)

        q = (rmsnorm_2(c_q, mla_q_norm_g[l]) @ w_uq[l]).reshape(B, S, MLA_HEADS, MLA_QK)
        kv = (rmsnorm_2(c_kv, mla_kv_norm_g[l]) @ w_ukv[l]).reshape(B, S, MLA_HEADS, MLA_NOPE + MLA_DV)
        k_nope, v = kv[..., :MLA_NOPE], kv[..., MLA_NOPE:]
        k_rope = jnp.broadcast_to(k_pe[:, :, None, :], (B, S, MLA_HEADS, MLA_ROPE))
        k = jnp.concatenate([k_nope, k_rope], axis=-1)
        q = rmsnorm_2(q, q_head_g[l])
        k = rmsnorm_2(k, k_head_g[l])
        q = jnp.concatenate([q[..., :MLA_NOPE], apply_rope(q[..., MLA_NOPE:], cos, sin)], axis=-1)
        k = jnp.concatenate([k[..., :MLA_NOPE], apply_rope(k[..., MLA_NOPE:], cos, sin)], axis=-1)
        o_mla = block_causal_attention(q, k, v) * jax.nn.silu(m_gate)

        x = x + jnp.concatenate([o_gla, o_mla], axis=-1) @ w_out[l]
    return x


def setup_inputs(seed=0):
    out = dict(first_inputs(seed))
    for name, value in second_inputs(seed + 1).items():
        if name != "x":
            out[name + "_2"] = value
    return out


def reference(
    x, c, ada_w, ada_b, norm1_g, w_in, na_rpb, out_norm_na_g, out_norm_dil_g, w_out, norm2_g,
    peer_wq, peer_subkeys, peer_u, peer_v, final_g, positions_2, norm_g_2, w_in_2,
    w_gla_gate_up_2, b_gla_gate_2, gla_norm_g_2, mla_q_norm_g_2, w_uq_2, mla_kv_norm_g_2,
    w_ukv_2, q_head_g_2, k_head_g_2, w_out_2,
):
    x = first_block(
        x, c, ada_w, ada_b, norm1_g, w_in, na_rpb, out_norm_na_g, out_norm_dil_g, w_out,
        norm2_g, peer_wq, peer_subkeys, peer_u, peer_v, final_g,
    )
    return second_block(
        x, positions_2, norm_g_2, w_in_2, w_gla_gate_up_2, b_gla_gate_2, gla_norm_g_2,
        mla_q_norm_g_2, w_uq_2, mla_kv_norm_g_2, w_ukv_2, q_head_g_2, k_head_g_2, w_out_2,
    )


_drawn_inputs = setup_inputs


def setup_inputs(seed=0):
    import zlib

    import numpy as np

    out = dict(_drawn_inputs(seed))
    spreads = {}
    factors = {'norm1_g': 2.939,
     'out_norm_na_g': 3.858,
     'out_norm_dil_g': 3.702,
     'b_gla_gate_2': 8.0,
     'gla_norm_g_2': 4.926,
     'mla_q_norm_g_2': 8.0,
     'mla_kv_norm_g_2': 8.0,
     'q_head_g_2': 8.0,
     'k_head_g_2': 8.0}
    for name, (base, spread) in spreads.items():
        noise = np.random.default_rng([zlib.crc32(name.encode()), seed]).standard_normal(out[name].shape)
        drawn = base * np.exp(spread * noise) if base else spread * noise
        out[name] = __import__('jax').numpy.asarray(drawn.astype(out[name].dtype))
    for name, factor in factors.items():
        out[name] = (out[name] * factor).astype(out[name].dtype)
    return out
```

```python
from contextlib import ExitStack

import numpy as np

import concourse.bass as bass
from concourse import mybir

ALU = mybir.AluOpType
ACT = mybir.ActivationFunctionType
F32 = mybir.dt.float32
BF16 = mybir.dt.bfloat16
U32 = mybir.dt.uint32
I32 = mybir.dt.int32
AX = mybir.AxisListType

P = 128
S = 256
NT = S // P
D = 1024
KD = D // P
EPS = 1e-6
NEG = 1e30

HD = 64
NH = 16
GRID_W = 64
ROWS = S // GRID_W
RPB_R, RPB_C = 15, 31
PH = 8
NKEY = 128
TOPK = 16
SLOTS = PH * TOPK
GROUP = 8
NG = NT * SLOTS // GROUP

LAYERS = 2
GH, GDK, GDV, GCH = 4, 64, 128, 64
GATE_TEMP = 16.0
MH, NOPE, ROPE, MDV = 4, 128, 64, 128
QK = NOPE + ROPE
QR, KVR = 256, 128
D_IN = 2512
LR = 16
O_V, O_LR, O_GG, O_C, O_MG = 512, 1024, 1040, 1552, 2000
CW = QR + KVR + ROPE

CONST = {}
_at = 0
for _name, _w in (("ident", 128), ("flip", 128), ("na_window", 512), ("segment", 256), ("same_chunk", 128),
                  ("causal", 384), ("inv_freq", 32), ("iota", 16)):
    CONST[_name] = (_at, _at + _w)
    _at += _w
NCONST = _at


def shape_constants():
    c = np.zeros((P, NCONST), np.float32)

    def put(name, value):
        a, b = CONST[name]
        c[:, a:b] = value

    p = np.arange(P)
    put("ident", np.eye(P))
    put("flip", (p[:, None] // 64 == p[None, :] // 64) & (p[:, None] % 64 == 63 - p[None, :] % 64))
    q = (np.arange(NT)[None, :, None] * P + p[:, None, None])
    k = np.arange(S)[None, None, :]
    c0 = np.clip(q % GRID_W - 8, 0, GRID_W - 16)
    inside = (k % GRID_W >= c0) & (k % GRID_W < c0 + 16)
    put("na_window", np.where(inside, 0.0, NEG).reshape(P, -1))
    put("segment", np.broadcast_to((np.arange(S) % GCH != 0), (P, S)))
    put("same_chunk", (p[:, None] // GCH == p[None, :] // GCH) & (p[:, None] <= p[None, :]))
    tri = np.where(p[None, :] <= p[:, None], 0.0, -NEG)
    put("causal", np.concatenate([tri, np.zeros((P, P)), tri], 1))
    put("inv_freq", np.broadcast_to(10000.0 ** (-np.arange(0, ROPE, 2) / ROPE), (P, ROPE // 2)))
    put("iota", np.broadcast_to(np.arange(16), (P, 16)))
    d = np.abs(q - k)
    count = (d <= 64).astype(int) + (d % 4 == 0) + (d % 16 == 0)
    logc = np.log(np.maximum(count, 1).astype(np.float64))
    slopes = 2.0 ** (-(np.arange(8) + 1.0))
    dil = slopes[None, :, None, None] * d[:, None] - logc[:, None]
    dil = np.where(count[:, None] > 0, dil, NEG).astype(np.float32)
    return c, np.ascontiguousarray(dil.reshape(P, -1))


class Banks:

    def __init__(self):
        self.uses = [0] * 8
        self.jobs = {}
        self.next = 0
        self.base = None

    def plan(self, name, bank=None):
        if bank is None:
            bank, self.next = self.next, (self.next + 1) % 6
        self.jobs[name] = (bank, self.uses[bank], self.base is not None)
        self.uses[bank] += 1

    def start_layer(self):
        self.base = list(self.uses)

    def end_layer(self):
        self.per_layer = [u - b for u, b in zip(self.uses, self.base)]

    def before(self, name, layer):
        bank, n, in_layer = self.jobs[name]
        return bank, (layer * self.per_layer[bank] + n if in_layer else n)


def attention_schedule():
    out, fill = [], 4
    for h in range(NH + 2):
        if h < NH:
            out.append(("S", h))
            if h % 2 == 0:
                out.append(("ada", fill))
                fill += 1
        if 1 <= h <= NH:
            out.append(("PT", h - 1))
        if h >= 2:
            out.append(("PV", h - 2))
            if (h - 2) % 8 == 7:
                out.append(("O", (h - 2) // 8))
    return out


def mla_schedule():
    out = []
    for h in range(MH + 2):
        if h < MH:
            out.append(("ms", h))
        if 1 <= h <= MH:
            out.append(("mPT", h - 1))
        if h >= 2:
            out.append(("mPV", h - 2))
    return out


def plan_banks():
    b = Banks()
    for i in range(8):
        b.plan(("nab", i))
    for n in range(4):
        b.plan(("ada", n))
    for t in range(NT):
        for g in range(2):
            b.plan(("xT", t, g))
    for ch in (0, 1, 3, 4):
        for j in range(2):
            b.plan(("qk", ch, j))
    for ch in (2, 5):
        for t in range(NT):
            b.plan(("v", ch, t))
    for kind, i in attention_schedule():
        if kind == "O":
            continue
        if kind == "PV":
            if i % 8 == 0:
                for qt in range(NT):
                    b.plan(("O", i // 8, qt), 6 + qt)
        else:
            b.plan((kind, i))
    for t in range(NT):
        for g in range(2):
            b.plan(("oT", t, g))
    for ch in range(2):
        for t in range(NT):
            b.plan(("y", ch, t))
    for t in range(NT):
        for g in range(2):
            b.plan(("hT", t, g))
    b.plan(("skT",))
    for ch in range(4):
        for j in range(2):
            b.plan(("pq", ch, j))
    for t in range(NT):
        for g in range(4):
            b.plan(("sc", t, g))
    for t in range(NT):
        for half in range(2):
            b.plan(("peer", t, half), 6 + half if t == 0 else 4 + half)
    b.next = 0
    b.start_layer()
    for t in range(NT):
        for g in range(2):
            b.plan(("zT", t, g))
    for j in range(2):
        b.plan(("gqk", j))
    b.plan(("lr",))
    for t in range(NT):
        b.plan(("c", t))
    b.plan(("gl",))
    for t in range(NT):
        b.plan(("gv", t))
    for t in range(NT):
        b.plan(("cT", t))
    b.plan(("keT",))
    for t in range(NT):
        for hp in range(2):
            b.plan(("uq", t, hp))
            b.plan(("ukv", t, hp))
    for odd in range(2):
        b.plan(("A", odd))
    for i in range(3):
        b.plan(("U", i))
    for t in range(NT):
        b.plan(("gg", t))
    for t in range(NT):
        b.plan(("mg", t))
    for odd in range(2):
        b.plan(("go", odd), 6 + odd)
    for t in range(NT):
        b.plan(("qnT", t))
        b.plan(("knT", t))
    b.plan(("qrT",))
    b.plan(("krT",))
    for kind, i in mla_schedule():
        if kind == "mPV":
            if i == 0:
                for qt in range(NT):
                    b.plan(("mo", qt), 6 + qt)
        else:
            b.plan((kind, i))
    for t in range(NT):
        for g in range(2):
            b.plan(("cT2", t, g))
    for ch in range(2):
        for t in range(NT):
            b.plan(("y2", ch, t))
    b.end_layer()
    return b


class Chain:

    def __init__(self, eng, sem):
        self.eng, self.sem, self.n, self.turn = eng, sem, 0, None

    def step(self, ins):
        ins.then_inc(self.sem, 1)
        self.n += 1

    def wait(self):
        self.eng.wait_ge(self.sem, self.n if self.turn is None else self.turn * self.per + self.n)

    def link(self, ins):
        self.step(ins)
        self.wait()

    def loop(self, turn, per):
        self.turn, self.per, self.from_ = turn, per, self.n

    def end_loop(self, turns):
        assert self.n - self.from_ == self.per, (self.n - self.from_, self.per)
        self.n, self.turn = self.from_ + self.per * turns, None


def program(nc, x, c, ada_w, ada_b, norm1_g, w_in, na_rpb, out_norm_na_g, out_norm_dil_g, w_out, norm2_g,
            peer_wq, peer_subkeys, peer_u, peer_v, final_g, positions_2, norm_g_2, w_in_2, w_gla_gate_up_2,
            b_gla_gate_2, gla_norm_g_2, mla_q_norm_g_2, w_uq_2, mla_kv_norm_g_2, w_ukv_2, q_head_g_2,
            k_head_g_2, w_out_2, shape_const, dil_bias_const, out):
    ctx = ExitStack()
    with ctx:
        def sb(name, shape, dt=F32):
            return ctx.enter_context(nc.sbuf_tensor(name, shape, dt))

        def sem(name):
            return ctx.enter_context(nc.semaphore(name))

        banks = plan_banks()
        bank = [ctx.enter_context(nc.psum_tensor(f"bank{i}", [P, 512], F32)) for i in range(8)]

        wring = sb("wring", [P, 4, 4096])
        xrow = sb("xrow", [P, NT, D])
        hrow = sb("hrow", [P, NT, D])
        hT = sb("hT", [P, KD, S])
        modb = sb("modb", [P, 6, D])
        gains = sb("gains", [P, 3, D])
        R = sb("R", [P, 16384])
        silu_cb = sb("silu_cb", [P, KD, P])
        pT = sb("pT", [P, 2, 512])
        const = sb("const", [P, NCONST - 640])
        skrow = sb("skrow", [P, 2, P])
        skT = sb("skT", [P, 2, P])
        ids = sb("ids", [P, NT * SLOTS], U32)
        gates = sb("gates", [P, NT * SLOTS])
        rope = sb("rope", [P, NT, 2, ROPE // 2])
        small = sb("small", [P, 256])

        def region(at, *shape, dt=F32):
            n = int(np.prod(shape))
            v = R[:, at:at + n] if dt == F32 else R[:, at:at + n].bitcast(dt)
            names = "abcd"[:len(shape)]
            return v if len(shape) == 1 else v.rearrange(
                f"p ({' '.join(names)}) -> p {' '.join(names)}", **dict(zip(names[1:], shape[1:])))

        early = {"flip": (6144 + 4096 * 2, 128), "na_window": (6144 + 4096 * 2 + 128, 512)}
        kept = ["ident", "segment", "same_chunk", "causal", "inv_freq", "iota"]
        at_const, where = 0, {}
        for name in kept:
            a, b = CONST[name]
            where[name] = const[:, at_const:at_const + b - a]
            at_const += b - a
        ident, segment, causal, inv_freq, iota = (where[n] for n in ("ident", "segment", "causal", "inv_freq", "iota"))
        same_chunk = where["same_chunk"].bitcast(U32)

        bias = region(0, NH, NT, S)
        qkT = region(8192, 16, S)
        na_raw = region(8192, NT, 8, S)
        vrow = region(12288, NT, D)
        flip = region(12288, P)
        na_window = region(12288 + 128, NT, S)
        Tm = region(14336, 2, NT, S)
        Em = region(15360, 2, NT, S)
        junk = R[:, 15872:16384].bitcast(BF16)
        pqT = region(0, 16, S)
        scores = region(4096, NT, 16, NKEY)
        cand = region(8192, PH, TOPK * TOPK)
        hit = region(10240, PH, TOPK, TOPK)
        top_v = region(12288, NT, PH, 2, TOPK)
        top_i = region(12800, NT, PH, 2, TOPK, dt=U32)
        best_v = region(13312, NT, PH, TOPK)
        best_j = region(13568, PH, TOPK, dt=U32)
        best_ab = region(13696, 2, PH, TOPK, dt=U32)
        picked = region(13952, 2, PH, TOPK)
        ytmp = region(14336, 2, 512)
        urow = wring[:, 0:2, :].rearrange("p a (b d) -> p (a b) d", d=D)
        vgat = wring[:, 2:4, :].rearrange("p a (b d) -> p (a b) d", d=D)
        diag = hT[:, :, :].rearrange("p a b -> p (a b)").rearrange("p (s m) -> p s m", m=P)
        zeros = pT[:, 0, 0:P]

        M = modb[:, :, :].rearrange("p a b -> p (a b)")

        def mod_region(at, *shape):
            n = int(np.prod(shape))
            names = "abcd"[:len(shape)]
            return M[:, at:at + n].rearrange(
                f"p ({' '.join(names)}) -> p {' '.join(names)}", **dict(zip(names[1:], shape[1:])))

        gqT = mod_region(0, 2, S)
        gkT = mod_region(512, 2, S)
        log_a = mod_region(1024, 2, S)
        gtmp = mod_region(1536, 2, S)
        bcum = mod_region(2048, 2, S)
        eb = mod_region(2560, 2, S)
        ki = mod_region(3072, 2, S)
        ke = mod_region(3584, 2, S)
        keR = mod_region(4096, NT, 2, P)
        aT = mod_region(4608, NT, GH, P)
        up = mod_region(5632, 256)
        lrT = mod_region(5888, 256)
        gv = region(0, NT, 512)
        state = region(1024, 3, 2, GDV)
        crow = region(1792, NT, CW)
        cqT = region(2688, 3, S)
        qrow = region(3456, NT, MH, QK)
        kvrow = region(4992, NT, MH, NOPE + MDV)
        qrr = region(7040, NT, MH, ROPE)
        krr = region(7552, NT, MH, ROPE)
        qnT = region(8064, MH, S)
        knT = region(9088, MH, S)
        qrT = region(10112, 2, S)
        krT = region(10624, 2, S)
        mT = region(11136, 2, 384)
        mE = region(11904, 2, 384)
        mPT = pT[:, :, 0:384]
        silu_g = region(12672, NT, 512)
        silu_m = region(13696, NT, 512)
        wide = region(14720, 768)
        kpe = region(15488, NT, ROPE)
        kpr = region(15616, NT, ROPE)
        gains2 = gains[:, 1:3, :].rearrange("p a b -> p (a b)")
        g_in, g_gla, g_q, g_kv = gains2[:, 0:1024], gains2[:, 1024:1152], gains2[:, 1152:1408], gains2[:, 1408:1536]
        g_qh, g_kh = gains2[:, 1536:1728], gains2[:, 1728:1920]

        def col(a, n=1):
            return small[:, a:a + n]

        cT, csil = col(0, 8), col(8, 8)
        ss, rstd = col(16, 16), col(32, 16)
        accmin = col(48, 4)
        rsum = small[:, 56:88].rearrange("p (t h) -> p t h", t=NT)
        rinv = small[:, 88:104].rearrange("p (t h) -> p t h", t=NT)
        bgate = col(104, 2)
        posf = col(106, 2)
        posi = small[:, 108:110].bitcast(I32)
        a8 = small[:, 112:128].rearrange("p (b s) -> p b s", b=2)
        g8 = small[:, 128:144].rearrange("p (b s) -> p b s", b=2)
        w8 = small[:, 144:160].rearrange("p (b s) -> p b s", b=2)
        idu = small[:, 160:176].bitcast(U32).rearrange("p (b s) -> p b s", b=2)
        idv = small[:, 176:192].bitcast(U32).rearrange("p (b s) -> p b s", b=2)
        decay = small[:, 192:200].rearrange("p (a c) -> p a c", a=2)
        ssh, rstdh = col(200, 24), col(224, 24)
        eps = col(248)
        half_pi = col(249)
        gsum = small[:, 208:224]
        ssg = col(240, 8)

        w_landed = [sem(f"w_landed{i}") for i in range(4)]
        bank_full = [sem(f"bank_full{i}") for i in range(8)]
        bank_free = [sem(f"bank_free{i}") for i in range(8)]
        x_landed, c_landed, const_landed, gains_landed = sem("x_landed"), sem("c_landed"), sem("const_landed"), sem("gains_landed")
        adab_landed, rpb_landed, dil_landed, sk_landed = sem("adab_landed"), sem("rpb_landed"), sem("dil_landed"), sem("sk_landed")
        fing_landed, gains2_landed = sem("fing_landed"), sem("gains2_landed")
        act_step, dve_step, pool_step = sem("act_step"), sem("dve_step"), sem("pool_step")
        consts_set = sem("consts_set")
        silu_ready = sem("silu_ready")
        cb_ready = sem("cb_ready")
        ang_ready = sem("ang_ready")
        rope_ready = sem("rope_ready")
        rstd_ready = sem("rstd_ready")
        rows_ready = sem("rows_ready")
        masked_ready = sem("masked_ready")
        exp_ready = sem("exp_ready")
        pv_done = sem("pv_done")
        x_ready = sem("x_ready")
        softmax_shift = sem("softmax_shift")
        gate_exp = sem("gate_exp")
        ids_ready = sem("ids_ready")
        u_landed = [sem(f"u_landed{i}") for i in range(GROUP)]
        v_landed = [sem(f"v_landed{i}") for i in range(GROUP)]
        u_free = sem("u_free")
        gelu_ready = sem("gelu_ready")
        weights_ready = sem("weights_ready")
        diag_ready = sem("diag_ready")
        v_free = sem("v_free")
        exp_gate = sem("exp_gate")
        dve_to_act = sem("dve_to_act")
        dve_to_pe = sem("dve_to_pe")
        m_masked, m_exp, m_pv = sem("m_masked"), sem("m_exp"), sem("m_pv")
        gains2_used = sem("gains2_used")
        waits_passed = sem("waits_passed")
        out_done = sem("out_done")

        def claim(pe, job, l=None):
            b, n = banks.before(job, l)
            if l is not None or n > 0:
                pe.wait_ge(bank_free[b], n)
            return bank[b]

        def full(ins, job):
            ins.then_inc(bank_full[banks.jobs[job][0]], 1)

        def await_full(eng, job, l=None):
            b, n = banks.before(job, l)
            eng.wait_ge(bank_full[b], n + 1)
            return bank[b]

        def free(ins, job):
            ins.then_inc(bank_free[banks.jobs[job][0]], 1)

        def drained(eng, job, l=None):
            b, n = banks.before(job, l)
            eng.wait_ge(bank_free[b], n + 1)

        def wait_alone(eng):
            eng.sem_inc(waits_passed, 1)

        def quad(ap):
            return ap.rearrange("p (a b) -> p a b", a=4)

        def chunk_dram(w, l, a, b):
            return w[l, :, a:b].rearrange("(k p) n -> p k n", p=P)

        W1 = [(ada_w, 512 * n, ("ada", n)) for n in range(4)]
        W1 += [(w_in, 512 * n, ("v", n, 1) if n in (2, 5) else ("qk", n, 1)) for n in (0, 1, 3, 4, 2, 5)]
        W1 += [(ada_w, 512 * n, ("ada", n)) for n in range(4, 12)]
        W1 += [(w_out, 512 * n, ("y", n, 1)) for n in range(2)]
        W1 += [(peer_wq, 512 * n, ("pq", n, 1)) for n in range(4)]
        W1_AT = {job: n for n, (_, _, job) in enumerate(W1)}
        CPL = 8
        W1_USES = len(W1) // 4

        def slot512(n):
            return wring[:, n % 4, :].rearrange("p (k m) -> p k m", k=KD)

        def weights1(pe, job):
            n = W1_AT[job]
            pe.wait_ge(w_landed[n % 4], 16 * (n // 4 + 1))
            return slot512(n)

        DMAS2 = [1, 2, 1, 2, 1, 1, 1, 1]

        def landed2(eng, n, l):
            s = n % 4
            per = 16 * (DMAS2[s] + DMAS2[s + 4])
            here = 16 * sum(DMAS2[j] for j in range(s, n + 1, 4))
            eng.wait_ge(w_landed[s], l * per + 16 * W1_USES + here)
            return wring[:, s, :]

        LAST2 = [("gqk", 1), ("c", 1), ("gv", 1), ("ukv", 1, 1), ("gg", 1), ("mg", 1), ("y2", 0, 1), ("y2", 1, 1)]

        block = ctx.enter_context(nc.Block())

        @block.sync
        def _(sp):
            for n, (w, a, _) in enumerate(W1):
                if n >= 4:
                    await_full(sp, W1[n - 4][2])
                sp.dma_start(slot512(n), chunk_dram(w, 0, a, a + 512)).then_inc(w_landed[n % 4], 16)

            def layer_chunk(n, l):
                dst, s = wring[:, n % 4, :], w_landed[n % 4]
                if n == 3:
                    sp.dma_start(dst[:, 0:1536].rearrange("p (k m) -> p k m", k=2),
                                 w_uq_2[l].rearrange("(k p) n -> p k n", p=P)).then_inc(s, 16)
                    sp.dma_start(dst[:, 1536:2560], w_ukv_2[l]).then_inc(s, 16)
                elif n == 1:
                    d = dst.rearrange("p (k m) -> p k m", k=KD)
                    sp.dma_start(d[:, :, 0:LR], chunk_dram(w_in_2, l, O_LR, O_LR + LR)).then_inc(s, 16)
                    sp.dma_start(d[:, :, LR:LR + CW], chunk_dram(w_in_2, l, O_C, O_C + CW)).then_inc(s, 16)
                else:
                    w, a = {0: (w_in_2, 0), 2: (w_in_2, O_V), 4: (w_in_2, O_GG), 5: (w_in_2, O_MG),
                            6: (w_out_2, 0), 7: (w_out_2, 512)}[n]
                    sp.dma_start(dst.rearrange("p (k m) -> p k m", k=KD), chunk_dram(w, l, a, a + 512)).then_inc(s, 16)

            for n in range(4):
                sp.wait_ge(u_free if n < 2 else v_free, NG * GROUP)
                layer_chunk(n, 0)
            with sp.Fori(0, LAYERS - 1) as l:
                for n in range(4, CPL):
                    await_full(sp, LAST2[n - 4], l)
                    layer_chunk(n, l)
                for n in range(4):
                    await_full(sp, LAST2[n + 4], l)
                    layer_chunk(n, l + 1)
            for n in range(4, CPL):
                await_full(sp, LAST2[n - 4], LAYERS - 1)
                layer_chunk(n, LAYERS - 1)
            sp.wait_ge(x_ready, NT * (3 + LAYERS))
            sp.dma_start(out[0].rearrange("(t p) d -> p t d", p=P), xrow[:, :, :]).then_inc(out_done, 16)
            sp.wait_ge(out_done, 16)

        @block.gpsimd
        def _(pool):
            chain = Chain(pool, pool_step)

            pool.dma_start(modb[:, :, :].rearrange("p a b -> p (a b)"), ada_b[0].partition_broadcast(P)).then_inc(adab_landed, 16)
            pool.dma_start(gains[:, 0, :], norm1_g[0].partition_broadcast(P)).then_inc(gains_landed, 16)
            pool.dma_start(gains[:, 1, :], norm2_g[0].partition_broadcast(P)).then_inc(gains_landed, 16)
            pool.dma_start(gains[:, 2, 0:512], out_norm_na_g[0].partition_broadcast(P)).then_inc(gains_landed, 16)
            pool.dma_start(gains[:, 2, 512:1024], out_norm_dil_g[0].partition_broadcast(P)).then_inc(gains_landed, 16)
            pool.dma_start(skrow[:, :, :], peer_subkeys[0].rearrange("s n d -> n s d")).then_inc(sk_landed, 16)

            pool.wait_ge(rows_ready, NT)
            pool.dma_start(gains[:, 0, :], final_g.partition_broadcast(P)).then_inc(fing_landed, 16)

            def gather(dst, table, index, landed):
                wait_alone(pool)
                pool.indirect_dma_start(dst, None, table, bass.IndirectOffsetOnAxis(index, 0)).then_inc(landed, 16)

            def stage_ids(dst, n):
                wait_alone(pool)
                chain.link(pool.tensor_copy(dst, ids[:, bass.ds(n * GROUP, GROUP)] if not isinstance(n, int)
                                            else ids[:, n * GROUP:(n + 1) * GROUP]))

            def u_rows(n, s, b, first=False):
                if not first:
                    pool.wait_ge(u_free, (n - 1) * GROUP + s + 1)
                gather(urow[:, s, :], peer_u[0], idu[:, b, s:s + 1], u_landed[s])

            def v_rows(n, s, b, first=False):
                if not first:
                    pool.wait_ge(v_free, (n - 1) * GROUP + s + 1)
                gather(vgat[:, s, :], peer_v[0], idv[:, b, s:s + 1], v_landed[s])

            def pair(n, first=False, last=False):
                for b in range(2):
                    if not (last and b == 1):
                        stage_ids(idu[:, (b + 1) % 2, :], n + b + 1)
                    stage_ids(idv[:, b, :], n + b)
                    for s in range(GROUP):
                        if not (last and b == 1):
                            u_rows(n + b + 1, s, (b + 1) % 2)
                        v_rows(n + b, s, b, first and b == 0)

            pool.wait_ge(ids_ready, NT)
            await_full(pool, ("pq", 3, 1))
            stage_ids(idu[:, 0, :], 0)
            for s in range(GROUP):
                u_rows(0, s, 0, first=True)
            pair(0, first=True)
            with pool.Fori(1, NG // 2 - 1) as m:
                chain.loop(m - 1, 4)
                pair(m * 2)
                chain.end_loop(NG // 2 - 2)
            pair(NG - 2, last=True)

            def load_gains(l):
                at = 0
                for g, n in ((norm_g_2, 1024), (gla_norm_g_2, 128), (mla_q_norm_g_2, 256), (mla_kv_norm_g_2, 128),
                             (q_head_g_2, QK), (k_head_g_2, QK)):
                    pool.dma_start(gains2[:, at:at + n], g[l].partition_broadcast(P)).then_inc(gains2_landed, 16)
                    at += n
                pool.dma_start(bgate, b_gla_gate_2[l].rearrange("(a p) -> p a", p=P), allow_slow_non_contiguous=True).then_inc(gains2_landed, 16)
                pool.dma_start(up[0:LR, :], w_gla_gate_up_2[l]).then_inc(gains2_landed, 16)

            pool.wait_ge(x_ready, NT * 2)
            load_gains(0)
            pool.wait_ge(gains2_used, 1)
            load_gains(1)

        @block.scalar
        def _(act):
            chain = Chain(act, act_step)

            act.dma_start(cT, c[0].rearrange("(k p) -> p k", p=P), allow_slow_non_contiguous=True).then_inc(c_landed, 16)
            act.dma_start(xrow[:, :, :], x[0].rearrange("(t p) d -> p t d", p=P)).then_inc(x_landed, 16)
            for name in kept:
                a, b = CONST[name]
                act.dma_start(where[name], shape_const[:, a:b]).then_inc(const_landed, 16)
            a, b = CONST["flip"]
            act.dma_start(flip, shape_const[:, a:b]).then_inc(const_landed, 16)
            a, b = CONST["na_window"]
            act.dma_start(na_window.rearrange("p t s -> p (t s)"), shape_const[:, a:b]).then_inc(const_landed, 16)
            act.dma_start(posi, positions_2[0].rearrange("(t p) -> p t", p=P), allow_slow_non_contiguous=True).then_inc(const_landed, 16)
            for r in range(ROWS):
                pb, qt = 64 * (r % 2), r // 2
                for kr in range(ROWS):
                    src = bass.AP(na_rpb.tensor, (kr - r + 7) * RPB_C - 48, [[1, 64], [RPB_R * RPB_C, 8], [1, 64]])
                    act.dma_start(na_raw[pb:pb + 64, qt, :, kr * GRID_W:(kr + 1) * GRID_W], src).then_inc(rpb_landed, 16)
            act.dma_start(bias[:, 8:16, :, :].rearrange("p h t s -> p (h t s)"), dil_bias_const).then_inc(dil_landed, 16)

            def rms(srcs, dim, cols, dst=None):
                for s, i in zip(srcs, cols):
                    w = int(np.prod(s.shape[1:]))
                    chain.link(act.activation(junk[:, 0:w], s, ACT.Square, accum_out=ss[:, i:i + 1]))
                a, b = cols[0], cols[-1] + 1
                chain.wait()
                chain.link(act.activation(ss[:, a:b], ss[:, a:b], ACT.Ln, scale=1.0 / dim, bias=eps))
                return act.activation(rstd[:, a:b], ss[:, a:b], ACT.Exp, scale=-0.5)

            act.wait_ge(c_landed, 16)
            act.activation(csil, cT, ACT.Silu).then_inc(silu_ready, 1)
            act.wait_ge(ang_ready, 1)
            act.activation(rope[:, :, :, :].rearrange("p t s f -> p (t s f)"),
                           rope[:, :, :, :].rearrange("p t s f -> p (t s f)"), ACT.Sin).then_inc(rope_ready, 1)
            act.wait_ge(x_landed, 16)
            act.wait_ge(consts_set, 1)
            rms([xrow[:, t, :] for t in range(NT)], D, [0, 1]).then_inc(rstd_ready, 1)

            def evac_T(kind, l=None):
                for t in range(NT):
                    for g in range(2):
                        pb = await_full(act, (kind, t, g), l)
                        free(act.activation(hT[:, 4 * g:4 * g + 4, t * P:(t + 1) * P], quad(pb[:, :]), ACT.Copy), (kind, t, g))

            evac_T("xT")
            for ch in (0, 1, 3, 4):
                for j in range(2):
                    pb = await_full(act, ("qk", ch, j))
                    i = {0: 0, 1: 4, 3: 8, 4: 12}[ch] + 2 * j
                    free(act.activation(qkT[:, i:i + 2, :].rearrange("p a b -> p (a b)"), pb[:, :], ACT.Copy,
                                        scale=-HD ** -0.5 if ch in (0, 3) else 1.0), ("qk", ch, j))
            for ch in (2, 5):
                for t in range(NT):
                    pb = await_full(act, ("v", ch, t))
                    a = 0 if ch == 2 else 512
                    free(act.activation(vrow[:, t, a:a + 512], pb[:, :], ACT.Copy), ("v", ch, t))

            for h in range(NH):
                act.wait_ge(masked_ready, h + 1)
                if h >= 2:
                    await_full(act, ("PT", h - 2))
                for qt in range(NT):
                    i = 2 * (h % 2) + qt
                    act.activation(Em[:, h % 2, qt, :], Tm[:, h % 2, qt, :], ACT.Exp, scale=-1.0,
                                   bias=accmin[:, i:i + 1], accum_out=rsum[:, qt, h:h + 1]).then_inc(exp_ready, 1)

            act.wait_ge(rows_ready, NT + 1)
            rms([hrow[:, t, g * 512:(g + 1) * 512] for t in range(NT) for g in range(2)], 512, [0, 1, 2, 3]).then_inc(rstd_ready, 1)
            evac_T("oT")
            for t in range(NT):
                act.wait_ge(x_ready, t + 1)
                rms([xrow[:, t, :]], D, [t]).then_inc(rstd_ready, 1)
            evac_T("hT")
            for ch in range(4):
                for j in range(2):
                    pb = await_full(act, ("pq", ch, j))
                    i = 4 * ch + 2 * j
                    free(act.activation(pqT[:, i:i + 2, :].rearrange("p a b -> p (a b)"), pb[:, :], ACT.Copy), ("pq", ch, j))
            for t in range(NT):
                for g in range(4):
                    pb = await_full(act, ("sc", t, g))
                    free(act.activation(scores[:, t, 4 * g:4 * g + 4, :].rearrange("p a b -> p (a b)"), pb[:, :], ACT.Copy),
                         ("sc", t, g))
            for t in range(NT):
                act.wait_ge(softmax_shift, t + 1)
                g = gates[:, t * SLOTS:(t + 1) * SLOTS]
                act.activation(g, g, ACT.Exp).then_inc(gate_exp, 1)

            def peer_group(n, b, first=False):
                act.wait_ge(u_free, (n + 1) * GROUP)
                act.activation(g8[:, b, :], a8[:, b, :], ACT.Gelu).then_inc(gelu_ready, 1)
                act.wait_ge(weights_ready, n + 1)
                for s in range(GROUP):
                    if not first:
                        act.wait_ge(v_free, (n - 2) * GROUP + s + 1)
                    act.activation(diag[:, b * GROUP + s, :], ident, ACT.Copy, scale=w8[:, b, s:s + 1]).then_inc(diag_ready, 1)

            for b in range(2):
                peer_group(b, b, first=True)
            with act.Fori(1, NG // 2) as m:
                for b in range(2):
                    peer_group(m * 2 + b, b)

            for t in range(NT):
                act.wait_ge(x_ready, NT + t + 1)
                rms([xrow[:, t, :]], D, [t]).then_inc(rstd_ready, 1)

            with act.Fori(0, LAYERS) as l:
                chain.loop(l, 48)
                for t in range(NT):
                    act.wait_ge(x_ready, l * NT + NT * 2 + t + 1)
                rms([xrow[:, t, :] for t in range(NT)], D, [4, 5]).then_inc(rstd_ready, 1)
                evac_T("zT", l)
                for j in range(2):
                    pb = await_full(act, ("gqk", j), l)
                    dst = (gqT, gkT)[j]
                    free(act.activation(dst.rearrange("p a b -> p (a b)"), pb[:, :], ACT.Copy,
                                        scale=GDK ** -0.5 if j == 0 else 1.0), ("gqk", j))
                pb = await_full(act, ("lr",), l)
                free(act.activation(lrT[0:LR, :], pb[0:LR, 0:S], ACT.Copy), ("lr",))
                for t in range(NT):
                    pb = await_full(act, ("c", t), l)
                    chain.link(act.activation(junk[:, 0:QR], pb[:, 0:QR], ACT.Square, accum_out=ss[:, 6 + t:7 + t]))
                    chain.link(act.activation(junk[:, 0:KVR], pb[:, QR:QR + KVR], ACT.Square, accum_out=ss[:, 8 + t:9 + t]))
                    free(act.activation(crow[:, t, :], pb[:, 0:CW], ACT.Copy), ("c", t))
                chain.wait()
                chain.step(act.activation(ss[:, 6:8], ss[:, 6:8], ACT.Ln, scale=1.0 / QR, bias=eps))
                chain.link(act.activation(ss[:, 8:10], ss[:, 8:10], ACT.Ln, scale=1.0 / KVR, bias=eps))
                act.activation(rstd[:, 6:10], ss[:, 6:10], ACT.Exp, scale=-0.5).then_inc(rstd_ready, 1)
                act.wait_ge(gains2_landed, l * 128 + 128)
                pb = await_full(act, ("gl",), l)
                for a in range(2):
                    chain.step(act.activation(gtmp[:, a, :], pb[:, a * S:(a + 1) * S], ACT.Abs, bias=bgate[:, a:a + 1]))
                chain.wait()
                gt = gtmp.rearrange("p a b -> p (a b)")
                chain.link(act.activation(gt, gt, ACT.Exp, scale=-1.0))
                act.activation(gt, gt, ACT.Ln, bias=1.0).then_inc(exp_gate, 1)
                for t in range(NT):
                    pb = await_full(act, ("gv", t), l)
                    free(act.activation(gv[:, t, :], pb[:, :], ACT.Copy), ("gv", t))
                act.wait_ge(dve_to_act, l * 2 + 1)
                act.activation(eb.rearrange("p a b -> p (a b)"), bcum.rearrange("p a b -> p (a b)"), ACT.Exp,
                               scale=1.0 / GATE_TEMP).then_inc(exp_gate, 1)
                act.activation(ki.rearrange("p a b -> p (a b)"), bcum.rearrange("p a b -> p (a b)"), ACT.Exp,
                               scale=-1.0 / GATE_TEMP).then_inc(exp_gate, 1)
                act.wait_ge(dve_to_act, l * 2 + 2)
                act.activation(ke.rearrange("p a b -> p (a b)"), ke.rearrange("p a b -> p (a b)"), ACT.Exp,
                               scale=1.0 / GATE_TEMP).then_inc(exp_gate, 1)
                for t in range(NT):
                    pb = await_full(act, ("cT", t), l)
                    free(act.activation(cqT[:, :, t * P:(t + 1) * P], pb[:, 0:384].rearrange("p (a b) -> p a b", a=3), ACT.Copy),
                         ("cT", t))
                for t in range(NT):
                    chain.link(act.activation(junk[:, 0:ROPE], crow[:, t, QR + KVR:CW], ACT.Square,
                                              accum_out=ssh[:, 16 + t:17 + t]))
                    for hp in range(2):
                        pb = await_full(act, ("uq", t, hp), l)
                        for i in range(2):
                            h = 2 * hp + i
                            chain.link(act.activation(junk[:, 0:QK], pb[:, i * QK:(i + 1) * QK], ACT.Square,
                                                      accum_out=ssh[:, 4 * t + h:4 * t + h + 1]))
                        free(act.activation(qrow[:, t, 2 * hp:2 * hp + 2, :].rearrange("p a b -> p (a b)"),
                                            pb[:, 0:2 * QK], ACT.Copy), ("uq", t, hp))
                        pb = await_full(act, ("ukv", t, hp), l)
                        for i in range(2):
                            h = 2 * hp + i
                            chain.link(act.activation(junk[:, 0:NOPE], pb[:, i * 256:i * 256 + NOPE], ACT.Square,
                                                      accum_out=ssh[:, 8 + 4 * t + h:9 + 4 * t + h]))
                        free(act.activation(kvrow[:, t, 2 * hp:2 * hp + 2, :].rearrange("p a b -> p (a b)"),
                                            pb[:, :], ACT.Copy), ("ukv", t, hp))
                    for h in range(MH):
                        i = 8 + 4 * t + h
                        if h == 0:
                            chain.wait()
                        chain.step(act.activation(ssh[:, i:i + 1], ssh[:, i:i + 1], ACT.Identity, bias=ssh[:, 16 + t:17 + t]))
                chain.wait()
                chain.link(act.activation(rstdh[:, 0:16], ssh[:, 0:16], ACT.Ln, scale=1.0 / QK, bias=eps))
                act.activation(rstdh[:, 0:16], rstdh[:, 0:16], ACT.Exp, scale=-0.5).then_inc(rstd_ready, 1)
                for kind, dst in (("gg", silu_g), ("mg", silu_m)):
                    for t in range(NT):
                        pb = await_full(act, (kind, t), l)
                        act.activation(dst[:, t, :], pb[:, :], ACT.Exp, scale=-1.0).then_inc(exp_gate, 1)
                for odd in range(2):
                    pb = await_full(act, ("go", odd), l)
                    for i in range(4):
                        j = 2 * i + odd
                        chain.link(act.activation(junk[:, 0:GDV], pb[:, i * GDV:(i + 1) * GDV], ACT.Square,
                                                  accum_out=ssg[:, j:j + 1]))
                chain.wait()
                chain.link(act.activation(ssg[:, 0:8], ssg[:, 0:8], ACT.Ln, scale=1.0 / GDV, bias=eps))
                act.activation(ssg[:, 0:8], ssg[:, 0:8], ACT.Exp, scale=-0.5).then_inc(rstd_ready, 1)
                for t in range(NT):
                    for kind, dst in (("qnT", qnT), ("knT", knT)):
                        pb = await_full(act, (kind, t), l)
                        free(act.activation(dst[:, :, t * P:(t + 1) * P], quad(pb[:, :]), ACT.Copy), (kind, t))
                for kind, dst in (("qrT",  qrT), ("krT", krT)):
                    pb = await_full(act, (kind,), l)
                    free(act.activation(dst.rearrange("p a b -> p (a b)"), pb[:, :], ACT.Copy), (kind,))
                for h in range(MH):
                    act.wait_ge(m_masked, l * MH + h + 1)
                    if h >= 2:
                        await_full(act, ("mPT", h - 2), l)
                    for qt in range(NT):
                        a, n = (0, P) if qt == 0 else (P, S)
                        i = 2 * (h % 2) + qt
                        act.activation(mE[:, h % 2, a:a + n], mT[:, h % 2, a:a + n], ACT.Exp, scale=-1.0,
                                       bias=accmin[:, i:i + 1], accum_out=rsum[:, qt, h:h + 1]).then_inc(m_exp, 1)
                evac_T("cT2", l)
                chain.end_loop(LAYERS)

        @block.tensor
        def _(pe):
            def transposes(kind, rows_before, l=None, rows=None):
                for t in range(NT):
                    pe.wait_ge(rows_ready, rows_before + t + 1)
                    for g in range(2):
                        pb = claim(pe, (kind, t, g), l)
                        for j in range(4):
                            a = (4 * g + j) * P
                            last = pe.transpose(pb[:, j * P:(j + 1) * P], hrow[:, t, a:a + P], ident)
                        full(last, (kind, t, g))

            def rows_product(job, w, n, t, l=None, k0=0, wcol=0):
                pb = claim(pe, job, l)
                for k in range(KD):
                    last = pe.matmul(pb[:, 0:n], hT[:, k, t * P:(t + 1) * P], w[:, k, wcol:wcol + n], start=k == 0, stop=k == KD - 1)
                full(last, job)

            def columns_product(job, w, j, l=None):
                pb = claim(pe, job, l)
                for i in range(2):
                    a = (2 * j + i) * P
                    for k in range(KD):
                        last = pe.matmul(pb[:, i * S:(i + 1) * S], w[:, k, a:a + P], hT[:, k, :], start=k == 0, stop=k == KD - 1)
                full(last, job)

            pe.wait_ge(const_landed, 16 * (len(kept) + 3))
            pe.wait_ge(rpb_landed, 16 * ROWS * ROWS)
            for i in range(8):
                pb = claim(pe, ("nab", i))
                qt, part = i // 4, i % 4
                src = na_raw[:, qt, 2 * part:2 * part + 2, :].rearrange("p a b -> p (a b)")
                full(pe.matmul(pb[:, :], flip, src, start=True, stop=True), ("nab", i))

            def ada(n):
                w = weights1(pe, ("ada", n))
                pb = claim(pe, ("ada", n))
                for k in range(KD):
                    last = pe.matmul(pb[:, :], silu_cb[:, k, :], w[:, k, :], start=k == 0, stop=k == KD - 1)
                full(last, ("ada", n))

            pe.wait_ge(cb_ready, 1)
            for n in range(4):
                ada(n)
            transposes("xT", 0)
            drained(pe, ("xT", 0, 1))
            drained(pe, ("xT", 1, 0))
            drained(pe, ("xT", 1, 1))
            drained(pe, ("xT", 0, 0))
            for ch in (0, 1, 3, 4):
                w = weights1(pe, ("qk", ch, 1))
                for j in range(2):
                    columns_product(("qk", ch, j), w, j)
            for ch in (2, 5):
                w = weights1(pe, ("v", ch, 1))
                for t in range(NT):
                    rows_product(("v", ch, t), w, 512, t)

            def scores_of(h):
                if h == 0:
                    for ch in (0, 1, 3, 4):
                        for j in range(2):
                            drained(pe, ("qk", ch, j))
                qi, ki_ = (h // 2, 4 + h // 2) if h < 8 else (8 + (h - 8) // 2, 12 + (h - 8) // 2)
                p0 = HD * (h % 2)
                pb = claim(pe, ("S", h))
                for qt in range(NT):
                    last = pe.matmul(pb[:, qt * S:(qt + 1) * S], qkT[p0:p0 + HD, qi, qt * P:(qt + 1) * P],
                                     qkT[p0:p0 + HD, ki_, :], start=True, stop=True)
                full(last, ("S", h))

            def transpose_probs(h):
                pe.wait_ge(exp_ready, 2 * h + 2)
                pb = claim(pe, ("PT", h))
                for qt in range(NT):
                    for kt in range(NT):
                        a = (2 * qt + kt) * P
                        last = pe.transpose(pb[:, a:a + P], Em[:, h % 2, qt, kt * P:(kt + 1) * P], ident)
                full(last, ("PT", h))

            def times_v(h):
                if h == 0:
                    for ch in (2, 5):
                        for t in range(NT):
                            drained(pe, ("v", ch, t))
                drained(pe, ("PT", h))
                g, i = h // 8, h % 8
                for qt in range(NT):
                    pb = claim(pe, ("O", g, qt)) if i == 0 else bank[6 + qt]
                    for kt in range(NT):
                        a = (2 * qt + kt) * P
                        last = pe.matmul(pb[:, i * HD:(i + 1) * HD], pT[:, h % 2, a:a + P], vrow[:, kt, h * HD:(h + 1) * HD],
                                         start=kt == 0, stop=kt == NT - 1)
                    if i == 7:
                        full(last, ("O", g, qt))
                if i < 7:
                    last.then_inc(pv_done, 1)

            for kind, i in attention_schedule():
                if kind == "S":
                    scores_of(i)
                elif kind == "ada":
                    ada(i)
                elif kind == "PT":
                    transpose_probs(i)
                elif kind == "PV":
                    times_v(i)

            transposes("oT", NT + 1)
            for t in range(NT):
                for g in range(2):
                    drained(pe, ("oT", t, g))
            for ch in range(2):
                w = weights1(pe, ("y", ch, 1))
                for t in range(NT):
                    rows_product(("y", ch, t), w, 512, t)

            transposes("hT", 2 * NT + 1)
            pe.wait_ge(sk_landed, 16)
            pb = claim(pe, ("skT",))
            for s in range(2):
                last = pe.transpose(pb[:, s * P:(s + 1) * P], skrow[:, s, :], ident)
            full(last, ("skT",))
            for t in range(NT):
                for g in range(2):
                    drained(pe, ("hT", t, g))
            for ch in range(4):
                w = weights1(pe, ("pq", ch, 1))
                for j in range(2):
                    columns_product(("pq", ch, j), w, j)
            drained(pe, ("skT",))
            for t in range(NT):
                for g in range(4):
                    drained(pe, ("pq", g, 0))
                    drained(pe, ("pq", g, 1))
                    pb = claim(pe, ("sc", t, g))
                    for j in range(4):
                        i = 4 * g + j
                        last = pe.matmul(pb[:, j * P:(j + 1) * P], pqT[:, i, t * P:(t + 1) * P], skT[:, i % 2, :],
                                         start=True, stop=True)
                    full(last, ("sc", t, g))

            def peer_group(n, b, t):
                pb = [bank[banks.jobs[("peer", t, half)][0]] for half in range(2)]
                for s in range(GROUP):
                    pe.wait_ge(v_landed[s], 16 * (n + 1) if isinstance(n, int) else n * 16 + 16)
                    pe.wait_ge(diag_ready, n * GROUP + s + 1)
                    for half in range(2):
                        last = pe.matmul(pb[half][:, :], diag[:, b * GROUP + s, :], vgat[:, s, half * 512:(half + 1) * 512],
                                         start=False, stop=False, skip_group_check=True)
                    last.then_inc(v_free, 1)

            pe.wait_ge(ids_ready, NT)
            for t in range(NT):
                for half in range(2):
                    pb = claim(pe, ("peer", t, half))
                    pe.matmul(pb[:, :], zeros, hrow[:, t, half * 512:(half + 1) * 512], start=True, stop=False,
                              skip_group_check=True)
                with pe.Fori(t * NG // 4, (t + 1) * NG // 4) as m:
                    for b in range(2):
                        peer_group(m * 2 + b, b, t)
                for half in range(2):
                    pb = bank[banks.jobs[("peer", t, half)][0]]
                    full(pe.matmul(pb[:, :], zeros, hrow[:, t, half * 512:(half + 1) * 512], start=False, stop=True,
                                   skip_group_check=True), ("peer", t, half))

            with pe.Fori(0, LAYERS) as l:
                for t in range(NT):
                    pe.wait_ge(rows_ready, l * (2 * NT) + (3 * NT + 1) + t + 1)
                    for g in range(2):
                        pb = claim(pe, ("zT", t, g), l)
                        for j in range(4):
                            a = (4 * g + j) * P
                            last = pe.transpose(pb[:, j * P:(j + 1) * P], hrow[:, t, a:a + P], ident)
                        full(last, ("zT", t, g))
                for t in range(NT):
                    for g in range(2):
                        drained(pe, ("zT", t, g), l)
                w = landed2(pe, 0, l).rearrange("p (k m) -> p k m", k=KD)
                for j in range(2):
                    columns_product(("gqk", j), w, j, l)
                w = landed2(pe, 1, l).rearrange("p (k m) -> p k m", k=KD)
                pb = claim(pe, ("lr",), l)
                for k in range(KD):
                    last = pe.matmul(pb[0:LR, 0:S], w[:, k, 0:LR], hT[:, k, :], start=k == 0, stop=k == KD - 1)
                full(last, ("lr",))
                for t in range(NT):
                    rows_product(("c", t), w, CW, t, l, wcol=LR)
                drained(pe, ("lr",), l)
                pe.wait_ge(gains2_landed, l * 128 + 128)
                pb = claim(pe, ("gl",), l)
                for a in range(2):
                    last = pe.matmul(pb[:, a * S:(a + 1) * S], up[0:LR, a * P:(a + 1) * P], lrT[0:LR, :], start=True, stop=True)
                full(last, ("gl",))
                w = landed2(pe, 2, l).rearrange("p (k m) -> p k m", k=KD)
                for t in range(NT):
                    rows_product(("gv", t), w, 512, t, l)
                for t in range(NT):
                    pe.wait_ge(dve_to_pe, l * 8 + 1 + t)
                    pb = claim(pe, ("cT", t), l)
                    for j in range(3):
                        last = pe.transpose(pb[:, j * P:(j + 1) * P], crow[:, t, j * P:(j + 1) * P], ident)
                    full(last, ("cT", t))
                pe.wait_ge(dve_to_pe, l * 8 + 3)
                pb = claim(pe, ("keT",), l)
                for t in range(NT):
                    for a in range(2):
                        i = 2 * t + a
                        last = pe.transpose(pb[:, i * P:(i + 1) * P], ke[:, a, t * P:(t + 1) * P], ident)
                full(last, ("keT",))
                w = landed2(pe, 3, l)
                wq_, wkv = w[:, 0:1536].rearrange("p (k m) -> p k m", k=2), w[:, 1536:2560]
                for t in range(NT):
                    drained(pe, ("cT", t), l)
                    for hp in range(2):
                        pb = claim(pe, ("uq", t, hp), l)
                        for k in range(2):
                            last = pe.matmul(pb[:, 0:2 * QK], cqT[:, k, t * P:(t + 1) * P], wq_[:, k, hp * 2 * QK:(hp + 1) * 2 * QK],
                                             start=k == 0, stop=k == 1)
                        full(last, ("uq", t, hp))
                        pb = claim(pe, ("ukv", t, hp), l)
                        full(pe.matmul(pb[:, :], cqT[:, 2, t * P:(t + 1) * P], wkv[:, hp * 512:(hp + 1) * 512],
                                       start=True, stop=True), ("ukv", t, hp))
                for odd in range(2):
                    pb = claim(pe, ("A", odd), l)
                    p0 = GDK * odd
                    for t in range(NT):
                        for a in range(2):
                            i = 2 * t + a
                            last = pe.matmul(pb[:, i * P:(i + 1) * P], ki[p0:p0 + GDK, a, t * P:(t + 1) * P],
                                             gqT[p0:p0 + GDK, a, t * P:(t + 1) * P], start=True, stop=True)
                    full(last, ("A", odd))
                drained(pe, ("keT",), l)
                for t in range(NT):
                    drained(pe, ("gv", t), l)
                for i in range(3):
                    pb = claim(pe, ("U", i), l)
                    wait_alone(pe)
                    q0, t = GCH * (i % 2), i // 2
                    for h in range(GH):
                        p0, a = GDK * (h % 2), h // 2
                        last = pe.matmul(pb[p0:p0 + GDK, a * GDV:(a + 1) * GDV], keR[q0:q0 + GCH, t, a, p0:p0 + GDK],
                                         gv[q0:q0 + GCH, t, h * GDV:(h + 1) * GDV], start=True, stop=True)
                    full(last, ("U", i))
                for n, kind in ((4, "gg"), (5, "mg")):
                    w = landed2(pe, n, l).rearrange("p (k m) -> p k m", k=KD)
                    for t in range(NT):
                        rows_product((kind, t), w, 512, t, l)
                pe.wait_ge(dve_to_pe, l * 8 + 6)
                for odd in range(2):
                    pb = claim(pe, ("go", odd), l)
                    p0 = GDK * odd
                    for t in range(NT):
                        for a in range(2):
                            h, i = 2 * a + odd, 2 * t + a
                            last = pe.matmul(pb[:, i * GDV:(i + 1) * GDV], aT[:, t, h, :], gv[:, t, h * GDV:(h + 1) * GDV],
                                             start=True, stop=False, skip_group_check=True)
                            for cc in range(2):
                                c_ = 2 * t + cc
                                if c_ > 0:
                                    last = pe.matmul(pb[cc * GCH:(cc + 1) * GCH, i * GDV:(i + 1) * GDV],
                                                     gqT[p0:p0 + GDK, a, c_ * GCH:(c_ + 1) * GCH],
                                                     state[p0:p0 + GDK, c_ - 1, a, :],
                                                     start=False, stop=True, skip_group_check=True)
                    full(last, ("go", odd))
                for t in range(NT):
                    pe.wait_ge(dve_to_pe, l * 8 + 7 + t)
                    for kind, src in (("qnT", qrow), ("knT", kvrow)):
                        pb = claim(pe, (kind, t), l)
                        for h in range(MH):
                            last = pe.transpose(pb[:, h * P:(h + 1) * P], src[:, t, h, 0:NOPE], ident)
                        full(last, (kind, t))
                for kind, src in (("qrT", qrr), ("krT", krr)):
                    pb = claim(pe, (kind,), l)
                    for a in range(2):
                        for t in range(NT):
                            i = (2 * a + t) * P
                            last = pe.transpose(pb[:, i:i + P], src[:, t, 2 * a:2 * a + 2, :].rearrange("p a b -> p (a b)"), ident)
                    full(last, (kind,))
                for kind, i in mla_schedule():
                    if kind == "ms":
                        if i == 0:
                            for t in range(NT):
                                drained(pe, ("qnT", t), l)
                                drained(pe, ("knT", t), l)
                            drained(pe, ("qrT",), l)
                            drained(pe, ("krT",), l)
                        p0, a = ROPE * (i % 2), i // 2
                        pb = claim(pe, ("ms", i), l)
                        for qt in range(NT):
                            o, n = (0, P) if qt == 0 else (P, S)
                            pe.matmul(pb[:, o:o + n], qnT[:, i, qt * P:(qt + 1) * P], knT[:, i, 0:n], start=True, stop=False)
                            last = pe.matmul(pb[:, o:o + n], qrT[p0:p0 + ROPE, a, qt * P:(qt + 1) * P],
                                             krT[p0:p0 + ROPE, a, 0:n], start=False, stop=True)
                        full(last, ("ms", i))
                    elif kind == "mPT":
                        pe.wait_ge(m_exp, l * (2 * MH) + 2 * i + 2)
                        pb = claim(pe, ("mPT", i), l)
                        for j in range(3):
                            last = pe.transpose(pb[:, j * P:(j + 1) * P], mE[:, i % 2, j * P:(j + 1) * P], ident)
                        full(last, ("mPT", i))
                    else:
                        drained(pe, ("mPT", i), l)
                        for qt in range(NT):
                            pb = claim(pe, ("mo", qt), l) if i == 0 else bank[6 + qt]
                            for kt in range(qt + 1):
                                j = qt + kt
                                last = pe.matmul(pb[:, i * MDV:(i + 1) * MDV], mPT[:, i % 2, j * P:(j + 1) * P],
                                                 kvrow[:, kt, i, NOPE:NOPE + MDV], start=kt == 0, stop=kt == qt)
                            if i == MH - 1:
                                full(last, ("mo", qt))
                        if i < MH - 1:
                            last.then_inc(m_pv, 1)
                for t in range(NT):
                    pe.wait_ge(rows_ready, l * (2 * NT) + (3 * NT + 1) + NT + t + 1)
                    for g in range(2):
                        pb = claim(pe, ("cT2", t, g), l)
                        for j in range(4):
                            a = (4 * g + j) * P
                            last = pe.transpose(pb[:, j * P:(j + 1) * P], hrow[:, t, a:a + P], ident)
                        full(last, ("cT2", t, g))
                for t in range(NT):
                    for g in range(2):
                        drained(pe, ("cT2", t, g), l)
                for ch in range(2):
                    w = landed2(pe, 6 + ch, l).rearrange("p (k m) -> p k m", k=KD)
                    for t in range(NT):
                        rows_product(("y2", ch, t), w, 512, t, l)

        @block.vector
        def _(dve):
            chain = Chain(dve, dve_step)

            def bc(ap, *shape):
                return ap.to_broadcast([P, *shape])

            chain.step(dve.memset(eps, EPS))
            chain.wait()
            dve.memset(half_pi, 0.0).then_inc(consts_set, 1)
            dve.wait_ge(silu_ready, 1)
            dve.tensor_copy(silu_cb[:, :, :], bc(csil.unsqueeze(2), KD, P)).then_inc(cb_ready, 1)

            dve.wait_ge(const_landed, 16 * (len(kept) + 3))
            chain.link(dve.tensor_copy(posf, posi))
            MAGIC, C1 = 1.5 * 2.0 ** 23, 6.28125
            C2 = float(np.float32(round((2 * np.pi - C1) * 2.0 ** 20) / 2.0 ** 20))
            C3 = 2 * np.pi - C1 - C2
            ang = Tm[:, 0, 0, 0:64].rearrange("p (t f) -> p t f", t=NT)
            turns = Tm[:, 0, 1, 0:128].rearrange("p (t s f) -> p t s f", t=NT, s=2)
            for t in range(NT):
                chain.step(dve.tensor_scalar(ang[:, t, :], inv_freq, posf[:, t:t + 1], None, ALU.mult))
            chain.wait()
            for s in range(2):
                chain.step(dve.tensor_scalar(turns[:, :, s, :], ang, 1 / (2 * np.pi), 0.25 * (1 - s), ALU.mult, ALU.add))
            chain.wait()
            tf = turns.rearrange("p t s f -> p (t s f)")
            chain.link(dve.tensor_scalar(tf, tf, MAGIC, None, ALU.add))
            chain.link(dve.tensor_scalar(tf, tf, MAGIC, None, ALU.subtract))
            for s in range(2):
                chain.step(dve.scalar_tensor_tensor(rope[:, :, s, :], turns[:, :, s, :], -C1, ang, ALU.mult, ALU.add))
            rf = rope[:, :, :, :].rearrange("p t s f -> p (t s f)")
            chain.wait()
            chain.link(dve.scalar_tensor_tensor(rf, tf, -C2, rf, ALU.mult, ALU.add))
            chain.link(dve.scalar_tensor_tensor(rf, tf, -C3, rf, ALU.mult, ALU.add))
            chain.link(dve.tensor_scalar(rope[:, :, 0, :], rope[:, :, 0, :], np.pi / 2, None, ALU.add))
            PI = float(np.nextafter(np.float32(np.pi), np.float32(0)))
            dve.tensor_scalar(rf, rf, PI, -PI, ALU.min, ALU.max).then_inc(ang_ready, 1)

            for i in range(8):
                qt, part = i // 4, i % 4
                pb = await_full(dve, ("nab", i))
                free(dve.tensor_tensor(bias[:, 2 * part:2 * part + 2, qt, :], bc(na_window[:, qt, :].unsqueeze(1), 2, S),
                                       pb[:, :].rearrange("p (a b) -> p a b", a=2), ALU.subtract), ("nab", i))

            def ada(n):
                pb = await_full(dve, ("ada", n))
                m = modb[:, n // 2, (n % 2) * 512:(n % 2 + 1) * 512]
                free(dve.tensor_tensor(m, pb[:, :], m, ALU.add), ("ada", n))

            dve.wait_ge(adab_landed, 16)
            for n in range(4):
                ada(n)
            for n in range(4):
                drained(dve, ("ada", n))

            def fold_gain(s, g):
                chain.link(dve.scalar_tensor_tensor(modb[:, s, :], modb[:, s, :], 1.0, gains[:, g, :], ALU.add, ALU.mult))

            def modulated(t, gain, shift):
                chain.link(dve.scalar_tensor_tensor(hrow[:, t, :], xrow[:, t, :], rstd[:, t:t + 1], modb[:, gain, :], ALU.mult, ALU.mult))
                dve.tensor_tensor(hrow[:, t, :], hrow[:, t, :], modb[:, shift, :], ALU.add).then_inc(rows_ready, 1)

            dve.wait_ge(gains_landed, 64)
            fold_gain(1, 0)
            dve.wait_ge(rstd_ready, 1)
            for t in range(NT):
                modulated(t, 1, 0)

            dve.wait_ge(dil_landed, 16)
            for i in range(8):
                drained(dve, ("nab", i))

            def normalize(g):
                dve.wait_ge(exp_ready, 2 * (8 * g + 8))
                chain.link(dve.reciprocal(rinv, rsum[:, :, 8 * g:8 * g + 8]))
                for qt in range(NT):
                    pb = await_full(dve, ("O", g, qt))
                    free(dve.tensor_tensor(hrow[:, qt, g * 512:(g + 1) * 512].rearrange("p (h d) -> p h d", h=8),
                                           pb[:, :].rearrange("p (h d) -> p h d", h=8),
                                           bc(rinv[:, qt, :].unsqueeze(2), 8, HD), ALU.mult), ("O", g, qt))

            for kind, h in attention_schedule():
                if kind == "S":
                    if h >= 2:
                        dve.wait_ge(exp_ready, 2 * (h - 2) + 2)
                    pb = await_full(dve, ("S", h))
                    for qt in range(NT):
                        i = 2 * (h % 2) + qt
                        ins = dve.tensor_tensor_reduce(Tm[:, h % 2, qt, :], pb[:, qt * S:(qt + 1) * S], bias[:, h, qt, :], 1.0, 3e38,
                                                       ALU.add, ALU.min, accmin[:, i:i + 1])
                        if qt == 0:
                            chain.step(ins)
                        else:
                            free(ins, ("S", h))
                    drained(dve, ("S", h))
                    chain.wait()
                    dve.sem_inc(masked_ready, 1)
                elif kind == "ada":
                    ada(h)
                elif kind == "PT":
                    if h >= 2:
                        if (h - 2) % 8 == 7:
                            await_full(dve, ("O", (h - 2) // 8, 1))
                        else:
                            dve.wait_ge(pv_done, (h - 2) - (h - 2) // 8 + 1)
                    pb = await_full(dve, ("PT", h))
                    free(dve.tensor_copy(pT[:, h % 2, :], pb[:, :]), ("PT", h))
                elif kind == "O":
                    normalize(h)
            for g in range(2):
                for qt in range(NT):
                    drained(dve, ("O", g, qt))
            dve.sem_inc(rows_ready, 1)
            for n in range(4, 12):
                drained(dve, ("ada", n))
            fold_gain(4, 1)
            dve.wait_ge(rstd_ready, 2)
            for t in range(NT):
                chain.step(dve.scalar_tensor_tensor(hrow[:, t, 0:512], hrow[:, t, 0:512], rstd[:, 2 * t:2 * t + 1], gains[:, 2, 0:512],
                                                    ALU.mult, ALU.mult))
                chain.wait()
                dve.scalar_tensor_tensor(hrow[:, t, 512:1024], hrow[:, t, 512:1024], rstd[:, 2 * t + 1:2 * t + 2],
                                         gains[:, 2, 512:1024], ALU.mult, ALU.mult).then_inc(rows_ready, 1)

            def add_gated(job, gate, ch, t, i, ready=None):
                pb = await_full(dve, job)
                a = slice(ch * 512, (ch + 1) * 512)
                free(dve.tensor_tensor(ytmp[:, i, :], pb[:, :], modb[:, gate, a], ALU.mult), job)
                drained(dve, job)
                ins = dve.tensor_tensor(xrow[:, t, a], xrow[:, t, a], ytmp[:, i, :], ALU.add)
                if ready is None:
                    chain.link(ins)
                else:
                    ins.then_inc(ready, 1)

            for ch in range(2):
                for t in range(NT):
                    add_gated(("y", ch, t), 2, ch, t, t, x_ready if ch == 1 else None)
            for t in range(NT):
                dve.wait_ge(x_ready, t + 1)
                dve.wait_ge(rstd_ready, 3 + t)
                modulated(t, 4, 3)

            pb = await_full(dve, ("skT",))
            free(dve.tensor_copy(skT[:, :, :].rearrange("p a b -> p (a b)"), pb[:, 0:2 * P]), ("skT",))

            def top16(units):
                for src, v, i in units:
                    chain.step(dve.max(v[:, 0:8], src))
                chain.wait()
                for src, v, i in units:
                    chain.step(dve.max_index(i[:, 0:8], v[:, 0:8], src))
                chain.wait()
                for src, v, i in units:
                    chain.step(dve.match_replace(src, v[:, 0:8], src, -3.0e38))
                chain.wait()
                for src, v, i in units:
                    chain.step(dve.max(v[:, 8:16], src))
                chain.wait()
                for src, v, i in units:
                    chain.step(dve.max_index(i[:, 8:16], v[:, 8:16], src))

            for t in range(NT):
                for g in range(4):
                    drained(dve, ("sc", t, g))
                    top16([(scores[:, t, 4 * g + j, :], top_v[:, t, (4 * g + j) // 2, j % 2, :], top_i[:, t, (4 * g + j) // 2, j % 2, :])
                           for j in range(4)])
                chain.wait()
                chain.link(dve.tensor_tensor(cand.rearrange("p h (a b) -> p h a b", a=TOPK),
                                             bc(top_v[:, t, :, 0, :].unsqueeze(3), PH, TOPK, TOPK),
                                             bc(top_v[:, t, :, 1, :].unsqueeze(2), PH, TOPK, TOPK), ALU.add))
                for q in range(2):
                    top16([(cand[:, h, :], best_v[:, t, h, :], best_j[:, h, :]) for h in range(4 * q, 4 * q + 4)])
                chain.wait()
                bj = best_j.rearrange("p h k -> p (h k)")
                chain.step(dve.tensor_scalar(best_ab[:, 0, :, :].rearrange("p h k -> p (h k)"), bj, 4, None, ALU.logical_shift_right))
                chain.step(dve.tensor_scalar(best_ab[:, 1, :, :].rearrange("p h k -> p (h k)"), bj, 15, None, ALU.bitwise_and))
                chain.step(dve.tensor_tensor(gates[:, t * SLOTS:(t + 1) * SLOTS].rearrange("p (h k) -> p h k", h=PH),
                                             best_v[:, t, :, :], bc(best_v[:, t, :, 0:1], PH, TOPK), ALU.subtract))
                chain.wait()
                dve.sem_inc(softmax_shift, 1)
                for s in range(2):
                    chain.link(dve.tensor_tensor(hit, bc(best_ab[:, s, :, :].unsqueeze(3), PH, TOPK, TOPK),
                                                 iota.unsqueeze(1).unsqueeze(1).to_broadcast([P, PH, TOPK, TOPK]), ALU.is_equal))
                    chain.link(dve.tensor_tensor(hit, hit, bc(top_i[:, t, :, s, :].unsqueeze(2), PH, TOPK, TOPK), ALU.mult))
                    chain.link(dve.tensor_reduce(picked[:, s, :, :].rearrange("p h k -> p (h k)"),
                                                 hit.rearrange("p h k a -> p (h k) a"), AX.X, ALU.add))
                chain.step(dve.scalar_tensor_tensor(ids[:, t * SLOTS:(t + 1) * SLOTS], picked[:, 0, :, :].rearrange("p h k -> p (h k)"),
                                                    float(NKEY), picked[:, 1, :, :].rearrange("p h k -> p (h k)"), ALU.mult, ALU.add))
                dve.wait_ge(gate_exp, t + 1)
                gv3 = gates[:, t * SLOTS:(t + 1) * SLOTS].rearrange("p (h k) -> p h k", h=PH)
                chain.link(dve.tensor_reduce(gsum[:, 0:PH], gv3, AX.X, ALU.add))
                chain.link(dve.reciprocal(gsum[:, 8:8 + PH], gsum[:, 0:PH]))
                chain.link(dve.tensor_tensor(gv3, gv3, bc(gsum[:, 8:8 + PH].unsqueeze(2), PH, TOPK), ALU.mult))
                if t == 0:
                    chain.link(dve.memset(zeros, 0.0))
                dve.sem_inc(ids_ready, 1)

            def peer_group(n, b, t):
                for s in range(GROUP):
                    dve.wait_ge(u_landed[s], n * 16 + 16)
                    dve.tensor_tensor_reduce(urow[:, s, :], urow[:, s, :], hrow[:, t, :], 1.0, 0.0, ALU.mult, ALU.add,
                                             a8[:, b, s:s + 1]).then_inc(u_free, 1)
                dve.wait_ge(gelu_ready, n + 1)
                dve.tensor_tensor(w8[:, b, :], g8[:, b, :], gates[:, bass.ds(n * GROUP, GROUP)], ALU.mult).then_inc(weights_ready, 1)

            dve.wait_ge(rows_ready, 3 * NT + 1)
            for t in range(NT):
                with dve.Fori(t * NG // 4, (t + 1) * NG // 4) as m:
                    for b in range(2):
                        peer_group(m * 2 + b, b, t)
            for t in range(NT):
                for half in range(2):
                    add_gated(("peer", t, half), 5, half, t, half, x_ready if half == 1 else None)
            dve.wait_ge(fing_landed, 16)
            for t in range(NT):
                dve.wait_ge(x_ready, NT + t + 1)
                dve.wait_ge(rstd_ready, 5 + t)
                dve.scalar_tensor_tensor(xrow[:, t, :], xrow[:, t, :], rstd[:, t:t + 1], gains[:, 0, :],
                                         ALU.mult, ALU.mult).then_inc(x_ready, 1)

            chain.link(dve.memset(aT.rearrange("p a b c -> p (a b c)"), 0.0))
            XR = 2 * NT
            with dve.Fori(0, LAYERS) as l:
                chain.loop(l, 66)
                dve.wait_ge(gains2_landed, l * 128 + 128)
                dve.wait_ge(rstd_ready, l * 4 + 7)
                for t in range(NT):
                    dve.scalar_tensor_tensor(hrow[:, t, :], xrow[:, t, :], rstd[:, 4 + t:5 + t], g_in, ALU.mult, ALU.mult)\
                        .then_inc(rows_ready, 1)
                for t in range(NT):
                    drained(dve, ("c", t), l)
                dve.wait_ge(rstd_ready, l * 4 + 8)
                for t in range(NT):
                    chain.step(dve.scalar_tensor_tensor(crow[:, t, QR:QR + KVR], crow[:, t, QR:QR + KVR], rstd[:, 8 + t:9 + t], g_kv,
                                                        ALU.mult, ALU.mult))
                    chain.wait()
                    dve.scalar_tensor_tensor(crow[:, t, 0:QR], crow[:, t, 0:QR], rstd[:, 6 + t:7 + t], g_q,
                                             ALU.mult, ALU.mult).then_inc(dve_to_pe, 1)
                pb = await_full(dve, ("gl",), l)
                dve.wait_ge(exp_gate, l * 8 + 1)
                for a in range(2):
                    chain.step(dve.tensor_scalar(log_a[:, a, :], pb[:, a * S:(a + 1) * S], bgate[:, a:a + 1], 0.0, ALU.add, ALU.min))
                chain.wait()
                la = log_a.rearrange("p a b -> p (a b)")
                free(dve.tensor_tensor(la, la, gtmp.rearrange("p a b -> p (a b)"), ALU.subtract), ("gl",))
                drained(dve, ("gl",), l)
                for a in range(2):
                    chain.step(dve.tensor_tensor_scan(bcum[:, a, :], segment, log_a[:, a, :], 0.0, ALU.mult, ALU.add))
                chain.wait()
                dve.sem_inc(dve_to_act, 1)
                b4 = bcum.rearrange("p a (c i) -> p a c i", i=GCH)
                for a in range(2):
                    ins = dve.tensor_tensor(ke[:, a, :].rearrange("p (c i) -> p c i", i=GCH),
                                            bc(b4[:, a, :, GCH - 1:GCH], S // GCH, GCH), b4[:, a, :, :], ALU.subtract)
                    chain.step(ins)
                chain.wait()
                dve.sem_inc(dve_to_act, 1)
                dve.wait_ge(exp_gate, l * 8 + 3)
                for j in range(2):
                    drained(dve, ("gqk", j), l)
                chain.step(dve.tensor_tensor(gqT, gqT, eb, ALU.mult))
                chain.step(dve.tensor_tensor(ki, ki, gkT, ALU.mult))
                dve.wait_ge(exp_gate, l * 8 + 4)
                chain.step(dve.tensor_tensor(ke, ke, gkT, ALU.mult))
                chain.wait()
                dve.sem_inc(dve_to_pe, 1)
                pb = await_full(dve, ("keT",), l)
                free(dve.tensor_copy(keR.rearrange("p t a b -> p (t a b)"), pb[:, :]), ("keT",))
                for odd in range(2):
                    pb = await_full(dve, ("A", odd), l)
                    wait_alone(dve)
                    free(dve.copy_predicated(aT.rearrange("p t (a o) m -> p t a o m", o=2)[:, :, :, odd, :],
                                             same_chunk.unsqueeze(1).unsqueeze(1).to_broadcast([P, NT, 2, P]),
                                             pb[:, :].rearrange("p (t a m) -> p t a m", t=NT, a=2)), ("A", odd))
                    drained(dve, ("A", odd), l)
                    dve.sem_inc(dve_to_pe, 1)
                e4 = eb.rearrange("p a (c i) -> p a c i", i=GCH)
                pb = await_full(dve, ("U", 0), l)
                free(dve.tensor_copy(state[:, 0, :, :].rearrange("p a b -> p (a b)"), pb[:, 0:2 * GDV]), ("U", 0))
                drained(dve, ("U", 0), l)
                for i in (1, 2):
                    pb = await_full(dve, ("U", i), l)
                    for a in range(2):
                        ins = dve.scalar_tensor_tensor(state[:, i, a, :], state[:, i - 1, a, :], e4[:, a, i, GCH - 1:GCH],
                                                       pb[:, a * GDV:(a + 1) * GDV], ALU.mult, ALU.add)
                        if a == 0:
                            chain.step(ins)
                        else:
                            free(ins, ("U", i))
                    drained(dve, ("U", i), l)
                    chain.wait()
                dve.sem_inc(dve_to_pe, 1)

                dve.wait_ge(rope_ready, 1)
                dve.wait_ge(rstd_ready, l * 4 + 9)
                w4 = wide.rearrange("p (h d) -> p h d", h=MH)
                HR = ROPE // 2
                for t in range(NT):
                    for hp in range(2):
                        drained(dve, ("uq", t, hp), l)
                        drained(dve, ("ukv", t, hp), l)
                    cos, sin = rope[:, t, 0, :], rope[:, t, 1, :]
                    rq, rk = rstdh[:, 4 * t:4 * t + 4], rstdh[:, 8 + 4 * t:12 + 4 * t]
                    chain.step(dve.tensor_tensor(qrow[:, t, :, :], qrow[:, t, :, :], bc(rq.unsqueeze(2), MH, QK), ALU.mult))
                    chain.step(dve.tensor_tensor(kvrow[:, t, :, 0:NOPE], kvrow[:, t, :, 0:NOPE], bc(rk.unsqueeze(2), MH, NOPE), ALU.mult))
                    chain.step(dve.tensor_tensor(kpe[:, t, :], crow[:, t, QR + KVR:CW], g_kh[:, NOPE:QK], ALU.mult))
                    chain.wait()
                    chain.step(dve.tensor_tensor(qrow[:, t, :, :], qrow[:, t, :, :], bc(g_qh.unsqueeze(1), MH, QK), ALU.mult))
                    chain.step(dve.tensor_tensor(kvrow[:, t, :, 0:NOPE], kvrow[:, t, :, 0:NOPE], bc(g_kh[:, 0:NOPE].unsqueeze(1), MH, NOPE), ALU.mult))
                    k1, k2 = kpe[:, t, 0:HR], kpe[:, t, HR:ROPE]
                    kp = wide[:, 512:640]
                    chain.step(dve.tensor_tensor(kp[:, 0:32], k1, cos, ALU.mult))
                    chain.step(dve.tensor_tensor(kp[:, 32:64], k2, sin, ALU.mult))
                    chain.step(dve.tensor_tensor(kp[:, 64:96], k1, sin, ALU.mult))
                    chain.step(dve.tensor_tensor(kp[:, 96:128], k2, cos, ALU.mult))
                    chain.wait()
                    q1, q2 = qrow[:, t, :, NOPE:NOPE + HR], qrow[:, t, :, NOPE + HR:QK]
                    cb, sb_ = bc(cos.unsqueeze(1), MH, HR), bc(sin.unsqueeze(1), MH, HR)
                    qp = wide[:, 0:512].rearrange("p (i h f) -> p i h f", i=4, h=MH)
                    chain.step(dve.tensor_tensor(qp[:, 0, :, :], q1, cb, ALU.mult))
                    chain.step(dve.tensor_tensor(qp[:, 1, :, :], q2, sb_, ALU.mult))
                    chain.step(dve.tensor_tensor(qp[:, 2, :, :], q1, sb_, ALU.mult))
                    chain.step(dve.tensor_tensor(qp[:, 3, :, :], q2, cb, ALU.mult))
                    chain.step(dve.tensor_tensor(kpr[:, t, 0:HR], kp[:, 0:32], kp[:, 32:64], ALU.subtract))
                    chain.step(dve.tensor_tensor(kpr[:, t, HR:ROPE], kp[:, 64:96], kp[:, 96:128], ALU.add))
                    chain.wait()
                    chain.step(dve.tensor_tensor(qrr[:, t, :, 0:HR], qp[:, 0, :, :], qp[:, 1, :, :], ALU.subtract))
                    chain.step(dve.tensor_tensor(qrr[:, t, :, HR:ROPE], qp[:, 2, :, :], qp[:, 3, :, :], ALU.add))
                    chain.step(dve.tensor_tensor(krr[:, t, :, :], bc(kpr[:, t, :].unsqueeze(1), MH, ROPE), bc(rk.unsqueeze(2), MH, ROPE), ALU.mult))
                    chain.wait()
                    dve.sem_inc(dve_to_pe, 1)

                for kind, dst, before in (("gg", silu_g, 4), ("mg", silu_m, 6)):
                    for t in range(NT):
                        dve.wait_ge(exp_gate, l * 8 + before + t + 1)
                        chain.link(dve.tensor_scalar(dst[:, t, :], dst[:, t, :], 1.0, None, ALU.add))
                        chain.link(dve.reciprocal(dst[:, t, :], dst[:, t, :]))
                        pb = await_full(dve, (kind, t), l)
                        free(dve.tensor_tensor(dst[:, t, :], dst[:, t, :], pb[:, :], ALU.mult), (kind, t))
                dve.wait_ge(rstd_ready, l * 4 + 10)
                for odd in range(2):
                    pb = await_full(dve, ("go", odd), l)
                    o = hrow[:, :, 0:512].rearrange("p t (a o d) -> p t a o d", a=2, o=2)[:, :, :, odd, :]
                    r4 = ssg.rearrange("p (t a o) -> p t a o", t=NT, a=2)[:, :, :, odd].unsqueeze(3)
                    free(dve.tensor_tensor(o, pb[:, :].rearrange("p (t a d) -> p t a d", t=NT, a=2),
                                           r4.to_broadcast([P, NT, 2, GDV]), ALU.mult), ("go", odd))
                    drained(dve, ("go", odd), l)
                for t in range(NT):
                    o = hrow[:, t, 0:512].rearrange("p (h d) -> p h d", h=GH)
                    chain.link(dve.tensor_tensor(o, o, bc(g_gla.unsqueeze(1), GH, GDV), ALU.mult))
                    drained(dve, ("gg", t), l)
                    chain.step(dve.tensor_tensor(hrow[:, t, 0:512], hrow[:, t, 0:512], silu_g[:, t, :], ALU.mult))
                chain.wait()
                dve.sem_inc(gains2_used, 1)

                for kind, h in mla_schedule():
                    if kind == "ms":
                        if h >= 2:
                            dve.wait_ge(m_exp, l * (2 * MH) + 2 * (h - 2) + 2)
                        pb = await_full(dve, ("ms", h), l)
                        wait_alone(dve)
                        for qt in range(NT):
                            a, n = (0, P) if qt == 0 else (P, S)
                            i = 2 * (h % 2) + qt
                            ins = dve.tensor_tensor_reduce(mT[:, h % 2, a:a + n], pb[:, a:a + n], causal[:, a:a + n], -QK ** -0.5, 3e38,
                                                           ALU.add, ALU.min, accmin[:, i:i + 1])
                            if qt == 0:
                                chain.step(ins)
                            else:
                                free(ins, ("ms", h))
                        drained(dve, ("ms", h), l)
                        chain.wait()
                        dve.sem_inc(m_masked, 1)
                    elif kind == "mPT":
                        if h >= 2:
                            dve.wait_ge(m_pv, l * (MH - 1) + (h - 2) + 1)
                        pb = await_full(dve, ("mPT", h), l)
                        free(dve.tensor_copy(mPT[:, h % 2, :], pb[:, 0:384]), ("mPT", h))
                dve.wait_ge(m_exp, l * (2 * MH) + 2 * MH)
                chain.link(dve.reciprocal(rinv[:, :, 0:MH], rsum[:, :, 0:MH]))
                for t in range(NT):
                    pb = await_full(dve, ("mo", t), l)
                    o = hrow[:, t, 512:1024]
                    free(dve.tensor_tensor(o.rearrange("p (h d) -> p h d", h=MH), quad(pb[:, :]),
                                           bc(rinv[:, t, 0:MH].unsqueeze(2), MH, MDV), ALU.mult), ("mo", t))
                    drained(dve, ("mo", t), l)
                    drained(dve, ("mg", t), l)
                    dve.tensor_tensor(o, o, silu_m[:, t, :], ALU.mult).then_inc(rows_ready, 1)
                for ch in range(2):
                    for t in range(NT):
                        pb = await_full(dve, ("y2", ch, t), l)
                        a = slice(ch * 512, (ch + 1) * 512)
                        free(dve.tensor_tensor(xrow[:, t, a], xrow[:, t, a], pb[:, :], ALU.add), ("y2", ch, t))
                        drained(dve, ("y2", ch, t), l)
                for t in range(NT):
                    dve.sem_inc(x_ready, 1)
                chain.end_loop(LAYERS)


_INS = ["x", "c", "ada_w", "ada_b", "norm1_g", "w_in", "na_rpb", "out_norm_na_g", "out_norm_dil_g", "w_out", "norm2_g",
        "peer_wq", "peer_subkeys", "peer_u", "peer_v", "final_g", "positions_2", "norm_g_2", "w_in_2",
        "w_gla_gate_up_2", "b_gla_gate_2", "gla_norm_g_2", "mla_q_norm_g_2", "w_uq_2", "mla_kv_norm_g_2", "w_ukv_2",
        "q_head_g_2", "k_head_g_2", "w_out_2"]


def kernel(**inputs):
    import concourse.bacc as bacc
    from concourse.bass_utils import run_bass_kernel_spmd

    nc = bacc.Bacc("TRN2", target_bir_lowering=False, num_devices=1)
    arrays, args = {}, []
    for name in _INS:
        a = np.ascontiguousarray(inputs[name])
        arrays[f"in_{name}"] = a
        args.append(nc.dram_tensor(f"in_{name}", a.shape, mybir.dt.from_np(a.dtype), kind="ExternalInput").ap())
    for name, a in zip(("shape_const", "dil_bias_const"), shape_constants()):
        arrays[name] = a
        args.append(nc.dram_tensor(name, a.shape, mybir.dt.from_np(a.dtype), kind="ExternalInput").ap())
    args.append(nc.dram_tensor("out_0", (1, S, D), F32, kind="ExternalOutput").ap())
    program(nc, *args)
    r = run_bass_kernel_spmd(nc, [arrays], core_ids=[0])
    return r.results[0]["out_0"]
```

```python
from contextlib import ExitStack

import numpy as np

import concourse.bass as bass
from concourse import mybir

ALU = mybir.AluOpType
ACT = mybir.ActivationFunctionType
F32 = mybir.dt.float32
BF16 = mybir.dt.bfloat16
U32 = mybir.dt.uint32
I32 = mybir.dt.int32
AX = mybir.AxisListType

P = 128
S = 256
NT = S // P
D = 1024
KD = D // P
EPS = 1e-6
NEG = 1e30

HD = 64
NH = 16
GRID_W = 64
ROWS = S // GRID_W
RPB_R, RPB_C = 15, 31
PH = 8
NKEY = 128
TOPK = 16
SLOTS = PH * TOPK
GROUP = 8
NG = NT * SLOTS // GROUP
PIECES = NT * PH // 2
GPP = NG // PIECES

LAYERS = 2
GH, GDK, GDV, GCH = 4, 64, 128, 64
GATE_TEMP = 16.0
MH, NOPE, ROPE, MDV = 4, 128, 64, 128
QK = NOPE + ROPE
QR, KVR = 256, 128
D_IN = 2512
LR = 16
O_V, O_LR, O_GG, O_C, O_MG = 512, 1024, 1040, 1552, 2000
CW = QR + KVR + ROPE

CONST = {}
_at = 0
for _name, _w in (("ident", 128), ("flip", 128), ("na_window", 512), ("segment", 256), ("same_chunk", 128),
                  ("causal", 384), ("inv_freq", 32), ("iota", 16)):
    CONST[_name] = (_at, _at + _w)
    _at += _w
NCONST = _at


def shape_constants():
    c = np.zeros((P, NCONST), np.float32)

    def put(name, value):
        a, b = CONST[name]
        c[:, a:b] = value

    p = np.arange(P)
    put("ident", np.eye(P))
    put("flip", (p[:, None] // 64 == p[None, :] // 64) & (p[:, None] % 64 == 63 - p[None, :] % 64))
    q = (np.arange(NT)[None, :, None] * P + p[:, None, None])
    k = np.arange(S)[None, None, :]
    c0 = np.clip(q % GRID_W - 8, 0, GRID_W - 16)
    inside = (k % GRID_W >= c0) & (k % GRID_W < c0 + 16)
    put("na_window", np.where(inside, 0.0, NEG).reshape(P, -1))
    put("segment", np.broadcast_to((np.arange(S) % GCH != 0), (P, S)))
    put("same_chunk", (p[:, None] // GCH == p[None, :] // GCH) & (p[:, None] <= p[None, :]))
    tri = np.where(p[None, :] <= p[:, None], 0.0, -NEG)
    put("causal", np.concatenate([tri, np.zeros((P, P)), tri], 1))
    put("inv_freq", np.broadcast_to(10000.0 ** (-np.arange(0, ROPE, 2) / ROPE), (P, ROPE // 2)))
    put("iota", np.broadcast_to(np.arange(16), (P, 16)))
    d = np.abs(q - k)
    count = (d <= 64).astype(int) + (d % 4 == 0) + (d % 16 == 0)
    logc = np.log(np.maximum(count, 1).astype(np.float64))
    slopes = 2.0 ** (-(np.arange(8) + 1.0))
    dil = slopes[None, :, None, None] * d[:, None] - logc[:, None]
    dil = np.where(count[:, None] > 0, dil, NEG).astype(np.float32)
    return c, np.ascontiguousarray(dil.reshape(P, -1))


class Banks:

    def __init__(self):
        self.uses = [0] * 8
        self.jobs = {}
        self.next = 0
        self.base = None

    def plan(self, name, bank=None):
        if bank is None:
            bank, self.next = self.next, (self.next + 1) % 6
        self.jobs[name] = (bank, self.uses[bank], self.base is not None)
        self.uses[bank] += 1

    def start_layer(self):
        self.base = list(self.uses)

    def end_layer(self):
        self.per_layer = [u - b for u, b in zip(self.uses, self.base)]

    def before(self, name, layer):
        bank, n, in_layer = self.jobs[name]
        return bank, (layer * self.per_layer[bank] + n if in_layer else n)


ADA = [2, 3, 0, 1] + list(range(4, 12))


def qkv_schedule():
    out, i = [], 4
    for n in (0, 1, 3, 4, 2, 5):
        out.append(("v" if n in (2, 5) else "qk", n))
        out.append(("ada", i))
        i += 1
        if n in (3, 4):
            out += [("nab", j) for j in range(4 * (n - 3), 4 * (n - 3) + 4)]
    return out


def router_schedule():
    out = []
    for ch in range(5):
        if ch < 4:
            out.append(("pq", ch))
        if ch == 0:
            out.append(("ada", 11))
        if ch > 0:
            out += [("sc", t, ch - 1) for t in range(NT)]
    return out


def attention_schedule():
    out = []
    for h in range(NH + 2):
        if h < NH:
            out.append(("S", h))
        if 1 <= h <= NH:
            out.append(("PT", h - 1))
        if h >= 2:
            out.append(("PV", h - 2))
            if (h - 2) % 8 == 7:
                out.append(("O", (h - 2) // 8))
    return out


def mla_schedule():
    out = []
    for h in range(MH + 2):
        if h < MH:
            out.append(("ms", h))
        if 1 <= h <= MH:
            out.append(("mPT", h - 1))
        if h >= 2:
            out.append(("mPV", h - 2))
    return out


def plan_banks():
    b = Banks()
    for i in range(4):
        b.plan(("ada", i))
    for t in range(NT):
        for g in range(2):
            b.plan(("xT", t, g))
    for kind, n in qkv_schedule():
        if kind in ("qk", "v"):
            for j in range(2):
                b.plan((kind, n, j))
        else:
            b.plan((kind, n))
    for kind, i in attention_schedule():
        if kind == "O":
            continue
        if kind == "PV":
            if i % 8 == 0:
                for qt in range(NT):
                    b.plan(("O", i // 8, qt), 6 + qt)
        else:
            b.plan((kind, i))
    for t in range(NT):
        for g in range(2):
            b.plan(("oT", t, g))
    for ch in range(2):
        for t in range(NT):
            b.plan(("y", ch, t))
        if ch == 0:
            b.plan(("ada", 10))
    for t in range(NT):
        for g in range(2):
            b.plan(("hT", t, g))
    b.plan(("skT",))
    for job in router_schedule():
        if job[0] == "pq":
            for j in range(2):
                b.plan(job + (j,))
        else:
            b.plan(job)
    for t in range(NT):
        for half in range(2):
            b.plan(("peer", t, half), 6 + half if t == 0 else 4 + half)
    b.next = 0
    b.start_layer()
    for t in range(NT):
        for g in range(2):
            b.plan(("zT", t, g))
    for j in range(2):
        b.plan(("gqk", j))
    b.plan(("lr",))
    for t in range(NT):
        b.plan(("c", t))
    b.plan(("gl",))
    for t in range(NT):
        b.plan(("gv", t))
    for t in range(NT):
        b.plan(("cT", t))
    b.plan(("keT",))
    for t in range(NT):
        for hp in range(2):
            b.plan(("uq", t, hp))
            b.plan(("ukv", t, hp))
    for odd in range(2):
        b.plan(("A", odd))
    for i in range(3):
        b.plan(("U", i))
    for t in range(NT):
        b.plan(("gg", t))
    for t in range(NT):
        b.plan(("mg", t))
    for odd in range(2):
        b.plan(("go", odd), 6 + odd)
    for t in range(NT):
        b.plan(("qnT", t))
        b.plan(("knT", t))
    b.plan(("qrT",))
    b.plan(("krT",))
    for kind, i in mla_schedule():
        if kind == "mPV":
            if i == 0:
                for qt in range(NT):
                    b.plan(("mo", qt), 6 + qt)
        else:
            b.plan((kind, i))
    for t in range(NT):
        for g in range(2):
            b.plan(("cT2", t, g))
    for ch in range(2):
        for t in range(NT):
            b.plan(("y2", ch, t))
    b.end_layer()
    return b


class Chain:

    def __init__(self, eng, sem):
        self.eng, self.sem, self.n, self.turn = eng, sem, 0, None

    def step(self, ins):
        ins.then_inc(self.sem, 1)
        self.n += 1

    def wait(self):
        self.eng.wait_ge(self.sem, self.n if self.turn is None else self.turn * self.per + self.n)

    def link(self, ins):
        self.step(ins)
        self.wait()

    def loop(self, turn, per):
        self.turn, self.per, self.from_ = turn, per, self.n

    def end_loop(self, turns):
        assert self.n - self.from_ == self.per, (self.n - self.from_, self.per)
        self.n, self.turn = self.from_ + self.per * turns, None


def program(nc, x, c, ada_w, ada_b, norm1_g, w_in, na_rpb, out_norm_na_g, out_norm_dil_g, w_out, norm2_g,
            peer_wq, peer_subkeys, peer_u, peer_v, final_g, positions_2, norm_g_2, w_in_2, w_gla_gate_up_2,
            b_gla_gate_2, gla_norm_g_2, mla_q_norm_g_2, w_uq_2, mla_kv_norm_g_2, w_ukv_2, q_head_g_2,
            k_head_g_2, w_out_2, shape_const, dil_bias_const, out):
    ctx = ExitStack()
    with ctx:
        def sb(name, shape, dt=F32):
            return ctx.enter_context(nc.sbuf_tensor(name, shape, dt))

        def sem(name):
            return ctx.enter_context(nc.semaphore(name))

        banks = plan_banks()
        bank = [ctx.enter_context(nc.psum_tensor(f"bank{i}", [P, 512], F32)) for i in range(8)]

        wring = sb("wring", [P, 4, 4096])
        xrow = sb("xrow", [P, NT, D])
        hrow = sb("hrow", [P, NT, D])
        hT = sb("hT", [P, KD, S])
        modb = sb("modb", [P, 6, D])
        gains = sb("gains", [P, 3, D])
        R = sb("R", [P, 16384])
        ada_sum = sb("ada_sum", [P, 2, 512])
        start = sb("start", [P, 640])
        pT = sb("pT", [P, 2, 512])
        const = sb("const", [P, NCONST - 640])
        skrow = sb("skrow", [P, 2, P])
        skT = sb("skT", [P, 2, P])
        ids = sb("ids", [P, NT * SLOTS], U32)
        gates = sb("gates", [P, NT * SLOTS])
        rope = sb("rope", [P, NT, 2, ROPE // 2])
        small = sb("small", [P, 256])

        def region(at, *shape, dt=F32):
            n = int(np.prod(shape))
            v = R[:, at:at + n] if dt == F32 else R[:, at:at + n].bitcast(dt)
            names = "abcd"[:len(shape)]
            return v if len(shape) == 1 else v.rearrange(
                f"p ({' '.join(names)}) -> p {' '.join(names)}", **dict(zip(names[1:], shape[1:])))

        kept = ["ident", "segment", "same_chunk", "causal", "inv_freq", "iota"]
        at_const, where = 0, {}
        for name in kept:
            a, b = CONST[name]
            where[name] = const[:, at_const:at_const + b - a]
            at_const += b - a
        ident, segment, causal, inv_freq, iota = (where[n] for n in ("ident", "segment", "causal", "inv_freq", "iota"))
        same_chunk = where["same_chunk"].bitcast(U32)

        bias = region(0, NH, NT, S)
        qkT = region(8192, 16, S)
        vrow = region(12288, NT, D)
        flip = start[:, 0:P]
        na_window = start[:, P:640].rearrange("p (t s) -> p t s", t=NT)
        na_raw = [hrow[:, :, :].rearrange("p a b -> p (a b)").rearrange("p (h s) -> p h s", h=8), region(14336, 8, S)]
        Tm = region(14336, 2, NT, S)
        Em = region(15360, 2, NT, S)
        junk = R[:, 15872:16384].bitcast(BF16)
        pqT = region(0, 16, S)
        scores = region(4096, PIECES, 4, NKEY)
        one_piece = region(8192, 4, NKEY)
        cand = region(8704, 2, TOPK * TOPK)
        hit = region(9216, 4, TOPK, TOPK)
        top_v = region(10240, 2, 2, TOPK)
        top_i = region(10304, 2, 2, TOPK, dt=U32)
        best_v = region(10368, 2, TOPK)
        best_j = region(10400, 2, TOPK, dt=U32)
        best_ab = region(10432, 2, 2, TOPK, dt=U32)
        picked = region(10496, 2, 2, TOPK)
        shifted = region(10560, 2, TOPK)
        ytmp = region(14336, 2, 512)
        urow = wring[:, 0:2, :].rearrange("p a (b d) -> p (a b) d", d=D)
        vgat = wring[:, 2:4, :].rearrange("p a (b d) -> p (a b) d", d=D)
        diag = hT[:, :, :].rearrange("p a b -> p (a b)").rearrange("p (s m) -> p s m", m=P)
        zeros = pT[:, 0, 0:P]
        ones = gates[:, 0:P]

        M = modb[:, :, :].rearrange("p a b -> p (a b)")

        def mod_region(at, *shape):
            n = int(np.prod(shape))
            names = "abcd"[:len(shape)]
            return M[:, at:at + n].rearrange(
                f"p ({' '.join(names)}) -> p {' '.join(names)}", **dict(zip(names[1:], shape[1:])))

        gqT = mod_region(0, 2, S)
        gkT = mod_region(512, 2, S)
        log_a = mod_region(1024, 2, S)
        gtmp = mod_region(1536, 2, S)
        bcum = mod_region(2048, 2, S)
        eb = mod_region(2560, 2, S)
        ki = mod_region(3072, 2, S)
        ke = mod_region(3584, 2, S)
        keR = mod_region(4096, NT, 2, P)
        aT = mod_region(4608, NT, GH, P)
        up = mod_region(5632, 256)
        lrT = mod_region(5888, 256)
        gv = region(0, NT, 512)
        state = region(1024, 3, 2, GDV)
        crow = region(1792, NT, CW)
        cqT = region(2688, 3, S)
        qrow = region(3456, NT, MH, QK)
        kvrow = region(4992, NT, MH, NOPE + MDV)
        qrr = region(7040, NT, MH, ROPE)
        krr = region(7552, NT, MH, ROPE)
        qnT = region(8064, MH, S)
        knT = region(9088, MH, S)
        qrT = region(10112, 2, S)
        krT = region(10624, 2, S)
        mT = region(11136, 2, 384)
        mE = region(11904, 2, 384)
        mPT = pT[:, :, 0:384]
        silu_g = region(12672, NT, 512)
        silu_m = region(13696, NT, 512)
        wide = region(14720, 768)
        kpe = region(15488, NT, ROPE)
        kpr = region(15616, NT, ROPE)
        gains2 = gains[:, 1:3, :].rearrange("p a b -> p (a b)")
        g_in, g_gla, g_q, g_kv = gains2[:, 0:1024], gains2[:, 1024:1152], gains2[:, 1152:1408], gains2[:, 1408:1536]
        g_qh, g_kh = gains2[:, 1536:1728], gains2[:, 1728:1920]

        def col(a, n=1):
            return small[:, a:a + n]

        cT, csil = col(0, 8), col(8, 8)
        ss, rstd = col(16, 16), col(32, 16)
        accmin = col(48, 4)
        rsum = small[:, 56:88].rearrange("p (t h) -> p t h", t=NT)
        rinv = small[:, 88:104].rearrange("p (t h) -> p t h", t=NT)
        bgate = col(104, 2)
        posf = col(106, 2)
        posi = small[:, 108:110].bitcast(I32)
        a8 = small[:, 112:128].rearrange("p (b s) -> p b s", b=2)
        g8 = small[:, 128:144].rearrange("p (b s) -> p b s", b=2)
        w8 = small[:, 144:160].rearrange("p (b s) -> p b s", b=2)
        idu = small[:, 160:176].bitcast(U32).rearrange("p (b s) -> p b s", b=2)
        idv = small[:, 176:192].bitcast(U32).rearrange("p (b s) -> p b s", b=2)
        decay = small[:, 192:200].rearrange("p (a c) -> p a c", a=2)
        ssh, rstdh = col(200, 24), col(224, 24)
        eps = col(248)
        half_pi = col(249)
        gsum = small[:, 208:224]
        ssg = col(240, 8)

        w_landed = [sem(f"w_landed{i}") for i in range(4)]
        bank_full = [sem(f"bank_full{i}") for i in range(8)]
        bank_free = [sem(f"bank_free{i}") for i in range(8)]
        x_landed, c_landed, const_landed, gains_landed = sem("x_landed"), sem("c_landed"), sem("const_landed"), sem("gains_landed")
        adab_landed, rpb_landed, dil_landed, sk_landed = sem("adab_landed"), sem("rpb_landed"), sem("dil_landed"), sem("sk_landed")
        fing_landed, gains2_landed = sem("fing_landed"), sem("gains2_landed")
        act_step, dve_step, pool_step = sem("act_step"), sem("dve_step"), sem("pool_step")
        consts_set = sem("consts_set")
        silu_ready = sem("silu_ready")
        modb_zero = sem("modb_zero")
        ada_summed = sem("ada_summed")
        ang_ready = sem("ang_ready")
        rope_ready = sem("rope_ready")
        rstd_ready = sem("rstd_ready")
        rows_ready = sem("rows_ready")
        masked_ready = sem("masked_ready")
        exp_ready = sem("exp_ready")
        pv_done = sem("pv_done")
        x_ready = sem("x_ready")
        softmax_shift = sem("softmax_shift")
        gate_exp = sem("gate_exp")
        ids_ready = sem("ids_ready")
        u_landed = [sem(f"u_landed{i}") for i in range(GROUP)]
        v_landed = [sem(f"v_landed{i}") for i in range(GROUP)]
        u_free = sem("u_free")
        gelu_ready = sem("gelu_ready")
        weights_ready = sem("weights_ready")
        diag_ready = sem("diag_ready")
        v_free = sem("v_free")
        exp_gate = sem("exp_gate")
        dve_to_act = sem("dve_to_act")
        dve_to_pe = sem("dve_to_pe")
        m_masked, m_exp, m_pv = sem("m_masked"), sem("m_exp"), sem("m_pv")
        gains2_used = sem("gains2_used")
        waits_passed = sem("waits_passed")
        out_done = sem("out_done")

        def claim(pe, job, l=None):
            b, n = banks.before(job, l)
            if l is not None or n > 0:
                pe.wait_ge(bank_free[b], n)
            return bank[b]

        def full(ins, job):
            ins.then_inc(bank_full[banks.jobs[job][0]], 1)

        def await_full(eng, job, l=None):
            b, n = banks.before(job, l)
            eng.wait_ge(bank_full[b], n + 1)
            return bank[b]

        def free(ins, job):
            ins.then_inc(bank_free[banks.jobs[job][0]], 1)

        def drained(eng, job, l=None):
            b, n = banks.before(job, l)
            eng.wait_ge(bank_free[b], n + 1)

        def wait_alone(eng):
            eng.sem_inc(waits_passed, 1)

        def quad(ap):
            return ap.rearrange("p (a b) -> p a b", a=4)

        def chunk_dram(w, l, a, b):
            return w[l, :, a:b].rearrange("(k p) n -> p k n", p=P)

        W1 = [(ada_w, 512 * ADA[i], ("ada", i)) for i in range(4)]
        for kind, n in qkv_schedule():
            if kind == "ada":
                W1.append((ada_w, 512 * ADA[n], ("ada", n)))
            elif kind != "nab":
                W1.append((w_in, 512 * n, (kind, n, 1)))
        W1 += [(w_out, 512 * n, ("y", n, 1)) for n in range(2)]
        W1 += [(ada_w, 512 * ADA[i], ("ada", i)) for i in (10, 11)]
        W1 += [(peer_wq, 512 * n, ("pq", n, 1)) for n in range(4)]
        W1_AT = {job: n for n, (_, _, job) in enumerate(W1)}
        CPL = 8
        W1_USES = len(W1) // 4

        def slot512(n):
            return wring[:, n % 4, :].rearrange("p (k m) -> p k m", k=KD)

        def weights1(pe, job):
            n = W1_AT[job]
            pe.wait_ge(w_landed[n % 4], 16 * (n // 4 + 1))
            return slot512(n)

        DMAS2 = [1, 2, 1, 2, 1, 1, 1, 1]

        def landed2(eng, n, l):
            s = n % 4
            per = 16 * (DMAS2[s] + DMAS2[s + 4])
            here = 16 * sum(DMAS2[j] for j in range(s, n + 1, 4))
            eng.wait_ge(w_landed[s], l * per + 16 * W1_USES + here)
            return wring[:, s, :]

        LAST2 = [("gqk", 1), ("c", 1), ("gv", 1), ("ukv", 1, 1), ("gg", 1), ("mg", 1), ("y2", 0, 1), ("y2", 1, 1)]

        block = ctx.enter_context(nc.Block())

        @block.sync
        def _(sp):
            for n, (w, a, _) in enumerate(W1):
                if n >= 4:
                    before = W1[n - 4][2]
                    if before[0] == "ada":
                        sp.wait_ge(ada_summed, before[1] + 1)
                    else:
                        await_full(sp, before)
                sp.dma_start(slot512(n), chunk_dram(w, 0, a, a + 512)).then_inc(w_landed[n % 4], 16)

            def layer_chunk(n, l):
                dst, s = wring[:, n % 4, :], w_landed[n % 4]
                if n == 3:
                    sp.dma_start(dst[:, 0:1536].rearrange("p (k m) -> p k m", k=2),
                                 w_uq_2[l].rearrange("(k p) n -> p k n", p=P)).then_inc(s, 16)
                    sp.dma_start(dst[:, 1536:2560], w_ukv_2[l]).then_inc(s, 16)
                elif n == 1:
                    d = dst.rearrange("p (k m) -> p k m", k=KD)
                    sp.dma_start(d[:, :, 0:LR], chunk_dram(w_in_2, l, O_LR, O_LR + LR)).then_inc(s, 16)
                    sp.dma_start(d[:, :, LR:LR + CW], chunk_dram(w_in_2, l, O_C, O_C + CW)).then_inc(s, 16)
                else:
                    w, a = {0: (w_in_2, 0), 2: (w_in_2, O_V), 4: (w_in_2, O_GG), 5: (w_in_2, O_MG),
                            6: (w_out_2, 0), 7: (w_out_2, 512)}[n]
                    sp.dma_start(dst.rearrange("p (k m) -> p k m", k=KD), chunk_dram(w, l, a, a + 512)).then_inc(s, 16)

            for n in range(4):
                sp.wait_ge(u_free if n < 2 else v_free, NG * GROUP)
                layer_chunk(n, 0)
            with sp.Fori(0, LAYERS - 1) as l:
                for n in range(4, CPL):
                    await_full(sp, LAST2[n - 4], l)
                    layer_chunk(n, l)
                for n in range(4):
                    await_full(sp, LAST2[n + 4], l)
                    layer_chunk(n, l + 1)
            for n in range(4, CPL):
                await_full(sp, LAST2[n - 4], LAYERS - 1)
                layer_chunk(n, LAYERS - 1)
            sp.wait_ge(x_ready, NT * (3 + LAYERS))
            sp.dma_start(out[0].rearrange("(t p) d -> p t d", p=P), xrow[:, :, :]).then_inc(out_done, 16)
            sp.wait_ge(out_done, 16)

        @block.gpsimd
        def _(pool):
            chain = Chain(pool, pool_step)

            chain.link(pool.memset(modb[:, :, :].rearrange("p a b -> p (a b)"), 0.0))
            pool.dma_start(modb[0:1, :, :].rearrange("p a b -> p (a b)"), ada_b).then_inc(adab_landed, 16)
            pool.dma_start(gains[:, 0, :], norm1_g[0].partition_broadcast(P)).then_inc(gains_landed, 16)

            pool.wait_ge(ang_ready, 1)
            pool.wait_ge(rstd_ready, 1)
            for t in range(NT):
                for g in range(2):
                    drained(pool, ("xT", t, g))
            for r in range(ROWS):
                pb, qt = 64 * (r % 2), r // 2
                for kr in range(ROWS):
                    src = bass.AP(na_rpb.tensor, (kr - r + 7) * RPB_C - 48, [[1, 64], [RPB_R * RPB_C, 8], [1, 64]])
                    pool.dma_start(na_raw[qt][pb:pb + 64, :, kr * GRID_W:(kr + 1) * GRID_W], src).then_inc(rpb_landed, 16)
            pool.wait_ge(rows_ready, NT)
            pool.dma_start(gains[:, 0, :], final_g.partition_broadcast(P)).then_inc(fing_landed, 16)
            pool.dma_start(bias[:, 8:16, :, :].rearrange("p h t s -> p (h t s)"), dil_bias_const).then_inc(dil_landed, 16)
            pool.dma_start(gains[:, 2, 0:512], out_norm_na_g[0].partition_broadcast(P)).then_inc(gains_landed, 16)
            pool.dma_start(gains[:, 2, 512:1024], out_norm_dil_g[0].partition_broadcast(P)).then_inc(gains_landed, 16)
            pool.dma_start(gains[:, 1, :], norm2_g[0].partition_broadcast(P)).then_inc(gains_landed, 16)
            pool.dma_start(skrow[:, :, :], peer_subkeys[0].rearrange("s n d -> n s d")).then_inc(sk_landed, 16)

            def gather(dst, table, index, landed):
                wait_alone(pool)
                pool.indirect_dma_start(dst, None, table, bass.IndirectOffsetOnAxis(index, 0)).then_inc(landed, 16)

            def stage_ids(dst, n):
                wait_alone(pool)
                chain.link(pool.tensor_copy(dst, ids[:, bass.ds(n * GROUP, GROUP)] if not isinstance(n, int)
                                            else ids[:, n * GROUP:(n + 1) * GROUP]))

            def u_rows(n, s, b, first=False):
                if not first:
                    pool.wait_ge(u_free, (n - 1) * GROUP + s + 1)
                gather(urow[:, s, :], peer_u[0], idu[:, b, s:s + 1], u_landed[s])

            def v_rows(n, s, b, first=False):
                if not first:
                    pool.wait_ge(v_free, (n - 1) * GROUP + s + 1)
                gather(vgat[:, s, :], peer_v[0], idv[:, b, s:s + 1], v_landed[s])

            def piece(n, k, first=False, last=False):
                for b in range(GPP):
                    more = not (last and b == GPP - 1)
                    if more:
                        if b == GPP - 1:
                            pool.wait_ge(ids_ready, k + 2)
                        stage_ids(idu[:, (b + 1) % 2, :], n + b + 1)
                    stage_ids(idv[:, b % 2, :], n + b)
                    for s in range(GROUP):
                        if more:
                            u_rows(n + b + 1, s, (b + 1) % 2)
                        v_rows(n + b, s, b % 2, first and b == 0)

            pool.wait_ge(ids_ready, 1)
            await_full(pool, ("pq", 1, 1))
            stage_ids(idu[:, 0, :], 0)
            for s in range(GROUP):
                u_rows(0, s, 0, first=True)
            await_full(pool, ("pq", 3, 1))
            piece(0, 0, first=True)
            with pool.Fori(1, PIECES - 1) as k:
                chain.loop(k - 1, 2 * GPP)
                piece(k * GPP, k)
                chain.end_loop(PIECES - 2)
            piece(NG - GPP, PIECES - 1, last=True)

            def load_gains(l):
                at = 0
                for g, n in ((norm_g_2, 1024), (gla_norm_g_2, 128), (mla_q_norm_g_2, 256), (mla_kv_norm_g_2, 128),
                             (q_head_g_2, QK), (k_head_g_2, QK)):
                    pool.dma_start(gains2[:, at:at + n], g[l].partition_broadcast(P)).then_inc(gains2_landed, 16)
                    at += n
                pool.dma_start(bgate, b_gla_gate_2[l].rearrange("(a p) -> p a", p=P), allow_slow_non_contiguous=True).then_inc(gains2_landed, 16)
                pool.dma_start(up[0:LR, :], w_gla_gate_up_2[l]).then_inc(gains2_landed, 16)

            pool.wait_ge(x_ready, NT * 2)
            load_gains(0)
            pool.wait_ge(gains2_used, 1)
            load_gains(1)

        @block.scalar
        def _(act):
            chain = Chain(act, act_step)

            act.dma_start(cT, c[0].rearrange("(k p) -> p k", p=P), allow_slow_non_contiguous=True).then_inc(c_landed, 16)
            for name in kept:
                a, b = CONST[name]
                act.dma_start(where[name], shape_const[:, a:b]).then_inc(const_landed, 16)
            a, b = CONST["flip"]
            act.dma_start(flip, shape_const[:, a:b]).then_inc(const_landed, 16)
            a, b = CONST["na_window"]
            act.dma_start(na_window.rearrange("p t s -> p (t s)"), shape_const[:, a:b]).then_inc(const_landed, 16)
            act.dma_start(posi, positions_2[0].rearrange("(t p) -> p t", p=P), allow_slow_non_contiguous=True).then_inc(const_landed, 16)
            act.dma_start(xrow[:, :, :], x[0].rearrange("(t p) d -> p t d", p=P)).then_inc(x_landed, 16)
            def rms(srcs, dim, cols, dst=None):
                for s, i in zip(srcs, cols):
                    w = int(np.prod(s.shape[1:]))
                    chain.link(act.activation(junk[:, 0:w], s, ACT.Square, accum_out=ss[:, i:i + 1]))
                a, b = cols[0], cols[-1] + 1
                chain.wait()
                chain.link(act.activation(ss[:, a:b], ss[:, a:b], ACT.Ln, scale=1.0 / dim, bias=eps))
                return act.activation(rstd[:, a:b], ss[:, a:b], ACT.Exp, scale=-0.5)

            act.wait_ge(c_landed, 16)
            act.activation(csil, cT, ACT.Silu).then_inc(silu_ready, 1)
            act.wait_ge(x_landed, 16)
            act.wait_ge(consts_set, 1)
            rms([xrow[:, t, :] for t in range(NT)], D, [0, 1]).then_inc(rstd_ready, 1)

            def evac_T(kind, l=None):
                for t in range(NT):
                    for g in range(2):
                        pb = await_full(act, (kind, t, g), l)
                        free(act.activation(hT[:, 4 * g:4 * g + 4, t * P:(t + 1) * P], quad(pb[:, :]), ACT.Copy), (kind, t, g))

            def ada_out(i):
                n = ADA[i]
                pb = await_full(act, ("ada", i))
                free(act.activation(modb[:, n // 2, (n % 2) * 512:(n % 2 + 1) * 512], pb[:, :], ACT.Copy), ("ada", i))

            for i in range(4):
                ada_out(i)
            evac_T("xT")
            act.wait_ge(ang_ready, 1)
            act.activation(rope[:, :, :, :].rearrange("p t s f -> p (t s f)"),
                           rope[:, :, :, :].rearrange("p t s f -> p (t s f)"), ACT.Sin).then_inc(rope_ready, 1)
            for kind, n in qkv_schedule():
                if kind == "qk":
                    for j in range(2):
                        pb = await_full(act, ("qk", n, j))
                        i = {0: 0, 1: 4, 3: 8, 4: 12}[n] + 2 * j
                        free(act.activation(qkT[:, i:i + 2, :].rearrange("p a b -> p (a b)"), pb[:, :], ACT.Copy,
                                            scale=-HD ** -0.5 if n in (0, 3) else 1.0), ("qk", n, j))
                elif kind == "v":
                    for t in range(NT):
                        pb = await_full(act, ("v", n, t))
                        a = 0 if n == 2 else 512
                        free(act.activation(vrow[:, t, a:a + 512], pb[:, :], ACT.Copy), ("v", n, t))
                elif kind == "ada":
                    ada_out(n)

            for h in range(NH):
                act.wait_ge(masked_ready, h + 1)
                if h >= 2:
                    await_full(act, ("PT", h - 2))
                for qt in range(NT):
                    i = 2 * (h % 2) + qt
                    act.activation(Em[:, h % 2, qt, :], Tm[:, h % 2, qt, :], ACT.Exp, scale=-1.0,
                                   bias=accmin[:, i:i + 1], accum_out=rsum[:, qt, h:h + 1]).then_inc(exp_ready, 1)

            act.wait_ge(rows_ready, NT + 1)
            rms([hrow[:, t, g * 512:(g + 1) * 512] for t in range(NT) for g in range(2)], 512, [0, 1, 2, 3]).then_inc(rstd_ready, 1)
            evac_T("oT")
            ada_out(10)
            for t in range(NT):
                act.wait_ge(x_ready, t + 1)
                rms([xrow[:, t, :]], D, [t]).then_inc(rstd_ready, 1)
            evac_T("hT")

            def exponentials_of_gates(k):
                act.wait_ge(softmax_shift, k + 1)
                wait_alone(act)
                act.activation(shifted, shifted, ACT.Exp).then_inc(gate_exp, 1)

            for job in router_schedule():
                if job[0] == "pq":
                    ch = job[1]
                    for j in range(2):
                        pb = await_full(act, ("pq", ch, j))
                        i = 4 * ch + 2 * j
                        free(act.activation(pqT[:, i:i + 2, :].rearrange("p a b -> p (a b)"), pb[:, :], ACT.Copy), ("pq", ch, j))
                    if ch == 2:
                        exponentials_of_gates(0)
                elif job[0] == "ada":
                    ada_out(11)
                else:
                    _, t, g = job
                    pb = await_full(act, job)
                    free(act.activation(scores[:, 4 * t + g, :, :].rearrange("p a b -> p (a b)"), pb[:, :], ACT.Copy), job)

            def peer_group(n, b, first=False):
                act.wait_ge(u_free, (n + 1) * GROUP)
                act.activation(g8[:, b, :], a8[:, b, :], ACT.Gelu).then_inc(gelu_ready, 1)
                act.wait_ge(weights_ready, n + 1)
                for s in range(GROUP):
                    if not first:
                        act.wait_ge(v_free, (n - 2) * GROUP + s + 1)
                    act.activation(diag[:, b * GROUP + s, :], ident, ACT.Copy, scale=w8[:, b, s:s + 1]).then_inc(diag_ready, 1)

            def piece(k, first=False, last=False):
                for b in range(GPP):
                    peer_group(k * GPP + b, b % 2, first and b < 2)
                    if b == 1 and not last:
                        exponentials_of_gates(k + 1)

            piece(0, first=True)
            with act.Fori(1, PIECES - 1) as k:
                piece(k)
            piece(PIECES - 1, last=True)

            for t in range(NT):
                act.wait_ge(x_ready, NT + t + 1)
                rms([xrow[:, t, :]], D, [t]).then_inc(rstd_ready, 1)

            with act.Fori(0, LAYERS) as l:
                chain.loop(l, 48)
                for t in range(NT):
                    act.wait_ge(x_ready, l * NT + NT * 2 + t + 1)
                rms([xrow[:, t, :] for t in range(NT)], D, [4, 5]).then_inc(rstd_ready, 1)
                evac_T("zT", l)
                for j in range(2):
                    pb = await_full(act, ("gqk", j), l)
                    dst = (gqT, gkT)[j]
                    free(act.activation(dst.rearrange("p a b -> p (a b)"), pb[:, :], ACT.Copy,
                                        scale=GDK ** -0.5 if j == 0 else 1.0), ("gqk", j))
                pb = await_full(act, ("lr",), l)
                free(act.activation(lrT[0:LR, :], pb[0:LR, 0:S], ACT.Copy), ("lr",))
                for t in range(NT):
                    pb = await_full(act, ("c", t), l)
                    chain.link(act.activation(junk[:, 0:QR], pb[:, 0:QR], ACT.Square, accum_out=ss[:, 6 + t:7 + t]))
                    chain.link(act.activation(junk[:, 0:KVR], pb[:, QR:QR + KVR], ACT.Square, accum_out=ss[:, 8 + t:9 + t]))
                    free(act.activation(crow[:, t, :], pb[:, 0:CW], ACT.Copy), ("c", t))
                chain.wait()
                chain.step(act.activation(ss[:, 6:8], ss[:, 6:8], ACT.Ln, scale=1.0 / QR, bias=eps))
                chain.link(act.activation(ss[:, 8:10], ss[:, 8:10], ACT.Ln, scale=1.0 / KVR, bias=eps))
                act.activation(rstd[:, 6:10], ss[:, 6:10], ACT.Exp, scale=-0.5).then_inc(rstd_ready, 1)
                act.wait_ge(gains2_landed, l * 128 + 128)
                pb = await_full(act, ("gl",), l)
                for a in range(2):
                    chain.step(act.activation(gtmp[:, a, :], pb[:, a * S:(a + 1) * S], ACT.Abs, bias=bgate[:, a:a + 1]))
                chain.wait()
                gt = gtmp.rearrange("p a b -> p (a b)")
                chain.link(act.activation(gt, gt, ACT.Exp, scale=-1.0))
                act.activation(gt, gt, ACT.Ln, bias=1.0).then_inc(exp_gate, 1)
                for t in range(NT):
                    pb = await_full(act, ("gv", t), l)
                    free(act.activation(gv[:, t, :], pb[:, :], ACT.Copy), ("gv", t))
                act.wait_ge(dve_to_act, l * 2 + 1)
                act.activation(eb.rearrange("p a b -> p (a b)"), bcum.rearrange("p a b -> p (a b)"), ACT.Exp,
                               scale=1.0 / GATE_TEMP).then_inc(exp_gate, 1)
                act.activation(ki.rearrange("p a b -> p (a b)"), bcum.rearrange("p a b -> p (a b)"), ACT.Exp,
                               scale=-1.0 / GATE_TEMP).then_inc(exp_gate, 1)
                act.wait_ge(dve_to_act, l * 2 + 2)
                act.activation(ke.rearrange("p a b -> p (a b)"), ke.rearrange("p a b -> p (a b)"), ACT.Exp,
                               scale=1.0 / GATE_TEMP).then_inc(exp_gate, 1)
                for t in range(NT):
                    pb = await_full(act, ("cT", t), l)
                    free(act.activation(cqT[:, :, t * P:(t + 1) * P], pb[:, 0:384].rearrange("p (a b) -> p a b", a=3), ACT.Copy),
                         ("cT", t))
                for t in range(NT):
                    chain.link(act.activation(junk[:, 0:ROPE], crow[:, t, QR + KVR:CW], ACT.Square,
                                              accum_out=ssh[:, 16 + t:17 + t]))
                    for hp in range(2):
                        pb = await_full(act, ("uq", t, hp), l)
                        for i in range(2):
                            h = 2 * hp + i
                            chain.link(act.activation(junk[:, 0:QK], pb[:, i * QK:(i + 1) * QK], ACT.Square,
                                                      accum_out=ssh[:, 4 * t + h:4 * t + h + 1]))
                        free(act.activation(qrow[:, t, 2 * hp:2 * hp + 2, :].rearrange("p a b -> p (a b)"),
                                            pb[:, 0:2 * QK], ACT.Copy), ("uq", t, hp))
                        pb = await_full(act, ("ukv", t, hp), l)
                        for i in range(2):
                            h = 2 * hp + i
                            chain.link(act.activation(junk[:, 0:NOPE], pb[:, i * 256:i * 256 + NOPE], ACT.Square,
                                                      accum_out=ssh[:, 8 + 4 * t + h:9 + 4 * t + h]))
                        free(act.activation(kvrow[:, t, 2 * hp:2 * hp + 2, :].rearrange("p a b -> p (a b)"),
                                            pb[:, :], ACT.Copy), ("ukv", t, hp))
                    for h in range(MH):
                        i = 8 + 4 * t + h
                        if h == 0:
                            chain.wait()
                        chain.step(act.activation(ssh[:, i:i + 1], ssh[:, i:i + 1], ACT.Identity, bias=ssh[:, 16 + t:17 + t]))
                chain.wait()
                chain.link(act.activation(rstdh[:, 0:16], ssh[:, 0:16], ACT.Ln, scale=1.0 / QK, bias=eps))
                act.activation(rstdh[:, 0:16], rstdh[:, 0:16], ACT.Exp, scale=-0.5).then_inc(rstd_ready, 1)
                for kind, dst in (("gg", silu_g), ("mg", silu_m)):
                    for t in range(NT):
                        pb = await_full(act, (kind, t), l)
                        act.activation(dst[:, t, :], pb[:, :], ACT.Exp, scale=-1.0).then_inc(exp_gate, 1)
                for odd in range(2):
                    pb = await_full(act, ("go", odd), l)
                    for i in range(4):
                        j = 2 * i + odd
                        chain.link(act.activation(junk[:, 0:GDV], pb[:, i * GDV:(i + 1) * GDV], ACT.Square,
                                                  accum_out=ssg[:, j:j + 1]))
                chain.wait()
                chain.link(act.activation(ssg[:, 0:8], ssg[:, 0:8], ACT.Ln, scale=1.0 / GDV, bias=eps))
                act.activation(ssg[:, 0:8], ssg[:, 0:8], ACT.Exp, scale=-0.5).then_inc(rstd_ready, 1)
                for t in range(NT):
                    for kind, dst in (("qnT", qnT), ("knT", knT)):
                        pb = await_full(act, (kind, t), l)
                        free(act.activation(dst[:, :, t * P:(t + 1) * P], quad(pb[:, :]), ACT.Copy), (kind, t))
                for kind, dst in (("qrT",  qrT), ("krT", krT)):
                    pb = await_full(act, (kind,), l)
                    free(act.activation(dst.rearrange("p a b -> p (a b)"), pb[:, :], ACT.Copy), (kind,))
                for h in range(MH):
                    act.wait_ge(m_masked, l * MH + h + 1)
                    if h >= 2:
                        await_full(act, ("mPT", h - 2), l)
                    for qt in range(NT):
                        a, n = (0, P) if qt == 0 else (P, S)
                        i = 2 * (h % 2) + qt
                        act.activation(mE[:, h % 2, a:a + n], mT[:, h % 2, a:a + n], ACT.Exp, scale=-1.0,
                                       bias=accmin[:, i:i + 1], accum_out=rsum[:, qt, h:h + 1]).then_inc(m_exp, 1)
                evac_T("cT2", l)
                chain.end_loop(LAYERS)

        @block.tensor
        def _(pe):
            def transposes(kind, rows_before, l=None, rows=None):
                for t in range(NT):
                    pe.wait_ge(rows_ready, rows_before + t + 1)
                    for g in range(2):
                        pb = claim(pe, (kind, t, g), l)
                        for j in range(4):
                            a = (4 * g + j) * P
                            last = pe.transpose(pb[:, j * P:(j + 1) * P], hrow[:, t, a:a + P], ident)
                        full(last, (kind, t, g))

            def rows_product(job, w, n, t, l=None, k0=0, wcol=0):
                pb = claim(pe, job, l)
                for k in range(KD):
                    last = pe.matmul(pb[:, 0:n], hT[:, k, t * P:(t + 1) * P], w[:, k, wcol:wcol + n], start=k == 0, stop=k == KD - 1)
                full(last, job)

            def columns_product(job, w, j, l=None):
                pb = claim(pe, job, l)
                for i in range(2):
                    a = (2 * j + i) * P
                    for k in range(KD):
                        last = pe.matmul(pb[:, i * S:(i + 1) * S], w[:, k, a:a + P], hT[:, k, :], start=k == 0, stop=k == KD - 1)
                full(last, job)

            def ada(i):
                pe.wait_ge(ada_summed, i + 1)
                pb = claim(pe, ("ada", i))
                full(pe.matmul(pb[:, :], ones, ada_sum[:, i % 2, :], start=True, stop=True), ("ada", i))

            for i in range(4):
                ada(i)
            pe.wait_ge(const_landed, 16 * (len(kept) + 3))
            transposes("xT", 0)
            for t in range(NT):
                for g in range(2):
                    drained(pe, ("xT", t, g))
            for kind, n in qkv_schedule():
                if kind == "qk":
                    w = weights1(pe, ("qk", n, 1))
                    for j in range(2):
                        columns_product(("qk", n, j), w, j)
                elif kind == "v":
                    w = weights1(pe, ("v", n, 1))
                    for t in range(NT):
                        rows_product(("v", n, t), w, 512, t)
                elif kind == "ada":
                    ada(n)
                else:
                    pe.wait_ge(rpb_landed, 16 * ROWS * ROWS)
                    pb = claim(pe, ("nab", n))
                    qt, part = n // 4, n % 4
                    full(pe.matmul(pb[:, :], flip, na_raw[qt][:, 2 * part:2 * part + 2, :].rearrange("p a b -> p (a b)"),
                                   start=True, stop=True), ("nab", n))

            def scores_of(h):
                if h == 0:
                    for ch in (0, 1, 3, 4):
                        for j in range(2):
                            drained(pe, ("qk", ch, j))
                qi, ki_ = (h // 2, 4 + h // 2) if h < 8 else (8 + (h - 8) // 2, 12 + (h - 8) // 2)
                p0 = HD * (h % 2)
                pb = claim(pe, ("S", h))
                for qt in range(NT):
                    last = pe.matmul(pb[:, qt * S:(qt + 1) * S], qkT[p0:p0 + HD, qi, qt * P:(qt + 1) * P],
                                     qkT[p0:p0 + HD, ki_, :], start=True, stop=True)
                full(last, ("S", h))

            def transpose_probs(h):
                pe.wait_ge(exp_ready, 2 * h + 2)
                pb = claim(pe, ("PT", h))
                for qt in range(NT):
                    for kt in range(NT):
                        a = (2 * qt + kt) * P
                        last = pe.transpose(pb[:, a:a + P], Em[:, h % 2, qt, kt * P:(kt + 1) * P], ident)
                full(last, ("PT", h))

            def times_v(h):
                if h == 0:
                    for ch in (2, 5):
                        for t in range(NT):
                            drained(pe, ("v", ch, t))
                drained(pe, ("PT", h))
                g, i = h // 8, h % 8
                for qt in range(NT):
                    pb = claim(pe, ("O", g, qt)) if i == 0 else bank[6 + qt]
                    for kt in range(NT):
                        a = (2 * qt + kt) * P
                        last = pe.matmul(pb[:, i * HD:(i + 1) * HD], pT[:, h % 2, a:a + P], vrow[:, kt, h * HD:(h + 1) * HD],
                                         start=kt == 0, stop=kt == NT - 1)
                    if i == 7:
                        full(last, ("O", g, qt))
                if i < 7:
                    last.then_inc(pv_done, 1)

            for kind, i in attention_schedule():
                if kind == "S":
                    scores_of(i)
                elif kind == "PT":
                    transpose_probs(i)
                elif kind == "PV":
                    times_v(i)

            transposes("oT", NT + 1)
            for t in range(NT):
                for g in range(2):
                    drained(pe, ("oT", t, g))
            for ch in range(2):
                w = weights1(pe, ("y", ch, 1))
                for t in range(NT):
                    rows_product(("y", ch, t), w, 512, t)
                if ch == 0:
                    ada(10)

            transposes("hT", 2 * NT + 1)
            pe.wait_ge(sk_landed, 16)
            pb = claim(pe, ("skT",))
            for s in range(2):
                last = pe.transpose(pb[:, s * P:(s + 1) * P], skrow[:, s, :], ident)
            full(last, ("skT",))
            for t in range(NT):
                for g in range(2):
                    drained(pe, ("hT", t, g))
            for job in router_schedule():
                if job[0] == "pq":
                    ch = job[1]
                    w = weights1(pe, ("pq", ch, 1))
                    for j in range(2):
                        columns_product(("pq", ch, j), w, j)
                elif job[0] == "ada":
                    ada(11)
                else:
                    _, t, g = job
                    drained(pe, ("skT",))
                    drained(pe, ("pq", g, 0))
                    drained(pe, ("pq", g, 1))
                    pb = claim(pe, job)
                    for j in range(4):
                        i = 4 * g + j
                        last = pe.matmul(pb[:, j * P:(j + 1) * P], pqT[:, i, t * P:(t + 1) * P], skT[:, i % 2, :],
                                         start=True, stop=True)
                    full(last, job)

            def peer_group(n, b, t):
                pb = [bank[banks.jobs[("peer", t, half)][0]] for half in range(2)]
                for s in range(GROUP):
                    pe.wait_ge(v_landed[s], 16 * (n + 1) if isinstance(n, int) else n * 16 + 16)
                    pe.wait_ge(diag_ready, n * GROUP + s + 1)
                    for half in range(2):
                        last = pe.matmul(pb[half][:, :], diag[:, b * GROUP + s, :], vgat[:, s, half * 512:(half + 1) * 512],
                                         start=False, stop=False, skip_group_check=True)
                    last.then_inc(v_free, 1)

            pe.wait_ge(ids_ready, 1)
            for t in range(NT):
                for half in range(2):
                    pb = claim(pe, ("peer", t, half))
                    pe.matmul(pb[:, :], zeros, hrow[:, t, half * 512:(half + 1) * 512], start=True, stop=False,
                              skip_group_check=True)
                with pe.Fori(t * NG // 4, (t + 1) * NG // 4) as m:
                    for b in range(2):
                        peer_group(m * 2 + b, b, t)
                for half in range(2):
                    pb = bank[banks.jobs[("peer", t, half)][0]]
                    full(pe.matmul(pb[:, :], zeros, hrow[:, t, half * 512:(half + 1) * 512], start=False, stop=True,
                                   skip_group_check=True), ("peer", t, half))

            with pe.Fori(0, LAYERS) as l:
                for t in range(NT):
                    pe.wait_ge(rows_ready, l * (2 * NT) + (3 * NT + 1) + t + 1)
                    for g in range(2):
                        pb = claim(pe, ("zT", t, g), l)
                        for j in range(4):
                            a = (4 * g + j) * P
                            last = pe.transpose(pb[:, j * P:(j + 1) * P], hrow[:, t, a:a + P], ident)
                        full(last, ("zT", t, g))
                for t in range(NT):
                    for g in range(2):
                        drained(pe, ("zT", t, g), l)
                w = landed2(pe, 0, l).rearrange("p (k m) -> p k m", k=KD)
                for j in range(2):
                    columns_product(("gqk", j), w, j, l)
                w = landed2(pe, 1, l).rearrange("p (k m) -> p k m", k=KD)
                pb = claim(pe, ("lr",), l)
                for k in range(KD):
                    last = pe.matmul(pb[0:LR, 0:S], w[:, k, 0:LR], hT[:, k, :], start=k == 0, stop=k == KD - 1)
                full(last, ("lr",))
                for t in range(NT):
                    rows_product(("c", t), w, CW, t, l, wcol=LR)
                drained(pe, ("lr",), l)
                pe.wait_ge(gains2_landed, l * 128 + 128)
                pb = claim(pe, ("gl",), l)
                for a in range(2):
                    last = pe.matmul(pb[:, a * S:(a + 1) * S], up[0:LR, a * P:(a + 1) * P], lrT[0:LR, :], start=True, stop=True)
                full(last, ("gl",))
                w = landed2(pe, 2, l).rearrange("p (k m) -> p k m", k=KD)
                for t in range(NT):
                    rows_product(("gv", t), w, 512, t, l)
                for t in range(NT):
                    pe.wait_ge(dve_to_pe, l * 8 + 1 + t)
                    pb = claim(pe, ("cT", t), l)
                    for j in range(3):
                        last = pe.transpose(pb[:, j * P:(j + 1) * P], crow[:, t, j * P:(j + 1) * P], ident)
                    full(last, ("cT", t))
                pe.wait_ge(dve_to_pe, l * 8 + 3)
                pb = claim(pe, ("keT",), l)
                for t in range(NT):
                    for a in range(2):
                        i = 2 * t + a
                        last = pe.transpose(pb[:, i * P:(i + 1) * P], ke[:, a, t * P:(t + 1) * P], ident)
                full(last, ("keT",))
                w = landed2(pe, 3, l)
                wq_, wkv = w[:, 0:1536].rearrange("p (k m) -> p k m", k=2), w[:, 1536:2560]
                for t in range(NT):
                    drained(pe, ("cT", t), l)
                    for hp in range(2):
                        pb = claim(pe, ("uq", t, hp), l)
                        for k in range(2):
                            last = pe.matmul(pb[:, 0:2 * QK], cqT[:, k, t * P:(t + 1) * P], wq_[:, k, hp * 2 * QK:(hp + 1) * 2 * QK],
                                             start=k == 0, stop=k == 1)
                        full(last, ("uq", t, hp))
                        pb = claim(pe, ("ukv", t, hp), l)
                        full(pe.matmul(pb[:, :], cqT[:, 2, t * P:(t + 1) * P], wkv[:, hp * 512:(hp + 1) * 512],
                                       start=True, stop=True), ("ukv", t, hp))
                for odd in range(2):
                    pb = claim(pe, ("A", odd), l)
                    p0 = GDK * odd
                    for t in range(NT):
                        for a in range(2):
                            i = 2 * t + a
                            last = pe.matmul(pb[:, i * P:(i + 1) * P], ki[p0:p0 + GDK, a, t * P:(t + 1) * P],
                                             gqT[p0:p0 + GDK, a, t * P:(t + 1) * P], start=True, stop=True)
                    full(last, ("A", odd))
                drained(pe, ("keT",), l)
                for t in range(NT):
                    drained(pe, ("gv", t), l)
                for i in range(3):
                    pb = claim(pe, ("U", i), l)
                    wait_alone(pe)
                    q0, t = GCH * (i % 2), i // 2
                    for h in range(GH):
                        p0, a = GDK * (h % 2), h // 2
                        last = pe.matmul(pb[p0:p0 + GDK, a * GDV:(a + 1) * GDV], keR[q0:q0 + GCH, t, a, p0:p0 + GDK],
                                         gv[q0:q0 + GCH, t, h * GDV:(h + 1) * GDV], start=True, stop=True)
                    full(last, ("U", i))
                for n, kind in ((4, "gg"), (5, "mg")):
                    w = landed2(pe, n, l).rearrange("p (k m) -> p k m", k=KD)
                    for t in range(NT):
                        rows_product((kind, t), w, 512, t, l)
                pe.wait_ge(dve_to_pe, l * 8 + 6)
                for odd in range(2):
                    pb = claim(pe, ("go", odd), l)
                    p0 = GDK * odd
                    for t in range(NT):
                        for a in range(2):
                            h, i = 2 * a + odd, 2 * t + a
                            last = pe.matmul(pb[:, i * GDV:(i + 1) * GDV], aT[:, t, h, :], gv[:, t, h * GDV:(h + 1) * GDV],
                                             start=True, stop=False, skip_group_check=True)
                            for cc in range(2):
                                c_ = 2 * t + cc
                                if c_ > 0:
                                    last = pe.matmul(pb[cc * GCH:(cc + 1) * GCH, i * GDV:(i + 1) * GDV],
                                                     gqT[p0:p0 + GDK, a, c_ * GCH:(c_ + 1) * GCH],
                                                     state[p0:p0 + GDK, c_ - 1, a, :],
                                                     start=False, stop=True, skip_group_check=True)
                    full(last, ("go", odd))
                for t in range(NT):
                    pe.wait_ge(dve_to_pe, l * 8 + 7 + t)
                    for kind, src in (("qnT", qrow), ("knT", kvrow)):
                        pb = claim(pe, (kind, t), l)
                        for h in range(MH):
                            last = pe.transpose(pb[:, h * P:(h + 1) * P], src[:, t, h, 0:NOPE], ident)
                        full(last, (kind, t))
                for kind, src in (("qrT", qrr), ("krT", krr)):
                    pb = claim(pe, (kind,), l)
                    for a in range(2):
                        for t in range(NT):
                            i = (2 * a + t) * P
                            last = pe.transpose(pb[:, i:i + P], src[:, t, 2 * a:2 * a + 2, :].rearrange("p a b -> p (a b)"), ident)
                    full(last, (kind,))
                for kind, i in mla_schedule():
                    if kind == "ms":
                        if i == 0:
                            for t in range(NT):
                                drained(pe, ("qnT", t), l)
                                drained(pe, ("knT", t), l)
                            drained(pe, ("qrT",), l)
                            drained(pe, ("krT",), l)
                        p0, a = ROPE * (i % 2), i // 2
                        pb = claim(pe, ("ms", i), l)
                        for qt in range(NT):
                            o, n = (0, P) if qt == 0 else (P, S)
                            pe.matmul(pb[:, o:o + n], qnT[:, i, qt * P:(qt + 1) * P], knT[:, i, 0:n], start=True, stop=False)
                            last = pe.matmul(pb[:, o:o + n], qrT[p0:p0 + ROPE, a, qt * P:(qt + 1) * P],
                                             krT[p0:p0 + ROPE, a, 0:n], start=False, stop=True)
                        full(last, ("ms", i))
                    elif kind == "mPT":
                        pe.wait_ge(m_exp, l * (2 * MH) + 2 * i + 2)
                        pb = claim(pe, ("mPT", i), l)
                        for j in range(3):
                            last = pe.transpose(pb[:, j * P:(j + 1) * P], mE[:, i % 2, j * P:(j + 1) * P], ident)
                        full(last, ("mPT", i))
                    else:
                        drained(pe, ("mPT", i), l)
                        for qt in range(NT):
                            pb = claim(pe, ("mo", qt), l) if i == 0 else bank[6 + qt]
                            for kt in range(qt + 1):
                                j = qt + kt
                                last = pe.matmul(pb[:, i * MDV:(i + 1) * MDV], mPT[:, i % 2, j * P:(j + 1) * P],
                                                 kvrow[:, kt, i, NOPE:NOPE + MDV], start=kt == 0, stop=kt == qt)
                            if i == MH - 1:
                                full(last, ("mo", qt))
                        if i < MH - 1:
                            last.then_inc(m_pv, 1)
                for t in range(NT):
                    pe.wait_ge(rows_ready, l * (2 * NT) + (3 * NT + 1) + NT + t + 1)
                    for g in range(2):
                        pb = claim(pe, ("cT2", t, g), l)
                        for j in range(4):
                            a = (4 * g + j) * P
                            last = pe.transpose(pb[:, j * P:(j + 1) * P], hrow[:, t, a:a + P], ident)
                        full(last, ("cT2", t, g))
                for t in range(NT):
                    for g in range(2):
                        drained(pe, ("cT2", t, g), l)
                for ch in range(2):
                    w = landed2(pe, 6 + ch, l).rearrange("p (k m) -> p k m", k=KD)
                    for t in range(NT):
                        rows_product(("y2", ch, t), w, 512, t, l)

        @block.vector
        def _(dve):
            chain = Chain(dve, dve_step)

            def bc(ap, *shape):
                return ap.to_broadcast([P, *shape])

            chain.step(dve.memset(eps, EPS))
            chain.wait()
            chain.link(dve.memset(ones, 1.0))
            dve.sem_inc(consts_set, 1)

            def sum_ada(i):
                n = ADA[i]
                if i >= 2:
                    await_full(dve, ("ada", i - 2))
                w = weights1(dve, ("ada", i))
                acc = ada_sum[:, i % 2, :]
                for k in range(KD):
                    before = modb[:, n // 2, (n % 2) * 512:(n % 2 + 1) * 512] if k == 0 else acc
                    ins = dve.scalar_tensor_tensor(acc, w[:, k, :], csil[:, k:k + 1], before, ALU.mult, ALU.add)
                    if k < KD - 1:
                        chain.link(ins)
                    else:
                        ins.then_inc(ada_summed, 1)

            dve.wait_ge(silu_ready, 1)
            dve.wait_ge(adab_landed, 16)
            for i in range(4):
                sum_ada(i)

            def fold_gain(s, g):
                chain.link(dve.scalar_tensor_tensor(modb[:, s, :], modb[:, s, :], 1.0, gains[:, g, :], ALU.add, ALU.mult))

            def scaled(t, gain):
                chain.step(dve.scalar_tensor_tensor(hrow[:, t, :], xrow[:, t, :], rstd[:, t:t + 1], modb[:, gain, :], ALU.mult, ALU.mult))

            def shifted_rows(t, shift):
                chain.wait()
                dve.tensor_tensor(hrow[:, t, :], hrow[:, t, :], modb[:, shift, :], ALU.add).then_inc(rows_ready, 1)

            dve.wait_ge(gains_landed, 16)
            for i in range(2):
                drained(dve, ("ada", i))
            fold_gain(1, 0)
            dve.wait_ge(rstd_ready, 1)
            for t in range(NT):
                scaled(t, 1)
            for i in range(2, 4):
                drained(dve, ("ada", i))
            for t in range(NT):
                shifted_rows(t, 0)

            dve.wait_ge(const_landed, 16 * (len(kept) + 3))
            chain.link(dve.tensor_copy(posf, posi))
            MAGIC, C1 = 1.5 * 2.0 ** 23, 6.28125
            C2 = float(np.float32(round((2 * np.pi - C1) * 2.0 ** 20) / 2.0 ** 20))
            C3 = 2 * np.pi - C1 - C2
            ang = Tm[:, 0, 0, 0:64].rearrange("p (t f) -> p t f", t=NT)
            turns = Tm[:, 0, 1, 0:128].rearrange("p (t s f) -> p t s f", t=NT, s=2)
            for t in range(NT):
                chain.step(dve.tensor_scalar(ang[:, t, :], inv_freq, posf[:, t:t + 1], None, ALU.mult))
            chain.wait()
            for s in range(2):
                chain.step(dve.tensor_scalar(turns[:, :, s, :], ang, 1 / (2 * np.pi), 0.25 * (1 - s), ALU.mult, ALU.add))
            chain.wait()
            tf = turns.rearrange("p t s f -> p (t s f)")
            chain.link(dve.tensor_scalar(tf, tf, MAGIC, None, ALU.add))
            chain.link(dve.tensor_scalar(tf, tf, MAGIC, None, ALU.subtract))
            for s in range(2):
                chain.step(dve.scalar_tensor_tensor(rope[:, :, s, :], turns[:, :, s, :], -C1, ang, ALU.mult, ALU.add))
            rf = rope[:, :, :, :].rearrange("p t s f -> p (t s f)")
            chain.wait()
            chain.link(dve.scalar_tensor_tensor(rf, tf, -C2, rf, ALU.mult, ALU.add))
            chain.link(dve.scalar_tensor_tensor(rf, tf, -C3, rf, ALU.mult, ALU.add))
            chain.link(dve.tensor_scalar(rope[:, :, 0, :], rope[:, :, 0, :], np.pi / 2, None, ALU.add))
            PI = float(np.nextafter(np.float32(np.pi), np.float32(0)))
            dve.tensor_scalar(rf, rf, PI, -PI, ALU.min, ALU.max).then_inc(ang_ready, 1)

            def neighbourhood_bias(i):
                qt, part = i // 4, i % 4
                pb = await_full(dve, ("nab", i))
                free(dve.tensor_tensor(bias[:, 2 * part:2 * part + 2, qt, :], bc(na_window[:, qt, :].unsqueeze(1), 2, S),
                                       pb[:, :].rearrange("p (a b) -> p a b", a=2), ALU.subtract), ("nab", i))

            for kind, i in qkv_schedule():
                if kind == "ada":
                    sum_ada(i)
                elif kind == "nab":
                    neighbourhood_bias(i)

            dve.wait_ge(dil_landed, 16)
            for i in range(8):
                drained(dve, ("nab", i))

            def normalize(g):
                dve.wait_ge(exp_ready, 2 * (8 * g + 8))
                chain.link(dve.reciprocal(rinv, rsum[:, :, 8 * g:8 * g + 8]))
                for qt in range(NT):
                    pb = await_full(dve, ("O", g, qt))
                    free(dve.tensor_tensor(hrow[:, qt, g * 512:(g + 1) * 512].rearrange("p (h d) -> p h d", h=8),
                                           pb[:, :].rearrange("p (h d) -> p h d", h=8),
                                           bc(rinv[:, qt, :].unsqueeze(2), 8, HD), ALU.mult), ("O", g, qt))

            for kind, h in attention_schedule():
                if kind == "S":
                    if h >= 2:
                        dve.wait_ge(exp_ready, 2 * (h - 2) + 2)
                    pb = await_full(dve, ("S", h))
                    for qt in range(NT):
                        i = 2 * (h % 2) + qt
                        ins = dve.tensor_tensor_reduce(Tm[:, h % 2, qt, :], pb[:, qt * S:(qt + 1) * S], bias[:, h, qt, :], 1.0, 3e38,
                                                       ALU.add, ALU.min, accmin[:, i:i + 1])
                        if qt == 0:
                            chain.step(ins)
                        else:
                            free(ins, ("S", h))
                    drained(dve, ("S", h))
                    chain.wait()
                    dve.sem_inc(masked_ready, 1)
                elif kind == "PT":
                    if h >= 2:
                        if (h - 2) % 8 == 7:
                            await_full(dve, ("O", (h - 2) // 8, 1))
                        else:
                            dve.wait_ge(pv_done, (h - 2) - (h - 2) // 8 + 1)
                    pb = await_full(dve, ("PT", h))
                    free(dve.tensor_copy(pT[:, h % 2, :], pb[:, :]), ("PT", h))
                elif kind == "O":
                    normalize(h)
            for g in range(2):
                for qt in range(NT):
                    drained(dve, ("O", g, qt))
            dve.sem_inc(rows_ready, 1)
            dve.wait_ge(gains_landed, 64)
            dve.wait_ge(rstd_ready, 2)
            for t in range(NT):
                chain.step(dve.scalar_tensor_tensor(hrow[:, t, 0:512], hrow[:, t, 0:512], rstd[:, 2 * t:2 * t + 1], gains[:, 2, 0:512],
                                                    ALU.mult, ALU.mult))
                chain.wait()
                dve.scalar_tensor_tensor(hrow[:, t, 512:1024], hrow[:, t, 512:1024], rstd[:, 2 * t + 1:2 * t + 2],
                                         gains[:, 2, 512:1024], ALU.mult, ALU.mult).then_inc(rows_ready, 1)

            def add_gated(job, gate, ch, t, i, ready=None):
                pb = await_full(dve, job)
                a = slice(ch * 512, (ch + 1) * 512)
                free(dve.tensor_tensor(ytmp[:, i, :], pb[:, :], modb[:, gate, a], ALU.mult), job)
                drained(dve, job)
                ins = dve.tensor_tensor(xrow[:, t, a], xrow[:, t, a], ytmp[:, i, :], ALU.add)
                if ready is None:
                    chain.link(ins)
                else:
                    ins.then_inc(ready, 1)

            sum_ada(10)
            for n in range(4, 10):
                drained(dve, ("ada", n))
            fold_gain(4, 1)
            for ch in range(2):
                for t in range(NT):
                    add_gated(("y", ch, t), 2, ch, t, t, x_ready if ch == 1 else None)
                if ch == 0:
                    sum_ada(11)
            for t in range(NT):
                dve.wait_ge(x_ready, t + 1)
                dve.wait_ge(rstd_ready, 3 + t)
                scaled(t, 4)
                shifted_rows(t, 3)

            pb = await_full(dve, ("skT",))
            free(dve.tensor_copy(skT[:, :, :].rearrange("p a b -> p (a b)"), pb[:, 0:2 * P]), ("skT",))

            def steps_done():
                chain.wait()
                if chain.turn is not None:
                    wait_alone(dve)

            def top16(units):
                steps_done()
                for src, v, i in units:
                    chain.step(dve.max(v[:, 0:8], src))
                steps_done()
                for src, v, i in units:
                    chain.step(dve.max_index(i[:, 0:8], v[:, 0:8], src))
                steps_done()
                for src, v, i in units:
                    chain.step(dve.match_replace(src, v[:, 0:8], src, -3.0e38))
                steps_done()
                for src, v, i in units:
                    chain.step(dve.max(v[:, 8:16], src))
                steps_done()
                for src, v, i in units:
                    chain.step(dve.max_index(i[:, 8:16], v[:, 8:16], src))

            def best_halves(k):
                chain.wait()
                chain.link(dve.tensor_copy(one_piece.rearrange("p a b -> p (a b)"),
                                           scores[:, bass.ds(k, 1), :, :].rearrange("p o a b -> p (o a b)")))
                top16([(one_piece[:, j, :], top_v[:, j // 2, j % 2, :], top_i[:, j // 2, j % 2, :]) for j in range(4)])

            def best_pairs(k):
                chain.wait()
                chain.link(dve.tensor_tensor(cand.rearrange("p h (a b) -> p h a b", a=TOPK),
                                             bc(top_v[:, :, 0, :].unsqueeze(3), 2, TOPK, TOPK),
                                             bc(top_v[:, :, 1, :].unsqueeze(2), 2, TOPK, TOPK), ALU.add))
                top16([(cand[:, h, :], best_v[:, h, :], best_j[:, h, :]) for h in range(2)])
                chain.wait()
                chain.step(dve.tensor_tensor(shifted, best_v, bc(best_v[:, :, 0:1], 2, TOPK), ALU.subtract))
                chain.wait()
                dve.sem_inc(softmax_shift, 1)
                chain.step(dve.tensor_scalar(best_ab[:, :, 0, :], best_j, 4, None, ALU.logical_shift_right))
                chain.step(dve.tensor_scalar(best_ab[:, :, 1, :], best_j, 15, None, ALU.bitwise_and))

            def experts_and_gates(k):
                chain.wait()
                chain.link(dve.tensor_tensor(hit, bc(best_ab.rearrange("p h s k -> p (h s) k").unsqueeze(3), 4, TOPK, TOPK),
                                             iota.unsqueeze(1).unsqueeze(1).to_broadcast([P, 4, TOPK, TOPK]), ALU.is_equal))
                chain.link(dve.tensor_tensor(hit, hit, bc(top_i.rearrange("p h s k -> p (h s) k").unsqueeze(2), 4, TOPK, TOPK), ALU.mult))
                chain.link(dve.tensor_reduce(picked.rearrange("p h s k -> p (h s k)"), hit.rearrange("p h k a -> p (h k) a"), AX.X, ALU.add))
                here = bass.ds(k * 2 * TOPK, 2 * TOPK)
                chain.link(dve.scalar_tensor_tensor(ids[:, here].rearrange("p (h k) -> p h k", h=2), picked[:, :, 0, :],
                                                    float(NKEY), picked[:, :, 1, :], ALU.mult, ALU.add))
                dve.sem_inc(ids_ready, 1)
                dve.wait_ge(gate_exp, k + 1)
                wait_alone(dve)
                chain.link(dve.tensor_reduce(gsum[:, 0:2], shifted, AX.X, ALU.add))
                chain.link(dve.reciprocal(gsum[:, 8:10], gsum[:, 0:2]))
                chain.step(dve.tensor_tensor(gates[:, here].rearrange("p (h k) -> p h k", h=2), shifted,
                                             bc(gsum[:, 8:10].unsqueeze(2), 2, TOPK), ALU.mult))

            chain.link(dve.memset(zeros, 0.0))
            await_full(dve, ("ada", 11))
            drained(dve, ("sc", 0, 0))
            best_halves(0)
            best_pairs(0)
            experts_and_gates(0)
            chain.wait()

            def peer_group(n, b, t):
                for s in range(GROUP):
                    dve.wait_ge(u_landed[s], n * 16 + 16)
                    dve.tensor_tensor_reduce(urow[:, s, :], urow[:, s, :], hrow[:, t, :], 1.0, 0.0, ALU.mult, ALU.add,
                                             a8[:, b, s:s + 1]).then_inc(u_free, 1)
                dve.wait_ge(gelu_ready, n + 1)
                dve.tensor_tensor(w8[:, b, :], g8[:, b, :], gates[:, bass.ds(n * GROUP, GROUP)], ALU.mult).then_inc(weights_ready, 1)

            dve.wait_ge(rows_ready, 3 * NT + 1)
            def piece(k, t, next_piece):
                for b in range(GPP):
                    peer_group(k * GPP + b, b % 2, t)
                    if next_piece and b < 3:
                        for job in router_schedule():
                            if job[0] == "sc" and b == 0:
                                drained(dve, job)
                        (best_halves, best_pairs, experts_and_gates)[b](k + 1)
                if next_piece:
                    chain.wait()

            half = PIECES // NT
            for t in range(NT):
                with dve.Fori(t * half, (t + 1) * half - (t == NT - 1)) as k:
                    chain.loop(k - t * half, 42)
                    piece(k, t, True)
                    chain.end_loop(half - (t == NT - 1))
            piece(PIECES - 1, NT - 1, False)
            for t in range(NT):
                for half in range(2):
                    add_gated(("peer", t, half), 5, half, t, half, x_ready if half == 1 else None)
            dve.wait_ge(fing_landed, 16)
            for t in range(NT):
                dve.wait_ge(x_ready, NT + t + 1)
                dve.wait_ge(rstd_ready, 5 + t)
                dve.scalar_tensor_tensor(xrow[:, t, :], xrow[:, t, :], rstd[:, t:t + 1], gains[:, 0, :],
                                         ALU.mult, ALU.mult).then_inc(x_ready, 1)

            chain.link(dve.memset(aT.rearrange("p a b c -> p (a b c)"), 0.0))
            XR = 2 * NT
            with dve.Fori(0, LAYERS) as l:
                chain.loop(l, 66)
                dve.wait_ge(gains2_landed, l * 128 + 128)
                dve.wait_ge(rstd_ready, l * 4 + 7)
                for t in range(NT):
                    dve.scalar_tensor_tensor(hrow[:, t, :], xrow[:, t, :], rstd[:, 4 + t:5 + t], g_in, ALU.mult, ALU.mult)\
                        .then_inc(rows_ready, 1)
                for t in range(NT):
                    drained(dve, ("c", t), l)
                dve.wait_ge(rstd_ready, l * 4 + 8)
                for t in range(NT):
                    chain.step(dve.scalar_tensor_tensor(crow[:, t, QR:QR + KVR], crow[:, t, QR:QR + KVR], rstd[:, 8 + t:9 + t], g_kv,
                                                        ALU.mult, ALU.mult))
                    chain.wait()
                    dve.scalar_tensor_tensor(crow[:, t, 0:QR], crow[:, t, 0:QR], rstd[:, 6 + t:7 + t], g_q,
                                             ALU.mult, ALU.mult).then_inc(dve_to_pe, 1)
                pb = await_full(dve, ("gl",), l)
                dve.wait_ge(exp_gate, l * 8 + 1)
                for a in range(2):
                    chain.step(dve.tensor_scalar(log_a[:, a, :], pb[:, a * S:(a + 1) * S], bgate[:, a:a + 1], 0.0, ALU.add, ALU.min))
                chain.wait()
                la = log_a.rearrange("p a b -> p (a b)")
                free(dve.tensor_tensor(la, la, gtmp.rearrange("p a b -> p (a b)"), ALU.subtract), ("gl",))
                drained(dve, ("gl",), l)
                for a in range(2):
                    chain.step(dve.tensor_tensor_scan(bcum[:, a, :], segment, log_a[:, a, :], 0.0, ALU.mult, ALU.add))
                chain.wait()
                dve.sem_inc(dve_to_act, 1)
                b4 = bcum.rearrange("p a (c i) -> p a c i", i=GCH)
                for a in range(2):
                    ins = dve.tensor_tensor(ke[:, a, :].rearrange("p (c i) -> p c i", i=GCH),
                                            bc(b4[:, a, :, GCH - 1:GCH], S // GCH, GCH), b4[:, a, :, :], ALU.subtract)
                    chain.step(ins)
                chain.wait()
                dve.sem_inc(dve_to_act, 1)
                dve.wait_ge(exp_gate, l * 8 + 3)
                for j in range(2):
                    drained(dve, ("gqk", j), l)
                chain.step(dve.tensor_tensor(gqT, gqT, eb, ALU.mult))
                chain.step(dve.tensor_tensor(ki, ki, gkT, ALU.mult))
                dve.wait_ge(exp_gate, l * 8 + 4)
                chain.step(dve.tensor_tensor(ke, ke, gkT, ALU.mult))
                chain.wait()
                dve.sem_inc(dve_to_pe, 1)
                pb = await_full(dve, ("keT",), l)
                free(dve.tensor_copy(keR.rearrange("p t a b -> p (t a b)"), pb[:, :]), ("keT",))
                for odd in range(2):
                    pb = await_full(dve, ("A", odd), l)
                    wait_alone(dve)
                    free(dve.copy_predicated(aT.rearrange("p t (a o) m -> p t a o m", o=2)[:, :, :, odd, :],
                                             same_chunk.unsqueeze(1).unsqueeze(1).to_broadcast([P, NT, 2, P]),
                                             pb[:, :].rearrange("p (t a m) -> p t a m", t=NT, a=2)), ("A", odd))
                    drained(dve, ("A", odd), l)
                    dve.sem_inc(dve_to_pe, 1)
                e4 = eb.rearrange("p a (c i) -> p a c i", i=GCH)
                pb = await_full(dve, ("U", 0), l)
                free(dve.tensor_copy(state[:, 0, :, :].rearrange("p a b -> p (a b)"), pb[:, 0:2 * GDV]), ("U", 0))
                drained(dve, ("U", 0), l)
                for i in (1, 2):
                    pb = await_full(dve, ("U", i), l)
                    for a in range(2):
                        ins = dve.scalar_tensor_tensor(state[:, i, a, :], state[:, i - 1, a, :], e4[:, a, i, GCH - 1:GCH],
                                                       pb[:, a * GDV:(a + 1) * GDV], ALU.mult, ALU.add)
                        if a == 0:
                            chain.step(ins)
                        else:
                            free(ins, ("U", i))
                    drained(dve, ("U", i), l)
                    chain.wait()
                dve.sem_inc(dve_to_pe, 1)

                dve.wait_ge(rope_ready, 1)
                dve.wait_ge(rstd_ready, l * 4 + 9)
                w4 = wide.rearrange("p (h d) -> p h d", h=MH)
                HR = ROPE // 2
                for t in range(NT):
                    for hp in range(2):
                        drained(dve, ("uq", t, hp), l)
                        drained(dve, ("ukv", t, hp), l)
                    cos, sin = rope[:, t, 0, :], rope[:, t, 1, :]
                    rq, rk = rstdh[:, 4 * t:4 * t + 4], rstdh[:, 8 + 4 * t:12 + 4 * t]
                    chain.step(dve.tensor_tensor(qrow[:, t, :, :], qrow[:, t, :, :], bc(rq.unsqueeze(2), MH, QK), ALU.mult))
                    chain.step(dve.tensor_tensor(kvrow[:, t, :, 0:NOPE], kvrow[:, t, :, 0:NOPE], bc(rk.unsqueeze(2), MH, NOPE), ALU.mult))
                    chain.step(dve.tensor_tensor(kpe[:, t, :], crow[:, t, QR + KVR:CW], g_kh[:, NOPE:QK], ALU.mult))
                    chain.wait()
                    chain.step(dve.tensor_tensor(qrow[:, t, :, :], qrow[:, t, :, :], bc(g_qh.unsqueeze(1), MH, QK), ALU.mult))
                    chain.step(dve.tensor_tensor(kvrow[:, t, :, 0:NOPE], kvrow[:, t, :, 0:NOPE], bc(g_kh[:, 0:NOPE].unsqueeze(1), MH, NOPE), ALU.mult))
                    k1, k2 = kpe[:, t, 0:HR], kpe[:, t, HR:ROPE]
                    kp = wide[:, 512:640]
                    chain.step(dve.tensor_tensor(kp[:, 0:32], k1, cos, ALU.mult))
                    chain.step(dve.tensor_tensor(kp[:, 32:64], k2, sin, ALU.mult))
                    chain.step(dve.tensor_tensor(kp[:, 64:96], k1, sin, ALU.mult))
                    chain.step(dve.tensor_tensor(kp[:, 96:128], k2, cos, ALU.mult))
                    chain.wait()
                    q1, q2 = qrow[:, t, :, NOPE:NOPE + HR], qrow[:, t, :, NOPE + HR:QK]
                    cb, sb_ = bc(cos.unsqueeze(1), MH, HR), bc(sin.unsqueeze(1), MH, HR)
                    qp = wide[:, 0:512].rearrange("p (i h f) -> p i h f", i=4, h=MH)
                    chain.step(dve.tensor_tensor(qp[:, 0, :, :], q1, cb, ALU.mult))
                    chain.step(dve.tensor_tensor(qp[:, 1, :, :], q2, sb_, ALU.mult))
                    chain.step(dve.tensor_tensor(qp[:, 2, :, :], q1, sb_, ALU.mult))
                    chain.step(dve.tensor_tensor(qp[:, 3, :, :], q2, cb, ALU.mult))
                    chain.step(dve.tensor_tensor(kpr[:, t, 0:HR], kp[:, 0:32], kp[:, 32:64], ALU.subtract))
                    chain.step(dve.tensor_tensor(kpr[:, t, HR:ROPE], kp[:, 64:96], kp[:, 96:128], ALU.add))
                    chain.wait()
                    chain.step(dve.tensor_tensor(qrr[:, t, :, 0:HR], qp[:, 0, :, :], qp[:, 1, :, :], ALU.subtract))
                    chain.step(dve.tensor_tensor(qrr[:, t, :, HR:ROPE], qp[:, 2, :, :], qp[:, 3, :, :], ALU.add))
                    chain.step(dve.tensor_tensor(krr[:, t, :, :], bc(kpr[:, t, :].unsqueeze(1), MH, ROPE), bc(rk.unsqueeze(2), MH, ROPE), ALU.mult))
                    chain.wait()
                    dve.sem_inc(dve_to_pe, 1)

                for kind, dst, before in (("gg", silu_g, 4), ("mg", silu_m, 6)):
                    for t in range(NT):
                        dve.wait_ge(exp_gate, l * 8 + before + t + 1)
                        chain.link(dve.tensor_scalar(dst[:, t, :], dst[:, t, :], 1.0, None, ALU.add))
                        chain.link(dve.reciprocal(dst[:, t, :], dst[:, t, :]))
                        pb = await_full(dve, (kind, t), l)
                        free(dve.tensor_tensor(dst[:, t, :], dst[:, t, :], pb[:, :], ALU.mult), (kind, t))
                dve.wait_ge(rstd_ready, l * 4 + 10)
                for odd in range(2):
                    pb = await_full(dve, ("go", odd), l)
                    o = hrow[:, :, 0:512].rearrange("p t (a o d) -> p t a o d", a=2, o=2)[:, :, :, odd, :]
                    r4 = ssg.rearrange("p (t a o) -> p t a o", t=NT, a=2)[:, :, :, odd].unsqueeze(3)
                    free(dve.tensor_tensor(o, pb[:, :].rearrange("p (t a d) -> p t a d", t=NT, a=2),
                                           r4.to_broadcast([P, NT, 2, GDV]), ALU.mult), ("go", odd))
                    drained(dve, ("go", odd), l)
                for t in range(NT):
                    o = hrow[:, t, 0:512].rearrange("p (h d) -> p h d", h=GH)
                    chain.link(dve.tensor_tensor(o, o, bc(g_gla.unsqueeze(1), GH, GDV), ALU.mult))
                    drained(dve, ("gg", t), l)
                    chain.step(dve.tensor_tensor(hrow[:, t, 0:512], hrow[:, t, 0:512], silu_g[:, t, :], ALU.mult))
                chain.wait()
                dve.sem_inc(gains2_used, 1)

                for kind, h in mla_schedule():
                    if kind == "ms":
                        if h >= 2:
                            dve.wait_ge(m_exp, l * (2 * MH) + 2 * (h - 2) + 2)
                        pb = await_full(dve, ("ms", h), l)
                        wait_alone(dve)
                        for qt in range(NT):
                            a, n = (0, P) if qt == 0 else (P, S)
                            i = 2 * (h % 2) + qt
                            ins = dve.tensor_tensor_reduce(mT[:, h % 2, a:a + n], pb[:, a:a + n], causal[:, a:a + n], -QK ** -0.5, 3e38,
                                                           ALU.add, ALU.min, accmin[:, i:i + 1])
                            if qt == 0:
                                chain.step(ins)
                            else:
                                free(ins, ("ms", h))
                        drained(dve, ("ms", h), l)
                        chain.wait()
                        dve.sem_inc(m_masked, 1)
                    elif kind == "mPT":
                        if h >= 2:
                            dve.wait_ge(m_pv, l * (MH - 1) + (h - 2) + 1)
                        pb = await_full(dve, ("mPT", h), l)
                        free(dve.tensor_copy(mPT[:, h % 2, :], pb[:, 0:384]), ("mPT", h))
                dve.wait_ge(m_exp, l * (2 * MH) + 2 * MH)
                chain.link(dve.reciprocal(rinv[:, :, 0:MH], rsum[:, :, 0:MH]))
                for t in range(NT):
                    pb = await_full(dve, ("mo", t), l)
                    o = hrow[:, t, 512:1024]
                    free(dve.tensor_tensor(o.rearrange("p (h d) -> p h d", h=MH), quad(pb[:, :]),
                                           bc(rinv[:, t, 0:MH].unsqueeze(2), MH, MDV), ALU.mult), ("mo", t))
                    drained(dve, ("mo", t), l)
                    drained(dve, ("mg", t), l)
                    dve.tensor_tensor(o, o, silu_m[:, t, :], ALU.mult).then_inc(rows_ready, 1)
                for ch in range(2):
                    for t in range(NT):
                        pb = await_full(dve, ("y2", ch, t), l)
                        a = slice(ch * 512, (ch + 1) * 512)
                        free(dve.tensor_tensor(xrow[:, t, a], xrow[:, t, a], pb[:, :], ALU.add), ("y2", ch, t))
                        drained(dve, ("y2", ch, t), l)
                for t in range(NT):
                    dve.sem_inc(x_ready, 1)
                chain.end_loop(LAYERS)


_INS = ["x", "c", "ada_w", "ada_b", "norm1_g", "w_in", "na_rpb", "out_norm_na_g", "out_norm_dil_g", "w_out", "norm2_g",
        "peer_wq", "peer_subkeys", "peer_u", "peer_v", "final_g", "positions_2", "norm_g_2", "w_in_2",
        "w_gla_gate_up_2", "b_gla_gate_2", "gla_norm_g_2", "mla_q_norm_g_2", "w_uq_2", "mla_kv_norm_g_2", "w_ukv_2",
        "q_head_g_2", "k_head_g_2", "w_out_2"]


def kernel(**inputs):
    import concourse.bacc as bacc
    from concourse.bass_utils import run_bass_kernel_spmd

    nc = bacc.Bacc("TRN2", target_bir_lowering=False, num_devices=1)
    arrays, args = {}, []
    for name in _INS:
        a = np.ascontiguousarray(inputs[name])
        arrays[f"in_{name}"] = a
        args.append(nc.dram_tensor(f"in_{name}", a.shape, mybir.dt.from_np(a.dtype), kind="ExternalInput").ap())
    for name, a in zip(("shape_const", "dil_bias_const"), shape_constants()):
        arrays[name] = a
        args.append(nc.dram_tensor(name, a.shape, mybir.dt.from_np(a.dtype), kind="ExternalInput").ap())
    args.append(nc.dram_tensor("out_0", (1, S, D), F32, kind="ExternalOutput").ap())
    program(nc, *args)
    r = run_bass_kernel_spmd(nc, [arrays], core_ids=[0])
    return r.results[0]["out_0"]
```

```python
from contextlib import ExitStack

import numpy as np

import concourse.bass as bass
from concourse import mybir

ALU = mybir.AluOpType
ACT = mybir.ActivationFunctionType
F32 = mybir.dt.float32
BF16 = mybir.dt.bfloat16
U32 = mybir.dt.uint32
I32 = mybir.dt.int32
AX = mybir.AxisListType

P = 128
S = 256
NT = S // P
D = 1024
KD = D // P
EPS = 1e-6
NEG = 1e30

HD = 64
NH = 16
GRID_W = 64
ROWS = S // GRID_W
RPB_R, RPB_C = 15, 31
PH = 8
NKEY = 128
TOPK = 16
SLOTS = PH * TOPK
GROUP = 8
NG = NT * SLOTS // GROUP
PIECES = NT * PH // 2
GPP = NG // PIECES

LAYERS = 2
GH, GDK, GDV, GCH = 4, 64, 128, 64
GATE_TEMP = 16.0
MH, NOPE, ROPE, MDV = 4, 128, 64, 128
QK = NOPE + ROPE
QR, KVR = 256, 128
D_IN = 2512
LR = 16
O_V, O_LR, O_GG, O_C, O_MG = 512, 1024, 1040, 1552, 2000
CW = QR + KVR + ROPE

CONST = {}
_at = 0
for _name, _w in (("ident", 128), ("flip", 128), ("na_window", 512), ("segment", 256), ("same_chunk", 128),
                  ("causal", 384), ("inv_freq", 32), ("iota", 16)):
    CONST[_name] = (_at, _at + _w)
    _at += _w
NCONST = _at


def shape_constants():
    c = np.zeros((P, NCONST), np.float32)

    def put(name, value):
        a, b = CONST[name]
        c[:, a:b] = value

    p = np.arange(P)
    put("ident", np.eye(P))
    put("flip", (p[:, None] // 64 == p[None, :] // 64) & (p[:, None] % 64 == 63 - p[None, :] % 64))
    q = (np.arange(NT)[None, :, None] * P + p[:, None, None])
    k = np.arange(S)[None, None, :]
    c0 = np.clip(q % GRID_W - 8, 0, GRID_W - 16)
    inside = (k % GRID_W >= c0) & (k % GRID_W < c0 + 16)
    put("na_window", np.where(inside, 0.0, NEG).reshape(P, -1))
    put("segment", np.broadcast_to((np.arange(S) % GCH != 0), (P, S)))
    put("same_chunk", (p[:, None] // GCH == p[None, :] // GCH) & (p[:, None] <= p[None, :]))
    tri = np.where(p[None, :] <= p[:, None], 0.0, -NEG)
    put("causal", np.concatenate([tri, np.zeros((P, P)), tri], 1))
    put("inv_freq", np.broadcast_to(10000.0 ** (-np.arange(0, ROPE, 2) / ROPE), (P, ROPE // 2)))
    put("iota", np.broadcast_to(np.arange(16), (P, 16)))
    d = np.abs(q - k)
    count = (d <= 64).astype(int) + (d % 4 == 0) + (d % 16 == 0)
    logc = np.log(np.maximum(count, 1).astype(np.float64))
    slopes = 2.0 ** (-(np.arange(8) + 1.0))
    dil = slopes[None, :, None, None] * d[:, None] - logc[:, None]
    dil = np.where(count[:, None] > 0, dil, NEG).astype(np.float32)
    return c, np.ascontiguousarray(dil.reshape(P, -1))


class Banks:

    def __init__(self):
        self.uses = [0] * 8
        self.jobs = {}
        self.next = 0
        self.base = None

    def plan(self, name, bank=None):
        if bank is None:
            bank, self.next = self.next, (self.next + 1) % 6
        self.jobs[name] = (bank, self.uses[bank], self.base is not None)
        self.uses[bank] += 1

    def start_layer(self):
        self.base = list(self.uses)

    def end_layer(self):
        self.per_layer = [u - b for u, b in zip(self.uses, self.base)]

    def before(self, name, layer):
        bank, n, in_layer = self.jobs[name]
        return bank, (layer * self.per_layer[bank] + n if in_layer else n)


ADA = [2, 3, 0, 1] + list(range(4, 12))


def qkv_schedule():
    out, i = [], 4
    for n in (0, 1, 3, 4, 2, 5):
        out.append(("v" if n in (2, 5) else "qk", n))
        out.append(("ada", i))
        i += 1
        if n in (3, 4):
            out += [("nab", j) for j in range(4 * (n - 3), 4 * (n - 3) + 4)]
    return out


def router_schedule():
    return [("pq", 0), ("sc", 0, 0), ("pq", 1), ("pq", 2), ("pq", 3)] + [
        ("sc", t, ch) for ch in range(4) for t in range(NT) if (t, ch) != (0, 0)]


def attention_schedule():
    out = []
    for h in range(NH + 2):
        if h < NH:
            out.append(("S", h))
            if h % 2 == 0:
                out.append(("sum ada", h // 2))
        if 1 <= h <= NH:
            out.append(("PT", h - 1))
        if h >= 2:
            out.append(("PV", h - 2))
            if (h - 2) % 8 == 7:
                out.append(("O", (h - 2) // 8))
        if h == 11:
            out.append(("norm", 0))
        if h == 12:
            out.append(("scale", 0))
        if h == 13:
            out.append(("oT", 0))
    return out


def y_schedule():
    out = [("half", ch, t, 0) for ch in range(2) for t in range(NT)]
    out += [("ada", 10), ("oT", 1)]
    for t in range(NT):
        out += [("half", ch, t, 1) for ch in range(2)]
    return out


def mla_schedule():
    out = []
    for h in range(MH + 2):
        if h < MH:
            out.append(("ms", h))
        if 1 <= h <= MH:
            out.append(("mPT", h - 1))
        if h >= 2:
            out.append(("mPV", h - 2))
        if h == MH:
            out.append(("cT2", 0))
    return out


def plan_banks():
    b = Banks()
    b.plan(("cols",))
    for t in range(NT):
        for g in range(2):
            b.plan(("xT", t, g))
    for i in range(2):
        b.plan(("adac", i))
    for kind, n in qkv_schedule():
        if kind in ("qk", "v"):
            for j in range(2):
                b.plan((kind, n, j))
        else:
            b.plan((kind, n))
    for kind, i in attention_schedule():
        if kind == "PV":
            if i % 8 == 0:
                for qt in range(NT):
                    b.plan(("O", i // 8, qt), 6 + qt)
        elif kind == "oT":
            for t in range(NT):
                b.plan(("oT", t, i))
        elif kind in ("S", "PT"):
            b.plan((kind, i))
    for job in y_schedule():
        if job[0] == "half" and job[3] == 0:
            b.plan(("y",) + job[1:3])
        elif job[0] == "ada":
            b.plan(job)
        elif job[0] == "oT":
            for t in range(NT):
                b.plan(("oT", t, job[1]), 6 + t)
    for job in router_schedule():
        if job[0] == "pq":
            if job[1] == 0:
                for t in range(NT):
                    for g in range(2):
                        b.plan(("hT", t, g), None if t == 0 else 6 + g)
                    if t == 0:
                        for j in range(2):
                            b.plan(job + (j,))
                b.plan(("ada", 11))
                b.plan(("skT",))
            else:
                for j in range(2):
                    b.plan(job + (j,))
        else:
            b.plan(job)
    for t in range(NT):
        for half in range(2):
            b.plan(("peer", t, half), 6 + half if t == 0 else 4 + half)
    b.next = 0
    b.start_layer()
    for t in range(NT):
        for g in range(2):
            b.plan(("zT", t, g))
        if t == 0:
            for j in range(2):
                b.plan(("gqk", j))
        b.plan(("c", t))
    b.plan(("lr",))
    b.plan(("gv", 0))
    for t in range(NT):
        b.plan(("cT", t))
    b.plan(("gl",))
    for t in range(NT):
        for hp in range(2):
            b.plan(("uq", t, hp))
            b.plan(("ukv", t, hp))
    b.plan(("gv", 1))
    b.plan(("keT",))
    for odd in range(2):
        b.plan(("A", odd), 6 + odd)
    for i in range(3):
        b.plan(("U", i))
    for t in range(NT):
        b.plan(("gg", t))
    for t in range(NT):
        b.plan(("mg", t))
    for odd in range(2):
        b.plan(("go", odd), 6 + odd)
    for t in range(NT):
        b.plan(("qnT", t))
        b.plan(("knT", t))
    b.plan(("qrT",))
    b.plan(("krT",))
    for kind, i in mla_schedule():
        if kind == "mPV":
            if i == 0:
                for qt in range(NT):
                    b.plan(("mo", qt), 6 + qt)
        elif kind == "cT2":
            for t in range(NT):
                b.plan(("cT2", t, 0))
        else:
            b.plan((kind, i))
    for t in range(NT):
        b.plan(("cT2", t, 1))
    for t in range(NT):
        for ch in range(2):
            b.plan(("y2", ch, t))
    b.end_layer()
    return b


class Chain:

    def __init__(self, eng, sem):
        self.eng, self.sem, self.n, self.turn = eng, sem, 0, None

    def step(self, ins):
        ins.then_inc(self.sem, 1)
        self.n += 1

    def wait(self):
        self.eng.wait_ge(self.sem, self.n if self.turn is None else self.turn * self.per + self.n)

    def link(self, ins):
        self.step(ins)
        self.wait()

    def loop(self, turn, per):
        self.turn, self.per, self.from_ = turn, per, self.n

    def end_loop(self, turns):
        assert self.n - self.from_ == self.per, (self.n - self.from_, self.per)
        self.n, self.turn = self.from_ + self.per * turns, None


def program(nc, x, c, ada_w, ada_b, norm1_g, w_in, na_rpb, out_norm_na_g, out_norm_dil_g, w_out, norm2_g,
            peer_wq, peer_subkeys, peer_u, peer_v, final_g, positions_2, norm_g_2, w_in_2, w_gla_gate_up_2,
            b_gla_gate_2, gla_norm_g_2, mla_q_norm_g_2, w_uq_2, mla_kv_norm_g_2, w_ukv_2, q_head_g_2,
            k_head_g_2, w_out_2, shape_const, dil_bias_const, out):
    ctx = ExitStack()
    with ctx:
        def sb(name, shape, dt=F32):
            return ctx.enter_context(nc.sbuf_tensor(name, shape, dt))

        def sem(name):
            return ctx.enter_context(nc.semaphore(name))

        banks = plan_banks()
        bank = [ctx.enter_context(nc.psum_tensor(f"bank{i}", [P, 512], F32)) for i in range(8)]

        wring = sb("wring", [P, 4, 4096])
        xrow = sb("xrow", [P, NT, D])
        hrow = sb("hrow", [P, NT, D])
        hT = sb("hT", [P, KD, S])
        modb = sb("modb", [P, 6, D])
        gains = sb("gains", [P, 3, D])
        R = sb("R", [P, 16384])
        vec_rows = sb("vec_rows", [24, P])
        vec = sb("vec", [P, 24])
        gain1 = sb("gain1", [P, KD])
        shift1 = sb("shift1", [P, KD])
        start = sb("start", [P, 640])
        pT = sb("pT", [P, 2, 512])
        const = sb("const", [P, NCONST - 640])
        skrow = sb("skrow", [P, 2, P])
        skT = sb("skT", [P, 2, P])
        ids = sb("ids", [P, NT * SLOTS], U32)
        gates = sb("gates", [P, NT * SLOTS])
        rope = sb("rope", [P, NT, 2, ROPE // 2])
        small = sb("small", [P, 256])

        def region(at, *shape, dt=F32):
            n = int(np.prod(shape))
            v = R[:, at:at + n] if dt == F32 else R[:, at:at + n].bitcast(dt)
            names = "abcd"[:len(shape)]
            return v if len(shape) == 1 else v.rearrange(
                f"p ({' '.join(names)}) -> p {' '.join(names)}", **dict(zip(names[1:], shape[1:])))

        kept = ["ident", "segment", "same_chunk", "causal", "inv_freq", "iota"]
        at_const, where = 0, {}
        for name in kept:
            a, b = CONST[name]
            where[name] = const[:, at_const:at_const + b - a]
            at_const += b - a
        ident, segment, causal, inv_freq, iota = (where[n] for n in ("ident", "segment", "causal", "inv_freq", "iota"))
        same_chunk = where["same_chunk"].bitcast(U32)

        first_sums = region(0, 4, 2, 512)
        ada_sum = modb[:, 0, :].rearrange("p (b n) -> p b n", b=2)
        junk1 = modb[:, 1, 0:512].bitcast(BF16)
        bias = region(0, NH, NT, S)
        qkT = region(8192, 16, S)
        vrow = region(12288, NT, D)
        flip = start[:, 0:P]
        na_window = start[:, P:640].rearrange("p (t s) -> p t s", t=NT)
        na_raw = [hrow[:, :, :].rearrange("p a b -> p (a b)").rearrange("p (h s) -> p h s", h=8), region(14336, 8, S)]
        Tm = region(14336, 2, NT, S)
        Em = region(15360, 2, NT, S)
        junk = R[:, 15872:16384].bitcast(BF16)
        pqT = region(0, 16, S)
        scores = region(4096, PIECES, 4, NKEY)
        one_piece = region(8192, 4, NKEY)
        cand = region(8704, 2, TOPK * TOPK)
        hit = region(9216, 4, TOPK, TOPK)
        top_v = region(10240, 2, 2, TOPK)
        top_i = region(10304, 2, 2, TOPK, dt=U32)
        best_v = region(10368, 2, TOPK)
        best_j = region(10400, 2, TOPK, dt=U32)
        best_ab = region(10432, 2, 2, TOPK, dt=U32)
        picked = region(10496, 2, 2, TOPK)
        shifted = region(10560, 2, TOPK)
        ytmp = region(14336, 2, 512)
        urow = wring[:, 0:2, :].rearrange("p a (b d) -> p (a b) d", d=D)
        vgat = wring[:, 2:4, :].rearrange("p a (b d) -> p (a b) d", d=D)
        diag = hT[:, :, :].rearrange("p a b -> p (a b)").rearrange("p (s m) -> p s m", m=P)
        zeros = pT[:, 0, 0:P]
        ones = gates[:, 0:P]

        M = modb[:, :, :].rearrange("p a b -> p (a b)")

        def mod_region(at, *shape):
            n = int(np.prod(shape))
            names = "abcd"[:len(shape)]
            return M[:, at:at + n].rearrange(
                f"p ({' '.join(names)}) -> p {' '.join(names)}", **dict(zip(names[1:], shape[1:])))

        gqT = mod_region(0, 2, S)
        gkT = mod_region(512, 2, S)
        log_a = mod_region(1024, 2, S)
        gtmp = mod_region(1536, 2, S)
        bcum = mod_region(2048, 2, S)
        eb = mod_region(2560, 2, S)
        ki = mod_region(3072, 2, S)
        ke = mod_region(3584, 2, S)
        aT = mod_region(4096, NT, GH, P)
        keR = mod_region(5120, NT, 2, P)
        up = pT[:, :, 384:512]
        lrT = mod_region(5632, 256)
        gv = region(0, NT, 512)
        state = region(1024, 3, 2, GDV)
        crow = region(1792, NT, CW)
        cqT = region(2688, 3, S)
        qrow = region(3456, NT, MH, QK)
        kvrow = region(4992, NT, MH, NOPE + MDV)
        qrr = region(7040, NT, MH, ROPE)
        krr = region(7552, NT, MH, ROPE)
        qnT = region(8064, MH, S)
        knT = region(9088, MH, S)
        qrT = region(10112, 2, S)
        krT = region(10624, 2, S)
        mT = region(11136, 2, 384)
        mE = region(11904, 2, 384)
        mPT = pT[:, :, 0:384]
        silu_g = region(12672, NT, 512)
        silu_m = region(13696, NT, 512)
        wide = region(14720, 768)
        kpe = region(15488, NT, ROPE)
        kpr = region(15616, NT, ROPE)
        gains2 = gains[:, 1:3, :].rearrange("p a b -> p (a b)")
        g_in, g_gla, g_q, g_kv = gains2[:, 0:1024], gains2[:, 1024:1152], gains2[:, 1152:1408], gains2[:, 1408:1536]
        g_qh, g_kh = gains2[:, 1536:1728], gains2[:, 1728:1920]

        def col(a, n=1):
            return small[:, a:a + n]

        cT, csil = col(0, 8), col(8, 8)
        ss, rstd = col(16, 16), col(32, 16)
        accmin = col(48, 4)
        rsum = small[:, 56:88].rearrange("p (t h) -> p t h", t=NT)
        rinv = small[:, 88:104].rearrange("p (t h) -> p t h", t=NT)
        bgate = col(104, 2)
        posf = col(106, 2)
        posi = small[:, 108:110].bitcast(I32)
        a8 = small[:, 112:128].rearrange("p (b s) -> p b s", b=2)
        g8 = small[:, 128:144].rearrange("p (b s) -> p b s", b=2)
        w8 = small[:, 144:160].rearrange("p (b s) -> p b s", b=2)
        idu = small[:, 160:176].bitcast(U32).rearrange("p (b s) -> p b s", b=2)
        idv = small[:, 176:192].bitcast(U32).rearrange("p (b s) -> p b s", b=2)
        decay = small[:, 192:200].rearrange("p (a c) -> p a c", a=2)
        ssh, rstdh = col(200, 24), col(224, 24)
        eps = col(248)
        minus_half = col(249)
        gsum = small[:, 208:224]
        ssg = col(240, 8)

        w_landed = [sem(f"w_landed{i}") for i in range(4)]
        bank_full = [sem(f"bank_full{i}") for i in range(8)]
        bank_free = [sem(f"bank_free{i}") for i in range(8)]
        x_landed, c_landed, const_landed, gains_landed = sem("x_landed"), sem("c_landed"), sem("const_landed"), sem("gains_landed")
        ident_landed, vec_landed = sem("ident_landed"), sem("vec_landed")
        first_half_landed = [sem(f"first_half_landed{i}") for i in range(4)]
        hT_modulated = sem("hT_modulated")
        squares_ready = sem("squares_ready")
        inv_rms_ready = sem("inv_rms_ready")
        heads_ready = sem("heads_ready")
        adab_landed, rpb_landed, dil_landed, sk_landed = sem("adab_landed"), sem("rpb_landed"), sem("dil_landed"), sem("sk_landed")
        fing_landed, gains2_landed = sem("fing_landed"), sem("gains2_landed")
        act_step, dve_step, pool_step = sem("act_step"), sem("dve_step"), sem("pool_step")
        consts_set = sem("consts_set")
        silu_ready = sem("silu_ready")
        ada_summed = sem("ada_summed")
        ang_ready = sem("ang_ready")
        rope_ready = sem("rope_ready")
        rstd_ready = sem("rstd_ready")
        rows_ready = sem("rows_ready")
        masked_ready = sem("masked_ready")
        exp_ready = sem("exp_ready")
        pv_done = sem("pv_done")
        x_ready = sem("x_ready")
        softmax_shift = sem("softmax_shift")
        gate_exp = sem("gate_exp")
        ids_ready = sem("ids_ready")
        u_landed = [sem(f"u_landed{i}") for i in range(GROUP)]
        v_landed = [sem(f"v_landed{i}") for i in range(GROUP)]
        u_free = sem("u_free")
        gelu_ready = sem("gelu_ready")
        weights_ready = sem("weights_ready")
        diag_ready = sem("diag_ready")
        v_free = sem("v_free")
        exp_gate = sem("exp_gate")
        dve_to_act = sem("dve_to_act")
        dve_to_pe = sem("dve_to_pe")
        m_masked, m_exp, m_pv = sem("m_masked"), sem("m_exp"), sem("m_pv")
        gains2_used = sem("gains2_used")
        linear_out_ready = sem("linear_out_ready")
        waits_passed = sem("waits_passed")
        out_done = sem("out_done")

        def claim(pe, job, l=None):
            b, n = banks.before(job, l)
            if l is not None or n > 0:
                pe.wait_ge(bank_free[b], n)
            return bank[b]

        def full(ins, job):
            ins.then_inc(bank_full[banks.jobs[job][0]], 1)

        def await_full(eng, job, l=None):
            b, n = banks.before(job, l)
            eng.wait_ge(bank_full[b], n + 1)
            return bank[b]

        def free(ins, job):
            ins.then_inc(bank_free[banks.jobs[job][0]], 1)

        def drained(eng, job, l=None):
            b, n = banks.before(job, l)
            eng.wait_ge(bank_free[b], n + 1)

        def wait_alone(eng):
            eng.sem_inc(waits_passed, 1)

        def quad(ap):
            return ap.rearrange("p (a b) -> p a b", a=4)

        def chunk_dram(w, l, a, b):
            return w[l, :, a:b].rearrange("(k p) n -> p k n", p=P)

        W1 = [(ada_w, 512 * ADA[i], ("ada", i)) for i in range(4)]
        for kind, n in qkv_schedule():
            if kind == "ada":
                W1.append((ada_w, 512 * ADA[n], ("ada", n)))
            elif kind != "nab":
                W1.append((w_in, 512 * n, (kind, n, 1)))
        W1 += [(ada_w, 512 * ADA[10], ("ada", 10))]
        W1 += [(w_out, 512 * n, ("y", n, 1)) for n in range(2)]
        W1 += [(ada_w, 512 * ADA[11], ("ada", 11))]
        W1 += [(peer_wq, 512 * n, ("pq", n, 1)) for n in range(4)]
        W1_AT = {job: n for n, (_, _, job) in enumerate(W1)}
        CPL = 8
        W1_USES = len(W1) // 4

        def slot512(n):
            return wring[:, n % 4, :].rearrange("p (k m) -> p k m", k=KD)

        def weights1(pe, job):
            n = W1_AT[job]
            pe.wait_ge(w_landed[n % 4], 16 * (n // 4 + 1))
            return slot512(n)

        DMAS2 = [1, 2, 1, 2, 1, 1, 1, 1]

        def landed2(eng, n, l):
            s = n % 4
            per = 16 * (DMAS2[s] + DMAS2[s + 4])
            here = 16 * sum(DMAS2[j] for j in range(s, n + 1, 4))
            eng.wait_ge(w_landed[s], l * per + 16 * W1_USES + here)
            return wring[:, s, :]

        LAST2 = [("gqk", 1), ("lr",), ("gv", 1), ("ukv", 1, 1), ("gg", 1), ("mg", 1), ("y2", 0, 1), ("y2", 1, 1)]

        block = ctx.enter_context(nc.Block())

        @block.sync
        def _(sp):
            for n, (w, a, _) in enumerate(W1):
                if n >= 4:
                    before = W1[n - 4][2]
                    if before[0] == "ada":
                        sp.wait_ge(ada_summed, before[1] + 1)
                    else:
                        await_full(sp, before)
                src, k = chunk_dram(w, 0, a, a + 512), 0
                if n < 4:
                    k = KD // 2
                    sp.dma_start(slot512(n)[:, 0:k, :], src[:, 0:k, :]).then_inc(first_half_landed[n], 16)
                sp.dma_start(slot512(n)[:, k:, :], src[:, k:, :]).then_inc(w_landed[n % 4], 16)

            def layer_chunk(n, l):
                dst, s = wring[:, n % 4, :], w_landed[n % 4]
                if n == 3:
                    sp.dma_start(dst[:, 0:1536].rearrange("p (k m) -> p k m", k=2),
                                 w_uq_2[l].rearrange("(k p) n -> p k n", p=P)).then_inc(s, 16)
                    sp.dma_start(dst[:, 1536:2560], w_ukv_2[l]).then_inc(s, 16)
                elif n == 1:
                    d = dst.rearrange("p (k m) -> p k m", k=KD)
                    sp.dma_start(d[:, :, 0:LR], chunk_dram(w_in_2, l, O_LR, O_LR + LR)).then_inc(s, 16)
                    sp.dma_start(d[:, :, LR:LR + CW], chunk_dram(w_in_2, l, O_C, O_C + CW)).then_inc(s, 16)
                else:
                    w, a = {0: (w_in_2, 0), 2: (w_in_2, O_V), 4: (w_in_2, O_GG), 5: (w_in_2, O_MG),
                            6: (w_out_2, 0), 7: (w_out_2, 512)}[n]
                    sp.dma_start(dst.rearrange("p (k m) -> p k m", k=KD), chunk_dram(w, l, a, a + 512)).then_inc(s, 16)

            sp.wait_ge(u_free, NG * GROUP)
            sp.wait_ge(v_free, NG * GROUP - 6)
            for n in range(4):
                if n == 2:
                    sp.wait_ge(v_free, NG * GROUP)
                layer_chunk(n, 0)
            with sp.Fori(0, LAYERS - 1) as l:
                for n in range(4, CPL):
                    await_full(sp, LAST2[n - 4], l)
                    layer_chunk(n, l)
                for n in range(4):
                    await_full(sp, LAST2[n + 4], l)
                    layer_chunk(n, l + 1)
            for n in range(4, CPL):
                await_full(sp, LAST2[n - 4], LAYERS - 1)
                layer_chunk(n, LAYERS - 1)
            sp.wait_ge(x_ready, NT * (3 + LAYERS))
            sp.dma_start(out[0].rearrange("(t p) d -> p t d", p=P), xrow[:, :, :]).then_inc(out_done, 16)
            sp.wait_ge(out_done, 16)

        @block.gpsimd
        def _(pool):
            chain = Chain(pool, pool_step)

            chain.step(pool.memset(minus_half, -0.5))
            chain.link(pool.memset(modb[:, 2:6, :].rearrange("p a b -> p (a b)"), 0.0))
            pool.dma_start(modb[0:1, 2:6, :].rearrange("p a b -> p (a b)"), ada_b[:, 2 * D:6 * D]).then_inc(adab_landed, 16)

            pool.wait_ge(ang_ready, 1)
            pool.wait_ge(rstd_ready, 1)
            for t in range(NT):
                for g in range(2):
                    drained(pool, ("xT", t, g))
            for r in range(ROWS):
                pb, qt = 64 * (r % 2), r // 2
                for kr in range(ROWS):
                    src = bass.AP(na_rpb.tensor, (kr - r + 7) * RPB_C - 48, [[1, 64], [RPB_R * RPB_C, 8], [1, 64]])
                    pool.dma_start(na_raw[qt][pb:pb + 64, :, kr * GRID_W:(kr + 1) * GRID_W], src).then_inc(rpb_landed, 16)
            for i in range(2):
                await_full(pool, ("adac", i))
            pool.dma_start(gains[:, 0, :], final_g.partition_broadcast(P)).then_inc(fing_landed, 16)
            pool.dma_start(bias[:, 8:16, :, :].rearrange("p h t s -> p (h t s)"), dil_bias_const).then_inc(dil_landed, 16)
            pool.dma_start(gains[:, 2, 0:512], out_norm_na_g[0].partition_broadcast(P)).then_inc(gains_landed, 16)
            pool.dma_start(gains[:, 2, 512:1024], out_norm_dil_g[0].partition_broadcast(P)).then_inc(gains_landed, 16)
            pool.dma_start(gains[:, 1, :], norm2_g[0].partition_broadcast(P)).then_inc(gains_landed, 16)
            pool.dma_start(skrow[:, :, :], peer_subkeys[0].rearrange("s n d -> n s d")).then_inc(sk_landed, 16)

            def load_gains(l):
                at = 0
                for g, n in ((norm_g_2, 1024), (gla_norm_g_2, 128), (mla_q_norm_g_2, 256), (mla_kv_norm_g_2, 128),
                             (q_head_g_2, QK), (k_head_g_2, QK)):
                    pool.dma_start(gains2[:, at:at + n], g[l].partition_broadcast(P)).then_inc(gains2_landed, 16)
                    at += n
                pool.dma_start(bgate, b_gla_gate_2[l].rearrange("(a p) -> p a", p=P), allow_slow_non_contiguous=True).then_inc(gains2_landed, 16)
                pool.dma_start(up[0:LR, :, :], w_gla_gate_up_2[l].rearrange("k (a m) -> k a m", a=2)).then_inc(gains2_landed, 16)

            def gather(dst, table, index, landed):
                wait_alone(pool)
                pool.indirect_dma_start(dst, None, table, bass.IndirectOffsetOnAxis(index, 0)).then_inc(landed, 16)

            def stage_ids(dst, n):
                wait_alone(pool)
                chain.link(pool.tensor_copy(dst, ids[:, bass.ds(n * GROUP, GROUP)] if not isinstance(n, int)
                                            else ids[:, n * GROUP:(n + 1) * GROUP]))

            def u_rows(n, s, b, first=False):
                if not first:
                    pool.wait_ge(u_free, (n - 1) * GROUP + s + 1)
                gather(urow[:, s, :], peer_u[0], idu[:, b, s:s + 1], u_landed[s])

            def v_rows(n, s, b, first=False):
                if not first:
                    pool.wait_ge(v_free, (n - 1) * GROUP + s + 1)
                gather(vgat[:, s, :], peer_v[0], idv[:, b, s:s + 1], v_landed[s])

            def piece(n, k, first=False, last=False):
                for b in range(GPP):
                    more = not (last and b == GPP - 1)
                    if more:
                        if b == GPP - 1:
                            pool.wait_ge(ids_ready, k + 2)
                        stage_ids(idu[:, (b + 1) % 2, :], n + b + 1)
                    stage_ids(idv[:, b % 2, :], n + b)
                    for s in range(GROUP):
                        if more:
                            u_rows(n + b + 1, s, (b + 1) % 2)
                        if first and b == 0 and s % (GROUP // 2) == 0:
                            await_full(pool, ("pq", 2 + s // (GROUP // 2), 1))
                        v_rows(n + b, s, b % 2, first and b == 0)

            def inverse_rms(n, *norms):
                pool.wait_ge(squares_ready, n)
                wait_alone(pool)
                for sums, _, dim in norms:
                    chain.step(pool.tensor_scalar(sums, sums, 1.0 / dim, EPS, ALU.mult, ALU.add))
                chain.wait()
                wait_alone(pool)
                for sums, dst, _ in norms:
                    chain.step(pool.tensor_tensor(dst, sums, minus_half.to_broadcast([P, sums.shape[-1]]), ALU.pow))
                chain.wait()
                pool.sem_inc(inv_rms_ready, 1)

            for g in range(2):
                inverse_rms(g + 1, (ss[:, 2 * g:2 * g + 2], rstd[:, 2 * g:2 * g + 2], 512))
            for t in range(NT):
                inverse_rms(3 + t, (ss[:, t:t + 1], rstd[:, t:t + 1], D))
            pool.wait_ge(rows_ready, 4 * NT)
            load_gains(0)

            pool.wait_ge(ids_ready, 1)
            await_full(pool, ("pq", 1, 1))
            stage_ids(idu[:, 0, :], 0)
            for s in range(GROUP):
                u_rows(0, s, 0, first=True)
            piece(0, 0, first=True)
            with pool.Fori(1, PIECES - 1) as k:
                chain.loop(k - 1, 2 * GPP)
                piece(k * GPP, k)
                chain.end_loop(PIECES - 2)
            piece(NG - GPP, PIECES - 1, last=True)

            inverse_rms(5, (ss[:, 1:2], rstd[:, 1:2], D))
            def layer(l, last=False):
                inverse_rms(l * 5 + 6, (ss[:, 5:6], rstd[:, 5:6], D))
                inverse_rms(l * 5 + 7, (ss[:, 6:8], rstd[:, 6:8], QR), (ss[:, 8:10], rstd[:, 8:10], KVR))
                inverse_rms(l * 5 + 8, (ssh[:, 0:16], rstdh[:, 0:16], QK))
                inverse_rms(l * 5 + 9, (ssg, ssg, GDV))
                if not last:
                    pool.wait_ge(gains2_used, l + 1)
                    load_gains(l + 1)
                    inverse_rms(l * 5 + 10, (ss[:, 4:5], rstd[:, 4:5], D))

            for l in range(LAYERS):
                layer(l, l == LAYERS - 1)

        @block.scalar
        def _(act):
            chain = Chain(act, act_step)

            act.dma_start(cT, c[0].rearrange("(k p) -> p k", p=P), allow_slow_non_contiguous=True).then_inc(c_landed, 16)
            a, b = CONST["ident"]
            act.dma_start(ident, shape_const[:, a:b]).then_inc(ident_landed, 16)
            act.dma_start(xrow[:, :, :], x[0].rearrange("(t p) d -> p t d", p=P)).then_inc(x_landed, 16)
            act.dma_start(vec_rows[0:16, :], ada_b[0, 0:2 * D].rearrange("(k p) -> k p", p=P)).then_inc(vec_landed, 16)
            act.dma_start(vec_rows[16:24, :], norm1_g[0].rearrange("(k p) -> k p", p=P)).then_inc(vec_landed, 16)
            for name in kept[1:]:
                a, b = CONST[name]
                act.dma_start(where[name], shape_const[:, a:b]).then_inc(const_landed, 16)
            a, b = CONST["flip"]
            act.dma_start(flip, shape_const[:, a:b]).then_inc(const_landed, 16)
            a, b = CONST["na_window"]
            act.dma_start(na_window.rearrange("p t s -> p (t s)"), shape_const[:, a:b]).then_inc(const_landed, 16)
            act.dma_start(posi, positions_2[0].rearrange("(t p) -> p t", p=P), allow_slow_non_contiguous=True).then_inc(const_landed, 16)

            def squares(srcs, cols, junk=junk1):
                for src, i in zip(srcs, cols):
                    w = int(np.prod(src.shape[1:]))
                    chain.link(act.activation(junk[:, 0:w], src, ACT.Square, accum_out=ss[:, i:i + 1]))
                act.sem_inc(squares_ready, 1)

            def rms(srcs, dim, cols, junk=junk1):
                for src, i in zip(srcs, cols):
                    w = int(np.prod(src.shape[1:]))
                    chain.link(act.activation(junk[:, 0:w], src, ACT.Square, accum_out=ss[:, i:i + 1]))
                a, b = cols[0], cols[-1] + 1
                chain.link(act.activation(ss[:, a:b], ss[:, a:b], ACT.Ln, scale=1.0 / dim, bias=eps))
                act.activation(rstd[:, a:b], ss[:, a:b], ACT.Exp, scale=-0.5).then_inc(rstd_ready, 1)

            act.wait_ge(c_landed, 16)
            act.activation(csil, cT, ACT.Silu).then_inc(silu_ready, 1)
            act.wait_ge(x_landed, 16)
            act.wait_ge(consts_set, 1)
            rms([xrow[:, t, :] for t in range(NT)], D, [0, 1], junk)

            def evac_T(kind, l=None, tiles=range(NT), groups=range(2)):
                for t in tiles:
                    for g in groups:
                        pb = await_full(act, (kind, t, g), l)
                        free(act.activation(hT[:, 4 * g:4 * g + 4, t * P:(t + 1) * P], quad(pb[:, :]), ACT.Copy), (kind, t, g))

            def ada_out(i):
                n = ADA[i]
                pb = await_full(act, ("ada", i))
                free(act.activation(modb[:, n // 2, (n % 2) * 512:(n % 2 + 1) * 512], pb[:, :], ACT.Copy), ("ada", i))

            evac_T("xT")
            act.wait_ge(ang_ready, 1)
            act.activation(rope[:, :, :, :].rearrange("p t s f -> p (t s f)"),
                           rope[:, :, :, :].rearrange("p t s f -> p (t s f)"), ACT.Sin).then_inc(rope_ready, 1)
            for kind, n in qkv_schedule():
                if kind == "qk":
                    for j in range(2):
                        pb = await_full(act, ("qk", n, j))
                        i = {0: 0, 1: 4, 3: 8, 4: 12}[n] + 2 * j
                        free(act.activation(qkT[:, i:i + 2, :].rearrange("p a b -> p (a b)"), pb[:, :], ACT.Copy,
                                            scale=-HD ** -0.5 if n in (0, 3) else 1.0), ("qk", n, j))
                elif kind == "v":
                    for t in range(NT):
                        pb = await_full(act, ("v", n, t))
                        a = 0 if n == 2 else 512
                        free(act.activation(vrow[:, t, a:a + 512], pb[:, :], ACT.Copy), ("v", n, t))
                elif kind == "ada":
                    ada_out(n)

            def norm_heads(g):
                act.wait_ge(heads_ready, g + 1)
                squares([hrow[:, t, g * 512:(g + 1) * 512] for t in range(NT)], [2 * g, 2 * g + 1])

            def evac_oT(g):
                for t in range(NT):
                    pb = await_full(act, ("oT", t, g))
                    free(act.activation(hT[:, 4 * g:4 * g + 4, t * P:(t + 1) * P], quad(pb[:, :]), ACT.Copy), ("oT", t, g))

            for kind, h in attention_schedule():
                if kind == "S":
                    act.wait_ge(masked_ready, h + 1)
                    if h >= 2:
                        await_full(act, ("PT", h - 2))
                    for qt in range(NT):
                        i = 2 * (h % 2) + qt
                        act.activation(Em[:, h % 2, qt, :], Tm[:, h % 2, qt, :], ACT.Exp, scale=-1.0,
                                       bias=accmin[:, i:i + 1], accum_out=rsum[:, qt, h:h + 1]).then_inc(exp_ready, 1)
                elif kind == "norm":
                    norm_heads(0)
                elif kind == "oT":
                    evac_oT(0)
            norm_heads(1)
            ada_out(10)
            evac_oT(1)
            for t in range(NT):
                act.wait_ge(x_ready, t + 1)
                squares([xrow[:, t, :]], [t])
            evac_T("hT")
            ada_out(11)

            def exponentials_of_gates(k):
                act.wait_ge(softmax_shift, k + 1)
                wait_alone(act)
                act.activation(shifted, shifted, ACT.Exp).then_inc(gate_exp, 1)

            def peer_group(n, b, first=False):
                act.wait_ge(u_free, (n + 1) * GROUP)
                act.activation(g8[:, b, :], a8[:, b, :], ACT.Gelu).then_inc(gelu_ready, 1)
                act.wait_ge(weights_ready, n + 1)
                for s in range(GROUP):
                    if not first:
                        act.wait_ge(v_free, (n - 2) * GROUP + s + 1)
                    act.activation(diag[:, b * GROUP + s, :], ident, ACT.Copy, scale=w8[:, b, s:s + 1]).then_inc(diag_ready, 1)

            for job in router_schedule():
                if job[0] == "pq":
                    ch = job[1]
                    for j in range(2):
                        pb = await_full(act, ("pq", ch, j))
                        i = 4 * ch + 2 * j
                        free(act.activation(pqT[:, i:i + 2, :].rearrange("p a b -> p (a b)"), pb[:, :], ACT.Copy), ("pq", ch, j))
                        if (ch, j) == (3, 1):
                            peer_group(0, 0, first=True)
                    if ch == 1:
                        exponentials_of_gates(0)
                else:
                    _, t, g = job
                    pb = await_full(act, job)
                    free(act.activation(scores[:, 4 * t + g, :, :].rearrange("p a b -> p (a b)"), pb[:, :], ACT.Copy), job)

            def piece(k, first=False, last=False):
                for b in range(GPP):
                    if not (first and b == 0):
                        peer_group(k * GPP + b, b % 2, first and b < 2)
                    if b == (2 if first else 1) and not last:
                        exponentials_of_gates(k + 1)

            def norm_after(t):
                act.wait_ge(x_ready, NT + 2 * t + 1)
                if t == 0:
                    rms([xrow[:, t, :]], D, [t])
                else:
                    squares([xrow[:, t, :]], [t])

            piece(0, first=True)
            with act.Fori(1, PIECES // NT) as k:
                piece(k)
            piece(PIECES // NT)
            norm_after(0)
            act.wait_ge(x_ready, NT + 2)
            rms([xrow[:, 0, :]], D, [4])
            with act.Fori(PIECES // NT + 1, PIECES - 1) as k:
                piece(k)
            piece(PIECES - 1, last=True)
            evac_T("zT", 0, [0])
            norm_after(1)

            def layer(l, last=False):
                act.wait_ge(x_ready, l * NT + NT * 3)
                squares([xrow[:, 1, :]], [5], junk)
                evac_T("zT", l, [1])
                for t in range(NT):
                    pb = await_full(act, ("c", t), l)
                    chain.link(act.activation(junk[:, 0:QR], pb[:, 0:QR], ACT.Square, accum_out=ss[:, 6 + t:7 + t]))
                    chain.link(act.activation(junk[:, 0:KVR], pb[:, QR:QR + KVR], ACT.Square, accum_out=ss[:, 8 + t:9 + t]))
                    free(act.activation(crow[:, t, :], pb[:, 0:CW], ACT.Copy), ("c", t))
                    if t == 0:
                        for j in range(2):
                            pb = await_full(act, ("gqk", j), l)
                            dst = (gqT, gkT)[j]
                            free(act.activation(dst.rearrange("p a b -> p (a b)"), pb[:, :], ACT.Copy,
                                                scale=GDK ** -0.5 if j == 0 else 1.0), ("gqk", j))
                pb = await_full(act, ("lr",), l)
                free(act.activation(lrT[0:LR, :], pb[0:LR, 0:S], ACT.Copy), ("lr",))
                chain.wait()
                act.sem_inc(squares_ready, 1)
                for t in range(NT):
                    pb = await_full(act, ("cT", t), l)
                    free(act.activation(cqT[:, :, t * P:(t + 1) * P], pb[:, 0:384].rearrange("p (a b) -> p a b", a=3), ACT.Copy),
                         ("cT", t))
                def values(t):
                    pb = await_full(act, ("gv", t), l)
                    free(act.activation(gv[:, t, :], pb[:, :], ACT.Copy), ("gv", t))

                values(0)
                act.wait_ge(gains2_landed, l * 128 + 128)
                pb = await_full(act, ("gl",), l)
                for a in range(2):
                    chain.step(act.activation(gtmp[:, a, :], pb[:, a * S:(a + 1) * S], ACT.Abs, bias=bgate[:, a:a + 1]))
                chain.wait()
                gt = gtmp.rearrange("p a b -> p (a b)")
                chain.link(act.activation(gt, gt, ACT.Exp, scale=-1.0))
                act.activation(gt, gt, ACT.Ln, bias=1.0).then_inc(exp_gate, 1)
                def decays():
                    act.wait_ge(dve_to_act, l * 2 + 1)
                    act.activation(eb.rearrange("p a b -> p (a b)"), bcum.rearrange("p a b -> p (a b)"), ACT.Exp,
                                   scale=1.0 / GATE_TEMP).then_inc(exp_gate, 1)
                    act.activation(ki.rearrange("p a b -> p (a b)"), bcum.rearrange("p a b -> p (a b)"), ACT.Exp,
                                   scale=-1.0 / GATE_TEMP).then_inc(exp_gate, 1)
                    act.wait_ge(dve_to_act, l * 2 + 2)
                    act.activation(ke.rearrange("p a b -> p (a b)"), ke.rearrange("p a b -> p (a b)"), ACT.Exp,
                                   scale=1.0 / GATE_TEMP).then_inc(exp_gate, 1)

                for t in range(NT):
                    chain.link(act.activation(junk[:, 0:ROPE], crow[:, t, QR + KVR:CW], ACT.Square,
                                              accum_out=ssh[:, 16 + t:17 + t]))
                    for hp in range(2):
                        pb = await_full(act, ("uq", t, hp), l)
                        for i in range(2):
                            h = 2 * hp + i
                            chain.link(act.activation(junk[:, 0:QK], pb[:, i * QK:(i + 1) * QK], ACT.Square,
                                                      accum_out=ssh[:, 4 * t + h:4 * t + h + 1]))
                        free(act.activation(qrow[:, t, 2 * hp:2 * hp + 2, :].rearrange("p a b -> p (a b)"),
                                            pb[:, 0:2 * QK], ACT.Copy), ("uq", t, hp))
                        pb = await_full(act, ("ukv", t, hp), l)
                        for i in range(2):
                            h = 2 * hp + i
                            chain.link(act.activation(junk[:, 0:NOPE], pb[:, i * 256:i * 256 + NOPE], ACT.Square,
                                                      accum_out=ssh[:, 8 + 4 * t + h:9 + 4 * t + h]))
                        free(act.activation(kvrow[:, t, 2 * hp:2 * hp + 2, :].rearrange("p a b -> p (a b)"),
                                            pb[:, :], ACT.Copy), ("ukv", t, hp))
                    if t == 0:
                        decays()
                    for h in range(MH):
                        i = 8 + 4 * t + h
                        if h == 0:
                            chain.wait()
                        chain.step(act.activation(ssh[:, i:i + 1], ssh[:, i:i + 1], ACT.Identity, bias=ssh[:, 16 + t:17 + t]))
                chain.wait()
                act.sem_inc(squares_ready, 1)
                values(1)
                for kind, dst in (("gg", silu_g), ("mg", silu_m)):
                    for t in range(NT):
                        pb = await_full(act, (kind, t), l)
                        free(act.activation(dst[:, t, :], pb[:, :], ACT.Silu), (kind, t))
                        if kind == "mg" and t == 0:
                            for odd in range(2):
                                pb = await_full(act, ("go", odd), l)
                                for i in range(4):
                                    j = 2 * i + odd
                                    chain.link(act.activation(junk[:, 0:GDV], pb[:, i * GDV:(i + 1) * GDV], ACT.Square,
                                                              accum_out=ssg[:, j:j + 1]))
                            chain.wait()
                            act.sem_inc(squares_ready, 1)
                for t in range(NT):
                    for kind, dst in (("qnT", qnT), ("knT", knT)):
                        pb = await_full(act, (kind, t), l)
                        free(act.activation(dst[:, :, t * P:(t + 1) * P], quad(pb[:, :]), ACT.Copy), (kind, t))
                for kind, dst in (("qrT",  qrT), ("krT", krT)):
                    pb = await_full(act, (kind,), l)
                    free(act.activation(dst.rearrange("p a b -> p (a b)"), pb[:, :], ACT.Copy), (kind,))
                for h in range(MH):
                    act.wait_ge(m_masked, l * MH + h + 1)
                    if h >= 2:
                        await_full(act, ("mPT", h - 2), l)
                    for qt in range(NT):
                        a, n = (0, P) if qt == 0 else (P, S)
                        i = 2 * (h % 2) + qt
                        act.activation(mE[:, h % 2, a:a + n], mT[:, h % 2, a:a + n], ACT.Exp, scale=-1.0,
                                       bias=accmin[:, i:i + 1], accum_out=rsum[:, qt, h:h + 1]).then_inc(m_exp, 1)
                    if h == MH - 1:
                        evac_T("cT2", l, groups=[0])
                evac_T("cT2", l, groups=[1])
                if not last:
                    act.wait_ge(x_ready, l * NT + NT * 3 + 1)
                    squares([xrow[:, 0, :]], [4], junk)
                    evac_T("zT", l + 1, [0])

            with act.Fori(0, LAYERS - 1) as l:
                chain.loop(l, 43)
                layer(l)
                chain.end_loop(LAYERS - 1)
            layer(LAYERS - 1, last=True)

        @block.tensor
        def _(pe):
            def transpose_tile(kind, t, rows_before, l=None):
                pe.wait_ge(rows_ready, rows_before + t + 1)
                for g in range(2):
                    pb = claim(pe, (kind, t, g), l)
                    for j in range(4):
                        a = (4 * g + j) * P
                        last = pe.transpose(pb[:, j * P:(j + 1) * P], hrow[:, t, a:a + P], ident)
                    full(last, (kind, t, g))

            def tile_products(kind, jobs, w, t, l=None):
                for g in range(2):
                    drained(pe, (kind, t, g), l)
                for j, job in enumerate(jobs):
                    pb = claim(pe, job, l) if t == 0 else bank[banks.jobs[job][0]]
                    for i in range(2):
                        a, o = (2 * j + i) * P, i * S + t * P
                        for k in range(KD):
                            last = pe.matmul(pb[:, o:o + P], w[:, k, a:a + P], hT[:, k, t * P:(t + 1) * P],
                                             start=k == 0, stop=k == KD - 1)
                    if t == NT - 1:
                        full(last, job)

            def rows_product(job, w, n, t, l=None, k0=0, wcol=0):
                pb = claim(pe, job, l)
                for k in range(KD):
                    last = pe.matmul(pb[:, 0:n], hT[:, k, t * P:(t + 1) * P], w[:, k, wcol:wcol + n], start=k == 0, stop=k == KD - 1)
                full(last, job)

            def columns_product(job, w, j, l=None, modulated=False):
                pb = claim(pe, job, l)
                for i in range(2):
                    a = (2 * j + i) * P
                    for k in range(KD):
                        if modulated and i == 0:
                            pe.wait_ge(hT_modulated, k + 1)
                        last = pe.matmul(pb[:, i * S:(i + 1) * S], w[:, k, a:a + P], hT[:, k, :], start=k == 0, stop=k == KD - 1)
                full(last, job)

            def ada(i):
                pe.wait_ge(ada_summed, i + 1)
                pb = claim(pe, ("ada", i))
                full(pe.matmul(pb[:, :], ones, ada_sum[:, i % 2, :], start=True, stop=True), ("ada", i))

            pe.wait_ge(ident_landed, 16)
            pe.wait_ge(vec_landed, 32)
            pb = claim(pe, ("cols",))
            full(pe.transpose(pb[:, 0:24], vec_rows[:, :], ident[0:24, 0:24]), ("cols",))
            for t in range(NT):
                transpose_tile("xT", t, 0)
            for i in range(4):
                pe.wait_ge(ada_summed, i + 1)
                pb = claim(pe, ("adac", i // 2)) if i % 2 == 0 else pb
                for j in range(4):
                    a = 4 * (i % 2) + j
                    for part in range(2):
                        last = pe.matmul(pb[:, a:a + 1], first_sums[:, i, part, j * P:(j + 1) * P], ones[:, 0:1],
                                         start=part == 0, stop=part == 1)
                if i % 2 == 1:
                    full(last, ("adac", i // 2))
            for kind, n in qkv_schedule():
                if kind == "qk":
                    w = weights1(pe, ("qk", n, 1))
                    for j in range(2):
                        columns_product(("qk", n, j), w, j, modulated=n == 0 and j == 0)
                elif kind == "v":
                    w = weights1(pe, ("v", n, 1))
                    for t in range(NT):
                        rows_product(("v", n, t), w, 512, t)
                elif kind == "ada":
                    ada(n)
                else:
                    pe.wait_ge(rpb_landed, 16 * ROWS * ROWS)
                    pb = claim(pe, ("nab", n))
                    qt, part = n // 4, n % 4
                    full(pe.matmul(pb[:, :], flip, na_raw[qt][:, 2 * part:2 * part + 2, :].rearrange("p a b -> p (a b)"),
                                   start=True, stop=True), ("nab", n))

            def scores_of(h):
                if h == 0:
                    for ch in (0, 1, 3, 4):
                        for j in range(2):
                            drained(pe, ("qk", ch, j))
                qi, ki_ = (h // 2, 4 + h // 2) if h < 8 else (8 + (h - 8) // 2, 12 + (h - 8) // 2)
                p0 = HD * (h % 2)
                pb = claim(pe, ("S", h))
                for qt in range(NT):
                    last = pe.matmul(pb[:, qt * S:(qt + 1) * S], qkT[p0:p0 + HD, qi, qt * P:(qt + 1) * P],
                                     qkT[p0:p0 + HD, ki_, :], start=True, stop=True)
                full(last, ("S", h))

            def transpose_probs(h):
                pe.wait_ge(exp_ready, 2 * h + 2)
                pb = claim(pe, ("PT", h))
                for qt in range(NT):
                    for kt in range(NT):
                        a = (2 * qt + kt) * P
                        last = pe.transpose(pb[:, a:a + P], Em[:, h % 2, qt, kt * P:(kt + 1) * P], ident)
                full(last, ("PT", h))

            def times_v(h):
                if h == 0:
                    for ch in (2, 5):
                        for t in range(NT):
                            drained(pe, ("v", ch, t))
                drained(pe, ("PT", h))
                g, i = h // 8, h % 8
                for qt in range(NT):
                    pb = claim(pe, ("O", g, qt)) if i == 0 else bank[6 + qt]
                    for kt in range(NT):
                        a = (2 * qt + kt) * P
                        last = pe.matmul(pb[:, i * HD:(i + 1) * HD], pT[:, h % 2, a:a + P], vrow[:, kt, h * HD:(h + 1) * HD],
                                         start=kt == 0, stop=kt == NT - 1)
                    if i == 7:
                        full(last, ("O", g, qt))
                if i < 7:
                    last.then_inc(pv_done, 1)

            def transpose_heads(g):
                for t in range(NT):
                    pe.wait_ge(rows_ready, NT * (g + 1) + t + 1)
                    pb = claim(pe, ("oT", t, g))
                    for j in range(4):
                        a = (4 * g + j) * P
                        last = pe.transpose(pb[:, j * P:(j + 1) * P], hrow[:, t, a:a + P], ident)
                    full(last, ("oT", t, g))

            for kind, i in attention_schedule():
                if kind == "S":
                    scores_of(i)
                elif kind == "oT":
                    transpose_heads(0)
                elif kind == "PT":
                    transpose_probs(i)
                elif kind == "PV":
                    times_v(i)

            for job in y_schedule():
                if job[0] == "ada":
                    ada(10)
                elif job[0] == "oT":
                    transpose_heads(1)
                else:
                    _, ch, t, half = job
                    if ch == 0:
                        drained(pe, ("oT", t, half))
                    y = ("y", ch, t)
                    w = weights1(pe, ("y", ch, 1))
                    pb = claim(pe, y) if half == 0 else bank[banks.jobs[y][0]]
                    for k in range(4 * half, 4 * half + 4):
                        last = pe.matmul(pb[:, :], hT[:, k, t * P:(t + 1) * P], w[:, k, :], start=k == 0, stop=k == KD - 1)
                    if half == 1:
                        full(last, y)

            def transpose_subkeys():
                pe.wait_ge(sk_landed, 16)
                pb = claim(pe, ("skT",))
                for s in range(2):
                    last = pe.transpose(pb[:, s * P:(s + 1) * P], skrow[:, s, :], ident)
                full(last, ("skT",))

            transpose_tile("hT", 0, 3 * NT)
            for job in router_schedule():
                if job[0] == "pq":
                    ch = job[1]
                    w = weights1(pe, ("pq", ch, 1))
                    if ch == 0:
                        for t in range(NT):
                            if t > 0:
                                transpose_tile("hT", t, 3 * NT)
                            tile_products("hT", [("pq", 0, j) for j in range(2)], w, t)
                        ada(11)
                        transpose_subkeys()
                    else:
                        for j in range(2):
                            columns_product(("pq", ch, j), w, j)
                else:
                    _, t, g = job
                    drained(pe, ("skT",))
                    drained(pe, ("pq", g, 0))
                    drained(pe, ("pq", g, 1))
                    pb = claim(pe, job)
                    for j in range(4):
                        i = 4 * g + j
                        last = pe.matmul(pb[:, j * P:(j + 1) * P], pqT[:, i, t * P:(t + 1) * P], skT[:, i % 2, :],
                                         start=True, stop=True)
                    full(last, job)

            def peer_group(n, b, t):
                pb = [bank[banks.jobs[("peer", t, half)][0]] for half in range(2)]
                for s in range(GROUP):
                    pe.wait_ge(v_landed[s], 16 * (n + 1) if isinstance(n, int) else n * 16 + 16)
                    pe.wait_ge(diag_ready, n * GROUP + s + 1)
                    for half in range(2):
                        last = pe.matmul(pb[half][:, :], diag[:, b * GROUP + s, :], vgat[:, s, half * 512:(half + 1) * 512],
                                         start=False, stop=False, skip_group_check=True)
                    last.then_inc(v_free, 1)

            pe.wait_ge(ids_ready, 1)
            for t in range(NT):
                for half in range(2):
                    pb = claim(pe, ("peer", t, half))
                    pe.matmul(pb[:, :], zeros, hrow[:, t, half * 512:(half + 1) * 512], start=True, stop=False,
                              skip_group_check=True)
                with pe.Fori(t * NG // 4, (t + 1) * NG // 4) as m:
                    for b in range(2):
                        peer_group(m * 2 + b, b, t)
                for half in range(2):
                    pb = bank[banks.jobs[("peer", t, half)][0]]
                    full(pe.matmul(pb[:, :], zeros, hrow[:, t, half * 512:(half + 1) * 512], start=False, stop=True,
                                   skip_group_check=True), ("peer", t, half))

            with pe.Fori(0, LAYERS) as l:
                for t in range(NT):
                    transpose_tile("zT", t, l * (2 * NT) + 4 * NT, l)
                    w = landed2(pe, 0, l).rearrange("p (k m) -> p k m", k=KD)
                    tile_products("zT", [("gqk", j) for j in range(2)], w, t, l)
                    w = landed2(pe, 1, l).rearrange("p (k m) -> p k m", k=KD)
                    rows_product(("c", t), w, CW, t, l, wcol=LR)
                pb = claim(pe, ("lr",), l)
                for k in range(KD):
                    last = pe.matmul(pb[0:LR, 0:S], w[:, k, 0:LR], hT[:, k, :], start=k == 0, stop=k == KD - 1)
                full(last, ("lr",))
                w_v = landed2(pe, 2, l).rearrange("p (k m) -> p k m", k=KD)
                rows_product(("gv", 0), w_v, 512, 0, l)
                for t in range(NT):
                    pe.wait_ge(dve_to_pe, l * 8 + 1 + t)
                    pb = claim(pe, ("cT", t), l)
                    for j in range(3):
                        last = pe.transpose(pb[:, j * P:(j + 1) * P], crow[:, t, j * P:(j + 1) * P], ident)
                    full(last, ("cT", t))
                drained(pe, ("lr",), l)
                pe.wait_ge(gains2_landed, l * 128 + 128)
                pb = claim(pe, ("gl",), l)
                for a in range(2):
                    last = pe.matmul(pb[:, a * S:(a + 1) * S], up[0:LR, a, :], lrT[0:LR, :], start=True, stop=True)
                full(last, ("gl",))
                w = landed2(pe, 3, l)
                wq_, wkv = w[:, 0:1536].rearrange("p (k m) -> p k m", k=2), w[:, 1536:2560]
                for t in range(NT):
                    drained(pe, ("cT", t), l)
                    for hp in range(2):
                        pb = claim(pe, ("uq", t, hp), l)
                        for k in range(2):
                            last = pe.matmul(pb[:, 0:2 * QK], cqT[:, k, t * P:(t + 1) * P], wq_[:, k, hp * 2 * QK:(hp + 1) * 2 * QK],
                                             start=k == 0, stop=k == 1)
                        full(last, ("uq", t, hp))
                        pb = claim(pe, ("ukv", t, hp), l)
                        full(pe.matmul(pb[:, :], cqT[:, 2, t * P:(t + 1) * P], wkv[:, hp * 512:(hp + 1) * 512],
                                       start=True, stop=True), ("ukv", t, hp))
                rows_product(("gv", 1), w_v, 512, 1, l)
                pe.wait_ge(dve_to_pe, l * 8 + 3)
                pb = claim(pe, ("keT",), l)
                for t in range(NT):
                    for a in range(2):
                        i = 2 * t + a
                        last = pe.transpose(pb[:, i * P:(i + 1) * P], ke[:, a, t * P:(t + 1) * P], ident)
                full(last, ("keT",))
                for odd in range(2):
                    pb = claim(pe, ("A", odd), l)
                    p0 = GDK * odd
                    for t in range(NT):
                        for a in range(2):
                            i = 2 * t + a
                            last = pe.matmul(pb[:, i * P:(i + 1) * P], ki[p0:p0 + GDK, a, t * P:(t + 1) * P],
                                             gqT[p0:p0 + GDK, a, t * P:(t + 1) * P], start=True, stop=True)
                    full(last, ("A", odd))
                drained(pe, ("keT",), l)
                for t in range(NT):
                    drained(pe, ("gv", t), l)
                for i in range(3):
                    pb = claim(pe, ("U", i), l)
                    wait_alone(pe)
                    q0, t = GCH * (i % 2), i // 2
                    for h in range(GH):
                        p0, a = GDK * (h % 2), h // 2
                        last = pe.matmul(pb[p0:p0 + GDK, a * GDV:(a + 1) * GDV], keR[q0:q0 + GCH, t, a, p0:p0 + GDK],
                                         gv[q0:q0 + GCH, t, h * GDV:(h + 1) * GDV], start=True, stop=True)
                    full(last, ("U", i))
                for n, kind in ((4, "gg"), (5, "mg")):
                    w = landed2(pe, n, l).rearrange("p (k m) -> p k m", k=KD)
                    for t in range(NT):
                        rows_product((kind, t), w, 512, t, l)
                        if kind == "mg" and t == 0:
                            pe.wait_ge(dve_to_pe, l * 8 + 8)
                            for odd in range(2):
                                pb = claim(pe, ("go", odd), l)
                                p0 = GDK * odd
                                for t in range(NT):
                                    for a in range(2):
                                        h, i = 2 * a + odd, 2 * t + a
                                        last = pe.matmul(pb[:, i * GDV:(i + 1) * GDV], aT[:, t, h, :], gv[:, t, h * GDV:(h + 1) * GDV],
                                                         start=True, stop=False, skip_group_check=True)
                                        for cc in range(2):
                                            c_ = 2 * t + cc
                                            if c_ > 0:
                                                last = pe.matmul(pb[cc * GCH:(cc + 1) * GCH, i * GDV:(i + 1) * GDV],
                                                                 gqT[p0:p0 + GDK, a, c_ * GCH:(c_ + 1) * GCH],
                                                                 state[p0:p0 + GDK, c_ - 1, a, :],
                                                                 start=False, stop=True, skip_group_check=True)
                                full(last, ("go", odd))
                for t in range(NT):
                    pe.wait_ge(dve_to_pe, l * 8 + 4 + t)
                    for kind, src in (("qnT", qrow), ("knT", kvrow)):
                        pb = claim(pe, (kind, t), l)
                        for h in range(MH):
                            last = pe.transpose(pb[:, h * P:(h + 1) * P], src[:, t, h, 0:NOPE], ident)
                        full(last, (kind, t))
                for kind, src in (("qrT", qrr), ("krT", krr)):
                    pb = claim(pe, (kind,), l)
                    for a in range(2):
                        for t in range(NT):
                            i = (2 * a + t) * P
                            last = pe.transpose(pb[:, i:i + P], src[:, t, 2 * a:2 * a + 2, :].rearrange("p a b -> p (a b)"), ident)
                    full(last, (kind,))
                def transpose_context(t, g):
                    pb = claim(pe, ("cT2", t, g), l)
                    for j in range(4):
                        a = (4 * g + j) * P
                        last = pe.transpose(pb[:, j * P:(j + 1) * P], hrow[:, t, a:a + P], ident)
                    full(last, ("cT2", t, g))

                for kind, i in mla_schedule():
                    if kind == "cT2":
                        pe.wait_ge(linear_out_ready, l + 1)
                        for t in range(NT):
                            transpose_context(t, 0)
                    elif kind == "ms":
                        if i == 0:
                            for t in range(NT):
                                drained(pe, ("qnT", t), l)
                                drained(pe, ("knT", t), l)
                            drained(pe, ("qrT",), l)
                            drained(pe, ("krT",), l)
                        p0, a = ROPE * (i % 2), i // 2
                        pb = claim(pe, ("ms", i), l)
                        for qt in range(NT):
                            o, n = (0, P) if qt == 0 else (P, S)
                            pe.matmul(pb[:, o:o + n], qnT[:, i, qt * P:(qt + 1) * P], knT[:, i, 0:n], start=True, stop=False)
                            last = pe.matmul(pb[:, o:o + n], qrT[p0:p0 + ROPE, a, qt * P:(qt + 1) * P],
                                             krT[p0:p0 + ROPE, a, 0:n], start=False, stop=True)
                        full(last, ("ms", i))
                    elif kind == "mPT":
                        pe.wait_ge(m_exp, l * (2 * MH) + 2 * i + 2)
                        pb = claim(pe, ("mPT", i), l)
                        for j in range(3):
                            last = pe.transpose(pb[:, j * P:(j + 1) * P], mE[:, i % 2, j * P:(j + 1) * P], ident)
                        full(last, ("mPT", i))
                    else:
                        drained(pe, ("mPT", i), l)
                        for qt in range(NT):
                            pb = claim(pe, ("mo", qt), l) if i == 0 else bank[6 + qt]
                            for kt in range(qt + 1):
                                j = qt + kt
                                last = pe.matmul(pb[:, i * MDV:(i + 1) * MDV], mPT[:, i % 2, j * P:(j + 1) * P],
                                                 kvrow[:, kt, i, NOPE:NOPE + MDV], start=kt == 0, stop=kt == qt)
                            if i == MH - 1:
                                full(last, ("mo", qt))
                        if i < MH - 1:
                            last.then_inc(m_pv, 1)
                for t in range(NT):
                    pe.wait_ge(rows_ready, l * (2 * NT) + 5 * NT + t + 1)
                    transpose_context(t, 1)
                for t in range(NT):
                    for g in range(2):
                        drained(pe, ("cT2", t, g), l)
                    for ch in range(2):
                        w = landed2(pe, 6 + ch, l).rearrange("p (k m) -> p k m", k=KD)
                        rows_product(("y2", ch, t), w, 512, t, l)

        @block.vector
        def _(dve):
            chain = Chain(dve, dve_step)

            def bc(ap, *shape):
                return ap.to_broadcast([P, *shape])

            chain.step(dve.memset(eps, EPS))
            chain.wait()
            chain.link(dve.memset(ones, 1.0))
            dve.sem_inc(consts_set, 1)

            def sum_ada(i, steps=range(KD)):
                n = ADA[i]
                w = slot512(W1_AT[("ada", i)])
                acc = ada_sum[:, i % 2, :]
                for k in steps:
                    if k == 0:
                        weights1(dve, ("ada", i))
                        if i >= 6:
                            await_full(dve, ("ada", i - 2))
                    chain.wait()
                    before = modb[:, n // 2, (n % 2) * 512:(n % 2 + 1) * 512] if k == 0 else acc
                    ins = dve.scalar_tensor_tensor(acc, w[:, k, :], csil[:, k:k + 1], before, ALU.mult, ALU.add)
                    if k < KD - 1:
                        chain.step(ins)
                    else:
                        ins.then_inc(ada_summed, 1)

            def fold_gain(s, g):
                chain.link(dve.scalar_tensor_tensor(modb[:, s, :], modb[:, s, :], 1.0, gains[:, g, :], ALU.add, ALU.mult))

            dve.wait_ge(rstd_ready, 1)
            for t in range(NT):
                dve.tensor_scalar(hrow[:, t, :], xrow[:, t, :], rstd[:, t:t + 1], None, ALU.mult).then_inc(rows_ready, 1)
            pb = await_full(dve, ("cols",))
            free(dve.tensor_copy(vec[:, :], pb[:, 0:24]), ("cols",))
            dve.wait_ge(silu_ready, 1)
            for i in range(4):
                dve.wait_ge(first_half_landed[i], 16)
                w = slot512(i)
                for k in range(KD):
                    if k == KD // 2:
                        weights1(dve, ("ada", i))
                    acc = first_sums[:, i, k % 2, :]
                    if k < 2:
                        chain.step(dve.tensor_scalar(acc, w[:, k, :], csil[:, k:k + 1], None, ALU.mult))
                    else:
                        dve.wait_ge(dve_step, chain.n - 1)
                        chain.step(dve.scalar_tensor_tensor(acc, w[:, k, :], csil[:, k:k + 1], acc, ALU.mult, ALU.add))
                chain.wait()
                dve.sem_inc(ada_summed, 1)
                if i == 1:
                    drained(dve, ("cols",))
                if i == 3:
                    pb = await_full(dve, ("adac", 0))
                    chain.link(dve.scalar_tensor_tensor(gain1[:, :], pb[:, 0:KD], 1.0, vec[:, KD:2 * KD], ALU.add, ALU.add))
                    free(dve.tensor_tensor(gain1[:, :], gain1[:, :], vec[:, 2 * KD:3 * KD], ALU.mult), ("adac", 0))
            pb = await_full(dve, ("adac", 1))
            free(dve.tensor_tensor(shift1[:, :], pb[:, 0:KD], vec[:, 0:KD], ALU.add), ("adac", 1))
            for i in range(2):
                drained(dve, ("adac", i))
            for t in range(NT):
                for g in range(2):
                    drained(dve, ("xT", t, g))
            for k in range(KD):
                dve.tensor_scalar(hT[:, k, :], hT[:, k, :], gain1[:, k:k + 1], shift1[:, k:k + 1], ALU.mult, ALU.add)\
                    .then_inc(hT_modulated, 1)

            dve.wait_ge(const_landed, 16 * (len(kept) + 2))
            chain.link(dve.tensor_copy(posf, posi))
            MAGIC, C1 = 1.5 * 2.0 ** 23, 6.28125
            C2 = float(np.float32(round((2 * np.pi - C1) * 2.0 ** 20) / 2.0 ** 20))
            C3 = 2 * np.pi - C1 - C2
            ang = Tm[:, 0, 0, 0:64].rearrange("p (t f) -> p t f", t=NT)
            turns = Tm[:, 0, 1, 0:128].rearrange("p (t s f) -> p t s f", t=NT, s=2)
            for t in range(NT):
                chain.step(dve.tensor_scalar(ang[:, t, :], inv_freq, posf[:, t:t + 1], None, ALU.mult))
            chain.wait()
            for s in range(2):
                chain.step(dve.tensor_scalar(turns[:, :, s, :], ang, 1 / (2 * np.pi), 0.25 * (1 - s), ALU.mult, ALU.add))
            chain.wait()
            tf = turns.rearrange("p t s f -> p (t s f)")
            chain.link(dve.tensor_scalar(tf, tf, MAGIC, None, ALU.add))
            chain.link(dve.tensor_scalar(tf, tf, MAGIC, None, ALU.subtract))
            for s in range(2):
                chain.step(dve.scalar_tensor_tensor(rope[:, :, s, :], turns[:, :, s, :], -C1, ang, ALU.mult, ALU.add))
            rf = rope[:, :, :, :].rearrange("p t s f -> p (t s f)")
            chain.wait()
            chain.link(dve.scalar_tensor_tensor(rf, tf, -C2, rf, ALU.mult, ALU.add))
            chain.link(dve.scalar_tensor_tensor(rf, tf, -C3, rf, ALU.mult, ALU.add))
            chain.link(dve.tensor_scalar(rope[:, :, 0, :], rope[:, :, 0, :], np.pi / 2, None, ALU.add))
            PI = float(np.nextafter(np.float32(np.pi), np.float32(0)))
            dve.tensor_scalar(rf, rf, PI, -PI, ALU.min, ALU.max).then_inc(ang_ready, 1)

            def neighbourhood_bias(i):
                qt, part = i // 4, i % 4
                pb = await_full(dve, ("nab", i))
                free(dve.tensor_tensor(bias[:, 2 * part:2 * part + 2, qt, :], bc(na_window[:, qt, :].unsqueeze(1), 2, S),
                                       pb[:, :].rearrange("p (a b) -> p a b", a=2), ALU.subtract), ("nab", i))

            dve.wait_ge(adab_landed, 16)
            for kind, i in qkv_schedule():
                if kind == "ada":
                    sum_ada(i)
                elif kind == "nab":
                    neighbourhood_bias(i)

            dve.wait_ge(dil_landed, 16)
            for i in range(8):
                drained(dve, ("nab", i))

            def normalize(g):
                dve.wait_ge(exp_ready, 2 * (8 * g + 8))
                chain.link(dve.reciprocal(rinv, rsum[:, :, 8 * g:8 * g + 8]))
                for qt in range(NT):
                    pb = await_full(dve, ("O", g, qt))
                    free(dve.tensor_tensor(hrow[:, qt, g * 512:(g + 1) * 512].rearrange("p (h d) -> p h d", h=8),
                                           pb[:, :].rearrange("p (h d) -> p h d", h=8),
                                           bc(rinv[:, qt, :].unsqueeze(2), 8, HD), ALU.mult), ("O", g, qt))
                for qt in range(NT):
                    drained(dve, ("O", g, qt))
                dve.sem_inc(heads_ready, 1)

            def scale_heads(g):
                dve.wait_ge(inv_rms_ready, 1 + g)
                for t in range(NT):
                    a, i = slice(g * 512, (g + 1) * 512), 2 * g + t
                    dve.scalar_tensor_tensor(hrow[:, t, a], hrow[:, t, a], rstd[:, i:i + 1], gains[:, 2, a],
                                             ALU.mult, ALU.mult).then_inc(rows_ready, 1)

            dve.wait_ge(gains_landed, 48)
            for kind, h in attention_schedule():
                if kind == "S":
                    if h >= 2:
                        dve.wait_ge(exp_ready, 2 * (h - 2) + 2)
                    pb = await_full(dve, ("S", h))
                    for qt in range(NT):
                        i = 2 * (h % 2) + qt
                        ins = dve.tensor_tensor_reduce(Tm[:, h % 2, qt, :], pb[:, qt * S:(qt + 1) * S], bias[:, h, qt, :], 1.0, 3e38,
                                                       ALU.add, ALU.min, accmin[:, i:i + 1])
                        if qt == 0:
                            chain.step(ins)
                        else:
                            free(ins, ("S", h))
                    drained(dve, ("S", h))
                    chain.wait()
                    dve.sem_inc(masked_ready, 1)
                elif kind == "PT":
                    if h >= 2:
                        if (h - 2) % 8 == 7:
                            await_full(dve, ("O", (h - 2) // 8, 1))
                        else:
                            dve.wait_ge(pv_done, (h - 2) - (h - 2) // 8 + 1)
                    pb = await_full(dve, ("PT", h))
                    free(dve.tensor_copy(pT[:, h % 2, :], pb[:, :]), ("PT", h))
                elif kind == "O":
                    normalize(h)
                elif kind == "scale":
                    scale_heads(0)
                elif kind == "sum ada":
                    sum_ada(10, [h])
            scale_heads(1)

            def add_gated(job, gate, ch, t, i, ready=None):
                pb = await_full(dve, job)
                a = slice(ch * 512, (ch + 1) * 512)
                free(dve.tensor_tensor(ytmp[:, i, :], pb[:, :], modb[:, gate, a], ALU.mult), job)
                drained(dve, job)
                ins = dve.tensor_tensor(xrow[:, t, a], xrow[:, t, a], ytmp[:, i, :], ALU.add)
                if ready is None:
                    chain.link(ins)
                else:
                    ins.then_inc(ready, 1)

            for i in range(4, 11):
                drained(dve, ("ada", i))
            fold_gain(4, 1)
            sum_ada(11)

            def modulated(t):
                dve.wait_ge(x_ready, t + 1)
                dve.wait_ge(inv_rms_ready, 3 + t)
                chain.link(dve.scalar_tensor_tensor(hrow[:, t, :], xrow[:, t, :], rstd[:, t:t + 1], modb[:, 4, :], ALU.mult, ALU.mult))
                dve.tensor_tensor(hrow[:, t, :], hrow[:, t, :], modb[:, 3, :], ALU.add).then_inc(rows_ready, 1)

            for t in range(NT):
                for ch in range(2):
                    add_gated(("y", ch, t), 2, ch, t, t, x_ready if ch == 1 else None)
                modulated(t)

            pb = await_full(dve, ("skT",))
            free(dve.tensor_copy(skT[:, :, :].rearrange("p a b -> p (a b)"), pb[:, 0:2 * P]), ("skT",))

            def steps_done():
                chain.wait()
                if chain.turn is not None:
                    wait_alone(dve)

            def top16(units):
                steps_done()
                for src, v, i in units:
                    chain.step(dve.max(v[:, 0:8], src))
                steps_done()
                for src, v, i in units:
                    chain.step(dve.max_index(i[:, 0:8], v[:, 0:8], src))
                steps_done()
                for src, v, i in units:
                    chain.step(dve.match_replace(src, v[:, 0:8], src, -3.0e38))
                steps_done()
                for src, v, i in units:
                    chain.step(dve.max(v[:, 8:16], src))
                steps_done()
                for src, v, i in units:
                    chain.step(dve.max_index(i[:, 8:16], v[:, 8:16], src))

            def best_halves(k):
                chain.wait()
                chain.link(dve.tensor_copy(one_piece.rearrange("p a b -> p (a b)"),
                                           scores[:, bass.ds(k, 1), :, :].rearrange("p o a b -> p (o a b)")))
                top16([(one_piece[:, j, :], top_v[:, j // 2, j % 2, :], top_i[:, j // 2, j % 2, :]) for j in range(4)])

            def best_pairs(k):
                chain.wait()
                chain.link(dve.tensor_tensor(cand.rearrange("p h (a b) -> p h a b", a=TOPK),
                                             bc(top_v[:, :, 0, :].unsqueeze(3), 2, TOPK, TOPK),
                                             bc(top_v[:, :, 1, :].unsqueeze(2), 2, TOPK, TOPK), ALU.add))
                top16([(cand[:, h, :], best_v[:, h, :], best_j[:, h, :]) for h in range(2)])
                chain.wait()
                chain.step(dve.tensor_tensor(shifted, best_v, bc(best_v[:, :, 0:1], 2, TOPK), ALU.subtract))
                chain.wait()
                dve.sem_inc(softmax_shift, 1)
                chain.step(dve.tensor_scalar(best_ab[:, :, 0, :], best_j, 4, None, ALU.logical_shift_right))
                chain.step(dve.tensor_scalar(best_ab[:, :, 1, :], best_j, 15, None, ALU.bitwise_and))

            def experts_and_gates(k):
                chain.wait()
                chain.link(dve.tensor_tensor(hit, bc(best_ab.rearrange("p h s k -> p (h s) k").unsqueeze(3), 4, TOPK, TOPK),
                                             iota.unsqueeze(1).unsqueeze(1).to_broadcast([P, 4, TOPK, TOPK]), ALU.is_equal))
                chain.link(dve.tensor_tensor(hit, hit, bc(top_i.rearrange("p h s k -> p (h s) k").unsqueeze(2), 4, TOPK, TOPK), ALU.mult))
                chain.link(dve.tensor_reduce(picked.rearrange("p h s k -> p (h s k)"), hit.rearrange("p h k a -> p (h k) a"), AX.X, ALU.add))
                here = bass.ds(k * 2 * TOPK, 2 * TOPK)
                chain.link(dve.scalar_tensor_tensor(ids[:, here].rearrange("p (h k) -> p h k", h=2), picked[:, :, 0, :],
                                                    float(NKEY), picked[:, :, 1, :], ALU.mult, ALU.add))
                dve.sem_inc(ids_ready, 1)
                dve.wait_ge(gate_exp, k + 1)
                wait_alone(dve)
                chain.link(dve.tensor_reduce(gsum[:, 0:2], shifted, AX.X, ALU.add))
                chain.link(dve.reciprocal(gsum[:, 8:10], gsum[:, 0:2]))
                chain.step(dve.tensor_tensor(gates[:, here].rearrange("p (h k) -> p h k", h=2), shifted,
                                             bc(gsum[:, 8:10].unsqueeze(2), 2, TOPK), ALU.mult))

            chain.step(dve.memset(aT.rearrange("p a b c -> p (a b c)"), 0.0))
            chain.link(dve.memset(zeros, 0.0))
            await_full(dve, ("ada", 11))
            drained(dve, ("sc", 0, 0))
            best_halves(0)
            best_pairs(0)
            experts_and_gates(0)
            chain.wait()

            def peer_group(n, b, t):
                for s in range(GROUP):
                    dve.wait_ge(u_landed[s], n * 16 + 16)
                    dve.tensor_tensor_reduce(urow[:, s, :], urow[:, s, :], hrow[:, t, :], 1.0, 0.0, ALU.mult, ALU.add,
                                             a8[:, b, s:s + 1]).then_inc(u_free, 1)
                dve.wait_ge(gelu_ready, n + 1)
                dve.tensor_tensor(w8[:, b, :], g8[:, b, :], gates[:, bass.ds(n * GROUP, GROUP)], ALU.mult).then_inc(weights_ready, 1)

            dve.wait_ge(rows_ready, 4 * NT)
            def piece(k, t, next_piece, first=False):
                steps = {0: [best_halves], 1: [best_pairs], 2: [experts_and_gates]}
                if first:
                    steps = {1: [best_halves], 2: [best_pairs, experts_and_gates]}
                for b in range(GPP):
                    peer_group(k * GPP + b, b % 2, t)
                    for step in steps.get(b, []) if next_piece else []:
                        for job in router_schedule():
                            if job[0] == "sc" and step is best_halves:
                                drained(dve, job)
                        step(k + 1)
                if next_piece:
                    chain.wait()

            def after_peer(t):
                for part in range(2):
                    add_gated(("peer", t, part), 5, part, t, part, x_ready if part == 1 else None)
                dve.wait_ge(fing_landed, 16)
                dve.wait_ge(x_ready, NT + 2 * t + 1)
                if t == 0:
                    dve.wait_ge(rstd_ready, 2)
                else:
                    dve.wait_ge(inv_rms_ready, 5)
                dve.scalar_tensor_tensor(xrow[:, t, :], xrow[:, t, :], rstd[:, t:t + 1], gains[:, 0, :],
                                         ALU.mult, ALU.mult).then_inc(x_ready, 1)

            def layer_norm(l, t, rms_count, x_count):
                dve.wait_ge(gains2_landed, l * 128 + 128)
                if rms_count is None:
                    dve.wait_ge(rstd_ready, 3)
                else:
                    dve.wait_ge(inv_rms_ready, rms_count)
                dve.wait_ge(x_ready, x_count)
                dve.scalar_tensor_tensor(hrow[:, t, :], xrow[:, t, :], rstd[:, 4 + t:5 + t], g_in, ALU.mult, ALU.mult)\
                    .then_inc(rows_ready, 1)

            half = PIECES // NT
            piece(0, 0, True, first=True)
            with dve.Fori(1, half) as k:
                chain.loop(k - 1, 42)
                piece(k, 0, True)
                chain.end_loop(half - 1)
            piece(half, 1, True)
            after_peer(0)
            layer_norm(0, 0, None, NT + 2)
            with dve.Fori(half + 1, PIECES - 1) as k:
                chain.loop(k - (half + 1), 42)
                piece(k, 1, True)
                chain.end_loop(half - 2)
            piece(PIECES - 1, NT - 1, False)
            after_peer(1)
            def layer(l, last=False):
                layer_norm(l, 1, l * 5 + 6, l * NT + 3 * NT)
                for t in range(NT):
                    drained(dve, ("c", t), l)
                dve.wait_ge(inv_rms_ready, l * 5 + 7)
                for t in range(NT):
                    chain.step(dve.scalar_tensor_tensor(crow[:, t, QR:QR + KVR], crow[:, t, QR:QR + KVR], rstd[:, 8 + t:9 + t], g_kv,
                                                        ALU.mult, ALU.mult))
                    chain.wait()
                    dve.scalar_tensor_tensor(crow[:, t, 0:QR], crow[:, t, 0:QR], rstd[:, 6 + t:7 + t], g_q,
                                             ALU.mult, ALU.mult).then_inc(dve_to_pe, 1)
                pb = await_full(dve, ("gl",), l)
                dve.wait_ge(exp_gate, l * 4 + 1)
                for a in range(2):
                    chain.step(dve.tensor_scalar(log_a[:, a, :], pb[:, a * S:(a + 1) * S], bgate[:, a:a + 1], 0.0, ALU.add, ALU.min))
                chain.wait()
                la = log_a.rearrange("p a b -> p (a b)")
                free(dve.tensor_tensor(la, la, gtmp.rearrange("p a b -> p (a b)"), ALU.subtract), ("gl",))
                drained(dve, ("gl",), l)
                for a in range(2):
                    chain.step(dve.tensor_tensor_scan(bcum[:, a, :], segment, log_a[:, a, :], 0.0, ALU.mult, ALU.add))
                chain.wait()
                dve.sem_inc(dve_to_act, 1)
                b4 = bcum.rearrange("p a (c i) -> p a c i", i=GCH)
                for a in range(2):
                    ins = dve.tensor_tensor(ke[:, a, :].rearrange("p (c i) -> p c i", i=GCH),
                                            bc(b4[:, a, :, GCH - 1:GCH], S // GCH, GCH), b4[:, a, :, :], ALU.subtract)
                    chain.step(ins)
                chain.wait()
                dve.sem_inc(dve_to_act, 1)
                dve.wait_ge(exp_gate, l * 4 + 3)
                for j in range(2):
                    drained(dve, ("gqk", j), l)
                chain.step(dve.tensor_tensor(gqT, gqT, eb, ALU.mult))
                chain.step(dve.tensor_tensor(ki, ki, gkT, ALU.mult))
                dve.wait_ge(exp_gate, l * 4 + 4)
                chain.step(dve.tensor_tensor(ke, ke, gkT, ALU.mult))
                chain.wait()
                dve.sem_inc(dve_to_pe, 1)
                pb = await_full(dve, ("keT",), l)
                free(dve.tensor_copy(keR.rearrange("p t a b -> p (t a b)"), pb[:, :]), ("keT",))
                dve.wait_ge(rope_ready, 1)
                dve.wait_ge(inv_rms_ready, l * 5 + 8)
                w4 = wide.rearrange("p (h d) -> p h d", h=MH)
                HR = ROPE // 2
                for t in range(NT):
                    for hp in range(2):
                        drained(dve, ("uq", t, hp), l)
                        drained(dve, ("ukv", t, hp), l)
                    cos, sin = rope[:, t, 0, :], rope[:, t, 1, :]
                    rq, rk = rstdh[:, 4 * t:4 * t + 4], rstdh[:, 8 + 4 * t:12 + 4 * t]
                    chain.step(dve.tensor_tensor(qrow[:, t, :, :], qrow[:, t, :, :], bc(rq.unsqueeze(2), MH, QK), ALU.mult))
                    chain.step(dve.tensor_tensor(kvrow[:, t, :, 0:NOPE], kvrow[:, t, :, 0:NOPE], bc(rk.unsqueeze(2), MH, NOPE), ALU.mult))
                    chain.step(dve.tensor_tensor(kpe[:, t, :], crow[:, t, QR + KVR:CW], g_kh[:, NOPE:QK], ALU.mult))
                    chain.wait()
                    chain.step(dve.tensor_tensor(qrow[:, t, :, :], qrow[:, t, :, :], bc(g_qh.unsqueeze(1), MH, QK), ALU.mult))
                    chain.step(dve.tensor_tensor(kvrow[:, t, :, 0:NOPE], kvrow[:, t, :, 0:NOPE], bc(g_kh[:, 0:NOPE].unsqueeze(1), MH, NOPE), ALU.mult))
                    k1, k2 = kpe[:, t, 0:HR], kpe[:, t, HR:ROPE]
                    kp = wide[:, 512:640]
                    chain.step(dve.tensor_tensor(kp[:, 0:32], k1, cos, ALU.mult))
                    chain.step(dve.tensor_tensor(kp[:, 32:64], k2, sin, ALU.mult))
                    chain.step(dve.tensor_tensor(kp[:, 64:96], k1, sin, ALU.mult))
                    chain.step(dve.tensor_tensor(kp[:, 96:128], k2, cos, ALU.mult))
                    chain.wait()
                    q1, q2 = qrow[:, t, :, NOPE:NOPE + HR], qrow[:, t, :, NOPE + HR:QK]
                    cb, sb_ = bc(cos.unsqueeze(1), MH, HR), bc(sin.unsqueeze(1), MH, HR)
                    qp = wide[:, 0:512].rearrange("p (i h f) -> p i h f", i=4, h=MH)
                    chain.step(dve.tensor_tensor(qp[:, 0, :, :], q1, cb, ALU.mult))
                    chain.step(dve.tensor_tensor(qp[:, 1, :, :], q2, sb_, ALU.mult))
                    chain.step(dve.tensor_tensor(qp[:, 2, :, :], q1, sb_, ALU.mult))
                    chain.step(dve.tensor_tensor(qp[:, 3, :, :], q2, cb, ALU.mult))
                    chain.step(dve.tensor_tensor(kpr[:, t, 0:HR], kp[:, 0:32], kp[:, 32:64], ALU.subtract))
                    chain.step(dve.tensor_tensor(kpr[:, t, HR:ROPE], kp[:, 64:96], kp[:, 96:128], ALU.add))
                    chain.wait()
                    chain.step(dve.tensor_tensor(qrr[:, t, :, 0:HR], qp[:, 0, :, :], qp[:, 1, :, :], ALU.subtract))
                    chain.step(dve.tensor_tensor(qrr[:, t, :, HR:ROPE], qp[:, 2, :, :], qp[:, 3, :, :], ALU.add))
                    chain.step(dve.tensor_tensor(krr[:, t, :, :], bc(kpr[:, t, :].unsqueeze(1), MH, ROPE), bc(rk.unsqueeze(2), MH, ROPE), ALU.mult))
                    chain.wait()
                    dve.sem_inc(dve_to_pe, 1)

                for odd in range(2):
                    pb = await_full(dve, ("A", odd), l)
                    wait_alone(dve)
                    free(dve.copy_predicated(aT.rearrange("p t (a o) m -> p t a o m", o=2)[:, :, :, odd, :],
                                             same_chunk.unsqueeze(1).unsqueeze(1).to_broadcast([P, NT, 2, P]),
                                             pb[:, :].rearrange("p (t a m) -> p t a m", t=NT, a=2)), ("A", odd))
                    drained(dve, ("A", odd), l)
                    dve.sem_inc(dve_to_pe, 1)
                e4 = eb.rearrange("p a (c i) -> p a c i", i=GCH)
                pb = await_full(dve, ("U", 0), l)
                free(dve.tensor_copy(state[:, 0, :, :].rearrange("p a b -> p (a b)"), pb[:, 0:2 * GDV]), ("U", 0))
                drained(dve, ("U", 0), l)
                for i in (1, 2):
                    pb = await_full(dve, ("U", i), l)
                    for a in range(2):
                        ins = dve.scalar_tensor_tensor(state[:, i, a, :], state[:, i - 1, a, :], e4[:, a, i, GCH - 1:GCH],
                                                       pb[:, a * GDV:(a + 1) * GDV], ALU.mult, ALU.add)
                        if a == 0:
                            chain.step(ins)
                        else:
                            free(ins, ("U", i))
                    drained(dve, ("U", i), l)
                    chain.wait()
                dve.sem_inc(dve_to_pe, 1)

                dve.wait_ge(inv_rms_ready, l * 5 + 9)
                for odd in range(2):
                    pb = await_full(dve, ("go", odd), l)
                    o = hrow[:, :, 0:512].rearrange("p t (a o d) -> p t a o d", a=2, o=2)[:, :, :, odd, :]
                    r4 = ssg.rearrange("p (t a o) -> p t a o", t=NT, a=2)[:, :, :, odd].unsqueeze(3)
                    free(dve.tensor_tensor(o, pb[:, :].rearrange("p (t a d) -> p t a d", t=NT, a=2),
                                           r4.to_broadcast([P, NT, 2, GDV]), ALU.mult), ("go", odd))
                    drained(dve, ("go", odd), l)
                for t in range(NT):
                    o = hrow[:, t, 0:512].rearrange("p (h d) -> p h d", h=GH)
                    chain.link(dve.tensor_tensor(o, o, bc(g_gla.unsqueeze(1), GH, GDV), ALU.mult))
                    drained(dve, ("gg", t), l)
                    chain.step(dve.tensor_tensor(hrow[:, t, 0:512], hrow[:, t, 0:512], silu_g[:, t, :], ALU.mult))
                chain.wait()
                dve.sem_inc(gains2_used, 1)
                dve.sem_inc(linear_out_ready, 1)

                for kind, h in mla_schedule():
                    if kind == "ms":
                        if h >= 2:
                            dve.wait_ge(m_exp, l * (2 * MH) + 2 * (h - 2) + 2)
                        pb = await_full(dve, ("ms", h), l)
                        wait_alone(dve)
                        for qt in range(NT):
                            a, n = (0, P) if qt == 0 else (P, S)
                            i = 2 * (h % 2) + qt
                            ins = dve.tensor_tensor_reduce(mT[:, h % 2, a:a + n], pb[:, a:a + n], causal[:, a:a + n], -QK ** -0.5, 3e38,
                                                           ALU.add, ALU.min, accmin[:, i:i + 1])
                            if qt == 0:
                                chain.step(ins)
                            else:
                                free(ins, ("ms", h))
                        drained(dve, ("ms", h), l)
                        chain.wait()
                        dve.sem_inc(m_masked, 1)
                    elif kind == "mPT":
                        if h >= 2:
                            dve.wait_ge(m_pv, l * (MH - 1) + (h - 2) + 1)
                        pb = await_full(dve, ("mPT", h), l)
                        free(dve.tensor_copy(mPT[:, h % 2, :], pb[:, 0:384]), ("mPT", h))
                dve.wait_ge(m_exp, l * (2 * MH) + 2 * MH)
                chain.link(dve.reciprocal(rinv[:, :, 0:MH], rsum[:, :, 0:MH]))
                for t in range(NT):
                    pb = await_full(dve, ("mo", t), l)
                    o = hrow[:, t, 512:1024]
                    free(dve.tensor_tensor(o.rearrange("p (h d) -> p h d", h=MH), quad(pb[:, :]),
                                           bc(rinv[:, t, 0:MH].unsqueeze(2), MH, MDV), ALU.mult), ("mo", t))
                    drained(dve, ("mo", t), l)
                    drained(dve, ("mg", t), l)
                    dve.tensor_tensor(o, o, silu_m[:, t, :], ALU.mult).then_inc(rows_ready, 1)
                for t in range(NT):
                    for ch in range(2):
                        pb = await_full(dve, ("y2", ch, t), l)
                        a = slice(ch * 512, (ch + 1) * 512)
                        free(dve.tensor_tensor(xrow[:, t, a], xrow[:, t, a], pb[:, :], ALU.add), ("y2", ch, t))
                        drained(dve, ("y2", ch, t), l)
                    dve.sem_inc(x_ready, 1)
                    if t == 0 and not last:
                        layer_norm(l + 1, 0, l * 5 + 10, l * NT + 3 * NT + 1)

            with dve.Fori(0, LAYERS - 1) as l:
                chain.loop(l, 58)
                layer(l)
                chain.end_loop(LAYERS - 1)
            layer(LAYERS - 1, last=True)


_INS = ["x", "c", "ada_w", "ada_b", "norm1_g", "w_in", "na_rpb", "out_norm_na_g", "out_norm_dil_g", "w_out", "norm2_g",
        "peer_wq", "peer_subkeys", "peer_u", "peer_v", "final_g", "positions_2", "norm_g_2", "w_in_2",
        "w_gla_gate_up_2", "b_gla_gate_2", "gla_norm_g_2", "mla_q_norm_g_2", "w_uq_2", "mla_kv_norm_g_2", "w_ukv_2",
        "q_head_g_2", "k_head_g_2", "w_out_2"]


def kernel(**inputs):
    import concourse.bacc as bacc
    from concourse.bass_utils import run_bass_kernel_spmd

    nc = bacc.Bacc("TRN2", target_bir_lowering=False, num_devices=1)
    arrays, args = {}, []
    for name in _INS:
        a = np.ascontiguousarray(inputs[name])
        arrays[f"in_{name}"] = a
        args.append(nc.dram_tensor(f"in_{name}", a.shape, mybir.dt.from_np(a.dtype), kind="ExternalInput").ap())
    for name, a in zip(("shape_const", "dil_bias_const"), shape_constants()):
        arrays[name] = a
        args.append(nc.dram_tensor(name, a.shape, mybir.dt.from_np(a.dtype), kind="ExternalInput").ap())
    args.append(nc.dram_tensor("out_0", (1, S, D), F32, kind="ExternalOutput").ap())
    program(nc, *args)
    r = run_bass_kernel_spmd(nc, [arrays], core_ids=[0])
    return r.results[0]["out_0"]
```
